# Optimizing a Trainium2 kernel written in Bass

```python
import jax, jax.numpy as jnp
from jax import lax
import numpy as np

D_MODEL = 1024
BATCH = 1
SEQ = 1024
DEPTH = 1

CHUNK = 64
N_BRANCH = 3
BRANCH_WIDTH = D_MODEL // 2
POOL_WINDOWS = (2, 4, 8, 16)
N_POOL_GROUPS = len(POOL_WINDOWS)
POOL_GROUP = BRANCH_WIDTH // N_POOL_GROUPS
CONV_K = 3
SB_HEAD_DIM = 64
SB_HEADS = BRANCH_WIDTH // SB_HEAD_DIM
Q_BLOCK = 128
RMS_EPS = 1e-6
IN_SIZES = (BRANCH_WIDTH,) * 10 + (N_BRANCH * D_MODEL,)
N_IN = sum(IN_SIZES)


def _split_points():
    return [int(p) for p in np.cumsum(IN_SIZES)[:-1]]

def rms_norm(x, g):
    xf = x.astype(jnp.float32)
    y = xf * lax.rsqrt(jnp.mean(xf * xf, axis=-1, keepdims=True) + RMS_EPS)
    return (y * g.astype(jnp.float32)).astype(x.dtype)

def pool_mixer(v, w_group, scale):
    b, s, _ = v.shape
    vg = v.astype(jnp.float32).reshape(b, s, N_POOL_GROUPS, POOL_GROUP)
    csum = jnp.cumsum(vg, axis=1)
    pos = jnp.arange(s)
    outs = []
    for gi, w in enumerate(POOL_WINDOWS):
        c = csum[:, :, gi]
        lag = jnp.pad(c[:, :s - w], ((0, 0), (w, 0), (0, 0)))
        cnt = jnp.minimum(pos + 1, w).astype(jnp.float32)[None, :, None]
        outs.append((c - lag) / cnt - vg[:, :, gi])
    pooled = jnp.stack(outs, axis=2).astype(v.dtype)
    mixed = jnp.einsum('bsgc,gcd->bsgd', pooled, w_group)
    return mixed.reshape(b, s, BRANCH_WIDTH) * scale

def conv_mixer(xc, gate_b, gate_c, w, bias):
    z = gate_c * xc
    y = lax.conv_general_dilated(
        z, w[:, None, :].astype(z.dtype), window_strides=(1,), padding=[(CONV_K - 1, 0)],
        dimension_numbers=('NWC', 'WIO', 'NWC'), feature_group_count=BRANCH_WIDTH)
    return gate_b * (y + bias)

def stick_breaking_attention(q, k, v):
    b, s, _ = q.shape
    nblk = s // Q_BLOCK
    qb = q.reshape(b, nblk, Q_BLOCK, SB_HEADS, SB_HEAD_DIM).transpose(1, 0, 2, 3, 4)
    kf = k.reshape(b, s, SB_HEADS, SB_HEAD_DIM).astype(jnp.float32)
    vf = v.reshape(b, s, SB_HEADS, SB_HEAD_DIM).astype(jnp.float32)
    key_pos = jnp.arange(s)
    scale = SB_HEAD_DIM ** -0.5

    def block(args):
        qi, i = args
        logits = jnp.einsum('bqhd,bkhd->bhqk', qi.astype(jnp.float32), kf) * scale
        q_pos = i * Q_BLOCK + jnp.arange(Q_BLOCK)
        mask = key_pos[None, :] < q_pos[:, None]
        log_keep = jnp.where(mask, jax.nn.log_sigmoid(-logits), 0.0)
        later = lax.cumsum(log_keep, axis=3, reverse=True) - log_keep
        weights = jnp.where(mask, jnp.exp(jax.nn.log_sigmoid(logits) + later), 0.0)
        return jnp.einsum('bhqk,bkhd->bqhd', weights, vf)

    out = lax.map(block, (qb, jnp.arange(nblk)))
    return out.transpose(1, 0, 2, 3, 4).reshape(b, s, BRANCH_WIDTH).astype(q.dtype)

def hybrid_layer(x, g_pre, w_in, pool_w, pool_scale, conv_w, conv_b, w_branch, w_out, g_post):
    b, s, _ = x.shape
    h = rms_norm(x, g_pre)
    u = jnp.einsum('bsd,dn->bsn', h, w_in)
    (pool_v, pool_g, conv_x, conv_gb, conv_gc, conv_g,
     sb_q, sb_k, sb_v, sb_g, merge) = jnp.split(u, _split_points(), axis=-1)
    y_pool = pool_mixer(pool_v, pool_w, pool_scale) * jax.nn.silu(pool_g)
    y_conv = conv_mixer(conv_x, conv_gb, conv_gc, conv_w, conv_b) * jax.nn.silu(conv_g)
    y_sb = stick_breaking_attention(sb_q, sb_k, sb_v) * jax.nn.silu(sb_g)
    branches = jnp.stack([y_pool, y_conv, y_sb], axis=2)
    proj = jnp.einsum('bsnw,nwd->bsnd', branches, w_branch)
    gates = jax.nn.sigmoid(merge.reshape(b, s, N_BRANCH, D_MODEL))
    merged = jnp.sum(gates * proj, axis=2)
    out = jnp.einsum('bsd,de->bse', merged, w_out)
    return x + rms_norm(out, g_post)

def first_inputs(seed: int = 0) -> dict:
    key = jax.random.key(seed)
    ks = jax.random.split(key, 10)
    f32 = jnp.float32
    x = jax.random.normal(ks[0], (BATCH, SEQ, D_MODEL), f32)
    pre_norm_g = 1.0 + 0.05 * jax.random.normal(ks[1], (DEPTH, D_MODEL), f32)
    w_in = jax.random.normal(ks[2], (DEPTH, D_MODEL, N_IN), f32) * D_MODEL ** -0.5
    pool_w = jax.random.normal(ks[3], (DEPTH, N_POOL_GROUPS, POOL_GROUP, POOL_GROUP), f32) * POOL_GROUP ** -0.5
    pool_scale = 1.0 + 0.1 * jax.random.normal(ks[4], (DEPTH, BRANCH_WIDTH), f32)
    conv_w = jax.random.normal(ks[5], (DEPTH, CONV_K, BRANCH_WIDTH), f32) * CONV_K ** -0.5
    conv_b = 0.01 * jax.random.normal(ks[6], (DEPTH, BRANCH_WIDTH), f32)
    w_branch = jax.random.normal(ks[7], (DEPTH, N_BRANCH, BRANCH_WIDTH, D_MODEL), f32) * BRANCH_WIDTH ** -0.5
    w_out = jax.random.normal(ks[8], (DEPTH, D_MODEL, D_MODEL), f32) * D_MODEL ** -0.5
    post_norm_g = 1.0 + 0.05 * jax.random.normal(ks[9], (DEPTH, D_MODEL), f32)
    return {"x": x, "pre_norm_g": pre_norm_g, "w_in": w_in, "pool_w": pool_w,
            "pool_scale": pool_scale, "conv_w": conv_w, "conv_b": conv_b,
            "w_branch": w_branch, "w_out": w_out, "post_norm_g": post_norm_g}

def first_block(x, pre_norm_g, w_in, pool_w, pool_scale, conv_w, conv_b, w_branch, w_out, post_norm_g):
    for l in range(DEPTH):
        x = hybrid_layer(x, pre_norm_g[l], w_in[l], pool_w[l], pool_scale[l], conv_w[l],
                         conv_b[l], w_branch[l], w_out[l], post_norm_g[l])
    return x


GRID_W = 64
CTX_LEN = 256

MLA_HEADS = 8
MLA_Q_RANK = 256
MLA_KV_RANK = 256
MLA_NOPE = 64
MLA_ROPE = 32
MLA_V = 64
MLA_SCALE = (MLA_NOPE + MLA_ROPE) ** -0.5

RET_HEADS = 4
RET_DK = 128
RET_DV = 128
RET_CHUNK = 128

D_FF = 2816
CONV_WIDTH = 3

ROPE_BASE = 10000.0
EPS = 1e-6

MLA_WIDTH = MLA_HEADS * MLA_V
RET_WIDTH = RET_HEADS * RET_DV
MIX_WIDTH = MLA_WIDTH + RET_WIDTH
IN_SIZES_2 = (MLA_Q_RANK, MLA_KV_RANK, MLA_ROPE, RET_HEADS * RET_DK, RET_HEADS * RET_DK, RET_WIDTH, RET_WIDTH)
IN_SPLITS = tuple(int(v) for v in np.cumsum(IN_SIZES_2)[:-1])
IN_COLS = int(sum(IN_SIZES_2))


def rmsnorm(x, g):
    xf = x.astype(jnp.float32)
    y = xf * lax.rsqrt(jnp.mean(xf * xf, axis=-1, keepdims=True) + EPS)
    return (y * g.astype(jnp.float32)).astype(x.dtype)

def modulate(h, shift, scale):
    return h * (1.0 + scale) + shift

def rope_angles(pos, dim):
    inv = ROPE_BASE ** (-jnp.arange(0, dim, 2, dtype=jnp.float32) / dim)
    return pos.astype(jnp.float32)[:, None] * inv[None, :]

def apply_rope(x, ang):
    x1, x2 = jnp.split(x, 2, axis=-1)
    cos = jnp.cos(ang)[None, :, None, :].astype(x.dtype)
    sin = jnp.sin(ang)[None, :, None, :].astype(x.dtype)
    return jnp.concatenate([x1 * cos - x2 * sin, x1 * sin + x2 * cos], axis=-1)

def axial_rope(x, pos):
    pos_row, pos_col = pos
    half = x.shape[-1] // 2
    xr = apply_rope(x[..., :half], rope_angles(pos_row, half))
    xc = apply_rope(x[..., half:], rope_angles(pos_col, half))
    return jnp.concatenate([xr, xc], axis=-1)

def split_proj(p):
    return jnp.split(p, IN_SPLITS, axis=-1)

def mla_queries(c_q, g_q, w_uq, pos):
    B, S, _ = c_q.shape
    q = (rmsnorm(c_q, g_q) @ w_uq).reshape(B, S, MLA_HEADS, MLA_NOPE + MLA_ROPE)
    q_nope, q_pe = q[..., :MLA_NOPE], q[..., MLA_NOPE:]
    if pos is not None:
        q_pe = axial_rope(q_pe, pos)
    return jnp.concatenate([q_nope, q_pe], axis=-1)

def mla_keys(c_kv, k_pe, g_kv, w_ukv, pos):
    B, S, _ = c_kv.shape
    kv = (rmsnorm(c_kv, g_kv) @ w_ukv).reshape(B, S, MLA_HEADS, MLA_NOPE + MLA_V)
    k_nope, v = kv[..., :MLA_NOPE], kv[..., MLA_NOPE:]
    k_pe = k_pe[:, :, None, :]
    if pos is not None:
        k_pe = axial_rope(k_pe, pos)
    k_pe = jnp.broadcast_to(k_pe, (B, S, MLA_HEADS, MLA_ROPE))
    return jnp.concatenate([k_nope, k_pe], axis=-1), v

def softmax_attention(q, k, v):
    s = jnp.einsum('bqhd,bkhd->bhqk', q, k).astype(jnp.float32) * MLA_SCALE
    p = jax.nn.softmax(s, axis=-1).astype(v.dtype)
    return jnp.einsum('bhqk,bkhd->bqhd', p, v)

def latent_attention(q, k_lat, v_lat, k_ctx, v_ctx):
    k = jnp.concatenate([k_lat, k_ctx], axis=1)
    v = jnp.concatenate([v_lat, v_ctx], axis=1)
    B, S, H, dq = q.shape
    qb = q.reshape(B, S // Q_BLOCK, Q_BLOCK, H, dq).swapaxes(0, 1)
    o = lax.map(lambda qi: softmax_attention(qi, k, v), qb)
    return o.swapaxes(0, 1).reshape(B, S, H * MLA_V)

def retention_inputs(rq, rk, rv, pos):
    B, S, _ = rq.shape
    q = rq.reshape(B, S, RET_HEADS, RET_DK)
    k = rk.reshape(B, S, RET_HEADS, RET_DK) * (RET_DK ** -0.5)
    v = rv.reshape(B, S, RET_HEADS, RET_DV)
    if pos is not None:
        ang = rope_angles(pos, RET_DK)
        q = apply_rope(q, ang)
        k = apply_rope(k, ang)
    return q, k, v

def retention_final_state(k, v, log_gamma, reverse):
    L = k.shape[1]
    j = jnp.arange(L, dtype=jnp.float32)
    expo = j if reverse else (L - 1.0 - j)
    w = jnp.exp(log_gamma[:, None] * expo[None, :])
    return jnp.einsum('bjhd,hj,bjhe->bhde', k.astype(jnp.float32), w, v.astype(jnp.float32))

def retention_chunkwise(q, k, v, log_gamma, init_state, strict):
    B, S, H, dk = q.shape
    dv = v.shape[-1]
    C = RET_CHUNK
    n = S // C
    idx = jnp.arange(C, dtype=jnp.float32)
    diff = idx[:, None] - idx[None, :]
    mask = (diff > 0) if strict else (diff >= 0)
    expo = jnp.where(mask, diff, 0.0)
    lg = log_gamma.astype(jnp.float32)
    decay_in = jnp.where(mask[None], jnp.exp(lg[:, None, None] * expo[None]), 0.0)
    xi = jnp.exp(lg[:, None] * (idx + 1.0)[None, :])[None, :, :, None]
    zeta = jnp.exp(lg[:, None] * (C - 1.0 - idx)[None, :])[None, :, :, None]
    g_chunk = jnp.exp(lg * C)[None, :, None, None]

    def to_chunks(a):
        return a.astype(jnp.float32).reshape(B, n, C, H, a.shape[-1]).transpose(1, 0, 3, 2, 4)

    def step(state, inp):
        qi, ki, vi = inp
        att = jnp.einsum('bhqd,bhkd->bhqk', qi, ki) * decay_in[None]
        inner = jnp.einsum('bhqk,bhke->bhqe', att, vi)
        cross = jnp.einsum('bhqd,bhde->bhqe', qi, state) * xi
        new_state = state * g_chunk + jnp.einsum('bhkd,bhke->bhde', ki * zeta, vi)
        return new_state, inner + cross

    _, out = lax.scan(step, init_state.astype(jnp.float32), (to_chunks(q), to_chunks(k), to_chunks(v)))
    return out.transpose(1, 0, 3, 2, 4).reshape(B, S, H, dv)

def head_groupnorm(y, g):
    B, S, H, dv = y.shape
    mu = jnp.mean(y, axis=-1, keepdims=True)
    var = jnp.mean(jnp.square(y - mu), axis=-1, keepdims=True)
    yn = ((y - mu) * lax.rsqrt(var + EPS)).reshape(B, S, H * dv)
    return yn * g.astype(jnp.float32)

def retention_bidir(q, k, v, gate, log_gamma, state_f, state_b, g_ret):
    flip = lambda a: jnp.flip(a, axis=1)
    y_f = retention_chunkwise(q, k, v, log_gamma[0], state_f, False)
    y_b = flip(retention_chunkwise(flip(q), flip(k), flip(v), log_gamma[1], state_b, True))
    y = head_groupnorm(y_f + y_b, g_ret)
    return (jax.nn.silu(gate.astype(jnp.float32)) * y).astype(v.dtype)

def conv_ffn(h, w_up, conv_w, conv_b, w_down):
    u = h @ w_up
    u = lax.conv_general_dilated(u, conv_w[:, None, :].astype(u.dtype), window_strides=(1,),
                                 padding=((CONV_WIDTH // 2, CONV_WIDTH // 2),),
                                 dimension_numbers=('NWC', 'WIO', 'NWC'),
                                 feature_group_count=u.shape[-1]) + conv_b
    a, g = jnp.split(u, 2, axis=-1)
    return (jax.nn.silu(g) * a) @ w_down

def second_inputs(seed: int = 0) -> dict:
    key = jax.random.key(seed)
    ks = jax.random.split(key, 21)
    nrm = lambda k, shape, scale: jax.random.normal(k, shape, jnp.float32) * scale
    h = jnp.arange(RET_HEADS, dtype=jnp.float32)
    decay_init = jnp.log(-jnp.log(1.0 - 2.0 ** (-5.0 - h)))
    return {
        'x': nrm(ks[0], (BATCH, SEQ, D_MODEL), 1.0),
        'c': nrm(ks[1], (BATCH, D_MODEL), 1.0),
        'ctx': nrm(ks[2], (BATCH, CTX_LEN, D_MODEL), 1.0),
        'c_ctx': nrm(ks[3], (D_MODEL,), 1.0),
        'w_ada': nrm(ks[4], (DEPTH, D_MODEL, 6 * D_MODEL), 0.5 * D_MODEL ** -0.5),
        'b_ada': nrm(ks[5], (DEPTH, 6 * D_MODEL), 0.02),
        'g_norm1': 1.0 + nrm(ks[6], (DEPTH, D_MODEL), 0.02),
        'w_in': nrm(ks[7], (DEPTH, D_MODEL, IN_COLS), D_MODEL ** -0.5),
        'g_q': 1.0 + nrm(ks[8], (DEPTH, MLA_Q_RANK), 0.02),
        'w_uq': nrm(ks[9], (DEPTH, MLA_Q_RANK, MLA_HEADS * (MLA_NOPE + MLA_ROPE)), MLA_Q_RANK ** -0.5),
        'g_kv': 1.0 + nrm(ks[10], (DEPTH, MLA_KV_RANK), 0.02),
        'w_ukv': nrm(ks[11], (DEPTH, MLA_KV_RANK, MLA_HEADS * (MLA_NOPE + MLA_V)), MLA_KV_RANK ** -0.5),
        'ret_decay': decay_init[None, None, :] + nrm(ks[12], (DEPTH, 2, RET_HEADS), 0.05),
        'g_ret': 1.0 + nrm(ks[13], (DEPTH, RET_WIDTH), 0.02),
        'w_out': nrm(ks[14], (DEPTH, MIX_WIDTH, D_MODEL), MIX_WIDTH ** -0.5),
        'g_norm2': 1.0 + nrm(ks[15], (DEPTH, D_MODEL), 0.02),
        'w_up': nrm(ks[16], (DEPTH, D_MODEL, 2 * D_FF), D_MODEL ** -0.5),
        'conv_w': nrm(ks[17], (DEPTH, CONV_WIDTH, 2 * D_FF), CONV_WIDTH ** -0.5),
        'conv_b': nrm(ks[18], (DEPTH, 2 * D_FF), 0.02),
        'w_down': nrm(ks[19], (DEPTH, D_FF, D_MODEL), D_FF ** -0.5),
        'g_final': 1.0 + nrm(ks[20], (D_MODEL,), 0.02),
    }

def second_block(x, c, ctx, c_ctx, w_ada, b_ada, g_norm1, w_in, g_q, w_uq, g_kv, w_ukv,
              ret_decay, g_ret, w_out, g_norm2, w_up, conv_w, conv_b, w_down, g_final):
    B, S, _ = x.shape
    rows = S // GRID_W
    pos_row = jnp.repeat(jnp.arange(rows, dtype=jnp.int32), GRID_W)
    pos_col = jnp.tile(jnp.arange(GRID_W, dtype=jnp.int32), rows)
    pos_grid = (pos_row, pos_col)
    pos_seq = jnp.arange(S, dtype=jnp.int32)

    for l in range(DEPTH):
        last = l == DEPTH - 1
        mod = jax.nn.silu(c) @ w_ada[l] + b_ada[l]
        sh1, sc1, gt1, sh2, sc2, gt2 = jnp.split(mod[:, None, :], 6, axis=-1)
        mod_c = jax.nn.silu(c_ctx) @ w_ada[l] + b_ada[l]
        shc1, scc1, gtc1, shc2, scc2, gtc2 = jnp.split(mod_c, 6)
        log_gamma = -jnp.exp(ret_decay[l].astype(jnp.float32))

        h = modulate(rmsnorm(x, g_norm1[l]), sh1, sc1)
        hc = modulate(rmsnorm(ctx, g_norm1[l]), shc1, scc1)
        cq, ckv, kpe, rq, rk, rv, rg = split_proj(h @ w_in[l])
        cq_c, ckv_c, kpe_c, rq_c, rk_c, rv_c, rg_c = split_proj(hc @ w_in[l])

        k_c, v_c = mla_keys(ckv_c, kpe_c, g_kv[l], w_ukv[l], None)
        qr_c, kr_c, vr_c = retention_inputs(rq_c, rk_c, rv_c, None)
        st_f = retention_final_state(kr_c, vr_c, log_gamma[0], False)
        st_b = retention_final_state(kr_c, vr_c, log_gamma[1], True)

        q = mla_queries(cq, g_q[l], w_uq[l], pos_grid)
        k, v = mla_keys(ckv, kpe, g_kv[l], w_ukv[l], pos_grid)
        o_mla = latent_attention(q, k, v, k_c, v_c)
        qr, kr, vr = retention_inputs(rq, rk, rv, pos_seq)
        o_ret = retention_bidir(qr, kr, vr, rg, log_gamma, st_f, st_b, g_ret[l])
        o = jnp.concatenate([o_mla, o_ret.astype(o_mla.dtype)], axis=-1) @ w_out[l]
        x_new = x + gt1 * o
        x_new = x_new + gt2 * conv_ffn(modulate(rmsnorm(x_new, g_norm2[l]), sh2, sc2),
                                       w_up[l], conv_w[l], conv_b[l], w_down[l])

        if not last:
            q_c = mla_queries(cq_c, g_q[l], w_uq[l], None)
            o_mla_c = softmax_attention(q_c, k_c, v_c).reshape(B, ctx.shape[1], MLA_WIDTH)
            zero_state = jnp.zeros_like(st_f)
            o_ret_c = retention_bidir(qr_c, kr_c, vr_c, rg_c, log_gamma, zero_state, zero_state, g_ret[l])
            o_c = jnp.concatenate([o_mla_c, o_ret_c.astype(o_mla_c.dtype)], axis=-1) @ w_out[l]
            ctx = ctx + gtc1 * o_c
            ctx = ctx + gtc2 * conv_ffn(modulate(rmsnorm(ctx, g_norm2[l]), shc2, scc2),
                                        w_up[l], conv_w[l], conv_b[l], w_down[l])
        x = x_new

    return rmsnorm(x, g_final)


def setup_inputs(seed=0):
    out = dict(first_inputs(seed))
    for name, value in second_inputs(seed + 1).items():
        if name != "x":
            out[name + "_2"] = value
    return out


def reference(
    x, pre_norm_g, w_in, pool_w, pool_scale, conv_w, conv_b, w_branch, w_out, post_norm_g, c_2,
    ctx_2, c_ctx_2, w_ada_2, b_ada_2, g_norm1_2, w_in_2, g_q_2, w_uq_2, g_kv_2, w_ukv_2,
    ret_decay_2, g_ret_2, w_out_2, g_norm2_2, w_up_2, conv_w_2, conv_b_2, w_down_2, g_final_2,
):
    x = first_block(
        x, pre_norm_g, w_in, pool_w, pool_scale, conv_w, conv_b, w_branch, w_out, post_norm_g,
    )
    return second_block(
        x, c_2, ctx_2, c_ctx_2, w_ada_2, b_ada_2, g_norm1_2, w_in_2, g_q_2, w_uq_2, g_kv_2,
        w_ukv_2, ret_decay_2, g_ret_2, w_out_2, g_norm2_2, w_up_2, conv_w_2, conv_b_2, w_down_2,
        g_final_2,
    )


_drawn_inputs = setup_inputs


def setup_inputs(seed=0):
    import zlib

    import numpy as np

    out = dict(_drawn_inputs(seed))
    spreads = {}
    factors = {'conv_b': 8.0,
     'ctx_2': 3.283,
     'c_ctx_2': 2.7,
     'b_ada_2': 3.52,
     'g_norm1_2': 8.0,
     'g_q_2': 8.0,
     'w_uq_2': 5.086,
     'g_kv_2': 8.0,
     'g_ret_2': 8.0,
     'g_norm2_2': 8.0,
     'conv_b_2': 8.0,
     'g_final_2': 2.827}
    for name, (base, spread) in spreads.items():
        noise = np.random.default_rng([zlib.crc32(name.encode()), seed]).standard_normal(out[name].shape)
        drawn = base * np.exp(spread * noise) if base else spread * noise
        out[name] = __import__('jax').numpy.asarray(drawn.astype(out[name].dtype))
    for name, factor in factors.items():
        out[name] = (out[name] * factor).astype(out[name].dtype)
    return out
```

```python
from contextlib import ExitStack, contextmanager

import numpy as np
import concourse.bass as bass
from concourse import mybir

F32 = mybir.dt.float32
F32R = mybir.dt.float32r
ACT = mybir.ActivationFunctionType
ALU = mybir.AluOpType
AX = mybir.AxisListType

P = 128
S = 1024
CTX = 256
SC = S + CTX
D = 1024
DT = D // P
W = 512
BT = W // P
NCH = S // 512
UNIT = 1024
EPS = 1e-6
POOL_WINDOWS = (2, 4, 8, 16)
HD = 64
PAIRS = BT
MLA_SCALE = 96.0 ** -0.5
RET_SCALE = 128.0 ** -0.5
RH = 4
NC = S // P
NCC = CTX // P
FF = 2816
FT = FF // P
CLAMP = 30.0
BIG = 1e30

PARAMS, _n = {}, 0
for _name, _w in (("pre_g", DT), ("pool_scale", BT), ("conv", 4 * BT), ("post_g", DT), ("c", 2 * DT),
                  ("b_ada", 6 * DT), ("g1", DT), ("gq", 2), ("gkv", 2), ("gret", RH), ("g2", DT),
                  ("conv2", 4 * 2 * FT), ("gfin", DT), ("decay", 2 * RH)):
    PARAMS[_name] = _n
    _n += _w
NPARAM = _n

CONSTS, _n = {}, 0
for _name, _w in (("tri", P), ("rest", P), ("ident", P), ("mask", P), ("mneg", P), ("cnt", 16 * BT),
                  ("fwd", P), ("bwd", P), ("xf", P), ("xb", P), ("zf", 1), ("zb", 1)):
    CONSTS[_name] = _n
    _n += _w
NCONST = _n


def constants():
    c = np.zeros((P, NCONST), np.float32)
    r = np.arange(P)
    k, q = r[:, None], r[None, :]

    def put(name, a):
        a = np.broadcast_to(a, (P, a.shape[-1]))
        c[:, CONSTS[name]:CONSTS[name] + a.shape[1]] = a

    put("tri", (k >= q).astype(np.float32))
    put("rest", (k < q).astype(np.float32))
    put("ident", (k == q).astype(np.float32))
    put("mask", (k < q).astype(np.float32))
    put("mneg", np.where(k < q, BIG, -BIG).astype(np.float32))
    for g, w in enumerate(POOL_WINDOWS):
        c[:, CONSTS["cnt"] + 16 * g:CONSTS["cnt"] + 16 * g + 16] = w / np.minimum(np.arange(16) + 1, w)
    put("fwd", np.maximum(q - k, 0).astype(np.float32))
    put("bwd", np.maximum(k - q, 0).astype(np.float32))
    put("xf", (q + 1).astype(np.float32))
    put("xb", (P - q).astype(np.float32))
    put("zf", (P - 1 - k).astype(np.float32))
    put("zb", k.astype(np.float32))
    return c


def rope_tables():
    def inv(dim):
        return (np.float32(10000.0) ** (-np.arange(0, dim, 2, dtype=np.float32) / np.float32(dim))).astype(np.float32)
    pos = np.arange(S, dtype=np.float32)
    a = inv(P)[:, None] * pos[None, :]
    a = np.concatenate([a, a])
    sign = np.where(np.arange(P) < P // 2, 1.0, -1.0)[:, None]
    ret = np.stack([np.cos(a), np.sin(a) * sign], 1)
    row, col = np.floor(pos / 64), pos % 64
    half = []
    for p in (row, col):
        b = inv(16)[:, None] * p[None, :].astype(np.float32)
        half.append(np.concatenate([b, b]))
    b = np.concatenate(half)
    sgn = np.tile(np.repeat([-1.0, 1.0], 8), 2)[:, None]
    mla = np.zeros((P, S))
    mla[64:96] = np.cos(b)
    mla[96:128] = np.sin(b) * sgn
    return ret.reshape(P, 2 * S).astype(np.float32), mla.astype(np.float32)


class At:

    def __init__(self, base, per=0, i=None):
        self.base, self.per, self.i = base, per, i

    def plus(self, n):
        return At(self.base + n, self.per, self.i)

    @property
    def slot(self):
        assert self.per % 2 == 0
        return self.base % 2

    def value(self, extra=0):
        return self.base + extra if self.i is None else self.per * self.i + (self.base + extra)

    def half(self, extra=0):
        return self.base // 2 + extra if self.i is None else (self.per // 2) * self.i + (self.base // 2 + extra)


class Chain:

    def __init__(self, eng, sem):
        self.eng, self.sem, self.n, self.i, self.per, self.start = eng, sem, 0, None, 0, 0

    def value(self):
        return self.n if self.i is None else self.per * self.i + self.n

    def __call__(self, ins):
        self.n += 1
        ins.then_inc(self.sem, 1)
        self.eng.wait_ge(self.sem, self.value())

    @contextmanager
    def body(self, i, per, times):
        self.i, self.per, self.start = i, per, self.n
        yield
        assert self.n - self.start == per, f"{self.n - self.start} steps in a body of {per}"
        self.i, self.n = None, self.start + per * times


class Core:
    pass



STAGES = (
    ("sb", PAIRS, 4, 4),
    ("merge_sb", 2, 6, 8),
    ("pool", 2, 6, 6),
    ("merge_pool", 2, 6, 8),
    ("conv", BT, 4, 4),
    ("merge_conv", 2, 6, 8),
    ("out1", 1, DT, DT),
    ("latents", 1, 5, 5),
    ("ret", RH, 4, 12),
    ("mla", PAIRS, 2, 36),
    ("out2", 1, DT, DT),
    ("up0", 1, 4, 4),
    ("ffn", FT // 2 - 1, 6, 12),
    ("down", 1, 2, 8),
)
FIRST_UNIT, FIRST_TILE, _u, _t = {}, {}, 0, 2
for _name, _steps, _units, _tiles in STAGES:
    FIRST_UNIT[_name], FIRST_TILE[_name] = _u, _t
    _u, _t = _u + _steps * _units, _t + _steps * _tiles
NUNITS = _u

ADA = 4
ADA_STEP, _u = {}, 0
for _name, _steps, _, _ in STAGES:
    if _name in ("merge_sb", "pool", "merge_pool", "conv", "merge_conv"):
        ADA_STEP[_name] = _u
        _u += _steps
assert ADA * _u == 6 * DT

BLOCKS = [(qc, kb, a, max(0, kb - 4 * qc) * P)
          for qc in range(NCH) for kb in range(4 * qc + 3, -1, -1) for a in range(2)]
NB = len(BLOCKS)


NLOGIT, NEX = 7, 3


def place(nc, name, kb, shape, dt):
    if kb == 0:
        with nc.sbuf_tensor(name, shape, dt) as t:
            return t
    with nc.sbuf_tensor(f"{name}_before", [P, int(kb * 256)], F32):
        with nc.sbuf_tensor(name, shape, dt) as t:
            pass
    return t


def lay_out(nc, ctx):
    k = Core()
    k.wh = place(nc, "weights_hi", 0, [P, 2, UNIT], F32R)
    k.wl = place(nc, "weights_lo", 8, [P, 2, UNIT], F32R)
    k.raw = place(nc, "weights_raw", 16, [P, 2, UNIT], F32)
    k.const = place(nc, "constants", 24, [P, NCONST], F32)
    k.params = place(nc, "params", 29, [P, NPARAM], F32)
    k.tri = place(nc, "tri", 30.5, [P, 2 * P], F32R)
    k.ones = place(nc, "ones", 31.5, [P, P], F32R)
    k.adaw = place(nc, "modulation_weights", 202, [P, UNIT], F32)
    k.one32 = place(nc, "ones_f32", 32, [P, P], F32)
    k.mod = place(nc, "modulation", 32.5, [P, 6 * DT, 2], F32)
    k.scf = place(nc, "silu_c", 33.25, [P, 2 * DT], F32)
    k.gm = place(nc, "gains", 33.5, [P, 4 * DT], F32)
    k.idle = place(nc, "idle", 33.75, [P, 4], F32)
    B = 34
    k.hh = place(nc, "h_hi", B, [P, DT, S], F32R)
    k.hl = place(nc, "h_lo", B + 32, [P, DT, S], F32R)
    k.yh = place(nc, "branch_hi", B + 64, [P, BT, S], F32R)
    k.yl = place(nc, "branch_lo", B + 80, [P, BT, S], F32R)
    k.outr = place(nc, "mixed", B + 64, [P, DT, S], F32)
    k.merged = place(nc, "merged", B + 96, [P, DT, S], F32)
    T = B + 96
    k.x = place(nc, "x", T, [P, DT, S], F32)
    N0 = T + 32
    k.sqh = place(nc, "squares_hi", N0, [P, 2, 512], F32R)
    k.sql = place(nc, "squares_lo", N0 + 4, [P, 2, 512], F32R)
    k.sq = place(nc, "squares", N0 + 8, [P, 512], F32)
    k.root = place(nc, "root", N0 + 10, [P, 512], F32)
    k.rstd = place(nc, "rstd", N0 + 12, [P, SC], F32)
    k.nt = place(nc, "normed", N0 + 17, [P, 2, 512], F32)
    k.qh = place(nc, "q_hi", T, [P, S], F32R)
    k.ql = place(nc, "q_lo", T + 4, [P, S], F32R)
    k.kh = place(nc, "k_hi", T + 8, [P, S], F32R)
    k.kl = place(nc, "k_lo", T + 12, [P, S], F32R)
    k.vh = place(nc, "v_hi", T + 16, [P, NC, P], F32R)
    k.vl = place(nc, "v_lo", T + 20, [P, NC, P], F32R)
    k.sph = place(nc, "softplus_hi", T + 24, [P, 4, 512], F32R)
    k.spl = place(nc, "softplus_lo", T + 32, [P, 4, 512], F32R)
    k.ph = place(nc, "weights_of_keys_hi", T + 40, [P, 2, 512], F32R)
    k.pl = place(nc, "weights_of_keys_lo", T + 44, [P, 2, 512], F32R)
    k.logit = place(nc, "logits_then_weights", T + 48, [P, NLOGIT, 512], F32)
    k.ex = place(nc, "exps_then_softplus", T + 62, [P, NEX, 512], F32)
    k.vy = place(nc, "v_then_y", T + 68, [P, S], F32)
    k.sg = place(nc, "silu_gate", T + 72, [P, S], F32)
    T2 = T + 32
    k.pv = place(nc, "pool_v", T2, [P, S], F32)
    k.pa = place(nc, "window_a", T2 + 4, [P, S], F32)
    k.pb = place(nc, "window_b", T2 + 8, [P, S], F32)
    k.poh = place(nc, "pooled_hi", T2 + 12, [P, S], F32R)
    k.pol = place(nc, "pooled_lo", T2 + 16, [P, S], F32R)
    k.psg = place(nc, "pool_gate", T2 + 20, [P, S], F32)
    k.py = place(nc, "pool_y", T2 + 24, [P, S], F32)
    k.sig = place(nc, "merge_gate", T2 + 28, [P, 2, S], F32)
    k.prod = place(nc, "gated", T2 + 36, [P, S], F32)
    k.cg = place(nc, "conv_gate_c", T2, [P, S], F32)
    k.cz = place(nc, "conv_z", T2 + 4, [P, S], F32)
    k.cy = place(nc, "conv_y", T2 + 8, [P, S], F32)
    k.csg = place(nc, "conv_gate", T2 + 12, [P, S], F32)

    k.h2h = place(nc, "h2_hi", B, [P, DT, SC], F32R)
    k.h2l = place(nc, "h2_lo", B + 40, [P, DT, SC], F32R)
    k.ctx = place(nc, "context", 184, [P, DT, CTX], F32)
    k.cq = place(nc, "latent_q", 114, [P, 2, S], F32)
    k.ckv = place(nc, "latent_kv", 122, [P, 2, SC], F32)
    k.kpe = place(nc, "key_rotated", 162, [P, SC], F32)
    k.kpt = place(nc, "key_rotated_part", 167, [P, S], F32)
    k.lat_table = place(nc, "mla_table_early", 171, [P, S], F32)
    k.rk = place(nc, "ret_k", 114, [P, SC], F32)
    k.rv = place(nc, "ret_v", 119, [P, SC], F32)
    k.rq = place(nc, "ret_q", 124, [P, S], F32)
    k.rt = place(nc, "ret_t", 128, [P, S], F32)
    k.rs = place(nc, "ret_states", 132, [P, NC, P], F32)
    k.rg = place(nc, "ret_gate", 136, [P, S], F32)
    k.rtab = place(nc, "ret_table", 140, [P, 2, S], F32)
    k.kz = [[place(nc, f"ret_k_tokens_{d}_{p}", 148 + 10 * n + 5 * m, [P, NC + NCC, P], F32R)
             for m, p in enumerate(("hi", "lo"))] for n, d in enumerate(("fwd", "bwd"))]
    k.st = [[place(nc, f"ret_states_{d}_{p}", 148 + 10 * n + 5 * m, [P, NC, P], F32R)
             for m, p in enumerate(("hi", "lo"))] for n, d in enumerate(("fwd", "bwd"))]
    k.rvt = [place(nc, f"ret_v_tokens_{p}", 168 + 5 * m, [P, NC + NCC, P], F32R) for m, p in enumerate(("hi", "lo"))]
    k.rkf = [place(nc, f"ret_k_features_{p}", 178 + 4 * m, [P, S], F32R) for m, p in enumerate(("hi", "lo"))]
    k.rqf = [place(nc, f"ret_q_then_scores_{p}", 186 + 4 * m, [P, S], F32R) for m, p in enumerate(("hi", "lo"))]
    k.rxf = [place(nc, f"ret_q_decayed_{p}", 194 + 4 * m, [P, S], F32R) for m, p in enumerate(("hi", "lo"))]
    k.dec = place(nc, "ret_decays", 202, [P, 5, P], F32)
    k.zeta = place(nc, "ret_zeta", 204.5, [P, 4], F32)
    k.lg = place(nc, "log_gamma", 204.6875, [P, 4 * RH], F32)
    k.cqn = [place(nc, f"latent_q_{p}", 34 + 8 * m, [P, 2, S], F32R) for m, p in enumerate(("hi", "lo"))]
    k.ckvn = [place(nc, f"latent_kv_{p}", 50 + 10 * m, [P, 2, SC], F32R) for m, p in enumerate(("hi", "lo"))]
    k.cqr = place(nc, "latent_q_back", 70, [P, 2, S], F32)
    k.ckvr = place(nc, "latent_kv_back", 78, [P, 2, SC], F32)
    k.mk = [place(nc, f"mla_k_{p}", 88 + 5 * m, [P, SC], F32R) for m, p in enumerate(("hi", "lo"))]
    k.mq = [place(nc, f"mla_q_{p}", 98 + 4 * m, [P, S], F32R) for m, p in enumerate(("hi", "lo"))]
    k.mv = [place(nc, f"mla_v_{p}", 106 + 5 * m, [P, NC + NCC, P], F32R) for m, p in enumerate(("hi", "lo"))]
    k.mvr = place(nc, "mla_v_raw", 116, [P, SC], F32)
    k.mqf = place(nc, "mla_q_f32", 121, [P, S], F32)
    k.mqt = place(nc, "mla_q_part", 125, [P, S], F32)
    k.mtab = place(nc, "mla_table", 129, [P, S], F32)
    k.kpr = place(nc, "key_rotated_back", 133, [P, SC], F32)
    k.pt = [place(nc, f"probs_turned_{p}", 138 + 20 * m, [P, 2, NC + NCC, 2 * P], F32R) for m, p in enumerate(("hi", "lo"))]
    k.probs = place(nc, "probs", 183, [P, 2, SC], F32)
    k.mo = place(nc, "mla_out", 193, [P, S], F32)
    k.stat = place(nc, "softmax_stats", 197, [P, 4, 16], F32)
    k.fh = place(nc, "ff_hi", B + 64, [P, 2, S], F32R)
    k.fl = place(nc, "ff_lo", B + 72, [P, 2, S], F32R)
    k.fa = place(nc, "ff_a", 162, [P, 2, S], F32)
    k.fg = place(nc, "ff_g", 170, [P, 2, S], F32)
    k.fs = place(nc, "ff_silu", 178, [P, S], F32)

    k.ps = ctx.enter_context(nc.psum_tensor("psum", [P, 8 * 512], F32))

    k.sems = {}

    def sem(name):
        if name not in k.sems:
            k.sems[name] = ctx.enter_context(nc.semaphore(name))
        return k.sems[name]
    k.sem = sem
    k.T, k.B = T, B
    k.x_ready = lambda eng, c: eng.wait_ge(sem(f"x_loaded{c // 512}"), 16)
    return k


def tile_bank(slot):
    return 1536 * slot


def one(t, i):
    return t[:, bass.ds(i, 1), :].rearrange("p a n -> p (a n)")


def f32(ap):
    return ap.bitcast(F32)


def three(pe, out, lhs, rhs, start, stop, loose=False, first=None):
    (lh, ll), (rh, rl) = lhs, rhs
    mm = pe.matmul(out, lh, rh, start=start, stop=False, skip_group_check=loose)
    if first is not None:
        mm.then_inc(first, 1)
    pe.matmul(out, lh, rl, start=False, stop=False, skip_group_check=loose)
    return pe.matmul(out, ll, rh, start=False, stop=stop, skip_group_check=loose)


def gemm_tile(k, pe, tile, unit, lhs, rhs, depth, width=S, new_unit=True):
    if new_unit:
        pe.wait_ge(k.sem("weights_split"), unit.value(1))
    pe.wait_ge(k.sem(f"tile_read{tile.slot}"), tile.half(0))
    c0 = tile_bank(tile.slot)
    first = k.sem("unit_started") if new_unit else None
    chunks = [(c, min(512, width - c)) for c in range(0, width, 512)]
    for i in range(depth):
        for n, (c, w) in enumerate(chunks):
            (lh, ll), (rh, rl) = lhs(i), rhs(i, c, w)
            mm = pe.matmul(k.ps[:, c0 + c:c0 + c + w], lh, rh, start=i == 0, stop=False)
            if first is not None:
                mm.then_inc(first, 1)
                first = None
            pe.matmul(k.ps[:, c0 + c:c0 + c + w], lh, rl, start=False, stop=False)
        for c, w in chunks:
            (lh, ll), (rh, rl) = lhs(i), rhs(i, c, w)
            mm = pe.matmul(k.ps[:, c0 + c:c0 + c + w], ll, rh, start=False, stop=i == depth - 1)
    mm.then_inc(k.sem("tile_done"), 1)


def unit_block(k, slot, stride=P, base=0):
    return lambda i: (k.wh[:, slot, base + i * stride:base + i * stride + P],
                      k.wl[:, slot, base + i * stride:base + i * stride + P])


def act_of(h, l):
    return lambda i, c, w: (h[:, i, c:c + w], l[:, i, c:c + w])


def full_gemm(k, pe, tile, unit):
    gemm_tile(k, pe, tile, unit, unit_block(k, unit.slot), act_of(k.hh, k.hl), DT)


def ada_load(k, act, a, stage, i, j):
    s = ADA_STEP[stage]
    n = ADA * i + (ADA * s + j)
    act.wait_ge(k.sem("ada_used"), n + 1)
    src = a.w_ada[n] if isinstance(n, int) else a.w_ada[bass.ds(n, 1)].rearrange("a p n -> (a p) n")
    act.dma_start(k.adaw[:, :], src).then_inc(k.sem("ada_loaded"), 16)


def ada_product(k, pe, stage, i, j):
    s = ADA_STEP[stage]
    if j == 0:
        pe.wait_ge(k.sem("ada_read"), i + (s + 1))
    pe.wait_ge(k.sem("ada_loaded"), 16 * ADA * i + 16 * (ADA * s + j + 1))
    for t in range(DT):
        mm = pe.matmul(k.ps[:, 3072 + 2 * j:3074 + 2 * j], k.adaw[:, P * t:P * t + P], k.scf[:, 2 * t:2 * t + 2],
                       start=t == 0, stop=t == DT - 1)
    mm.then_inc(k.sem("ada_used"), 1)


def ada_store(k, dve, stage, i):
    s = ADA_STEP[stage]
    dve.wait_ge(k.sem("ada_used"), ADA * i + (ADA * s + ADA + 1))
    dve.tensor_copy(k.mod[:, bass.ds(ADA * i + ADA * s, ADA), :],
                    k.ps[:, 3072:3072 + 2 * ADA].rearrange("p (t n) -> p t n", n=2)).then_inc(k.sem("ada_read"), 1)


def bank(k, tile, width=S, c=0):
    b = tile_bank(tile.slot) + c
    return k.ps[:, b:b + width]


def wait_tile(k, eng, tile):
    eng.wait_ge(k.sem("tile_done"), tile.value(-1))


def read_tile(k, ins, tile):
    return ins.then_inc(k.sem(f"tile_read{tile.slot}"), 1)


def at_stage(stage, what, i, j):
    first = (FIRST_UNIT if what == "unit" else FIRST_TILE)[stage]
    per = next(s[2 if what == "unit" else 3] for s in STAGES if s[0] == stage)
    return At(first + per * i + j) if isinstance(i, int) else At(first + j, per, i)



def load_weights(k, sp, stream, last):
    for u in range(2):
        sp.dma_start(k.raw[:, u, :], stream[u]).then_inc(k.sem(f"raw_loaded{u}"), 16)
    with sp.Fori(1, last // 2) as r:
        for s in range(2):
            sp.wait_ge(k.sem("weights_split"), 2 * r + (s - 1))
            sp.dma_start(k.raw[:, s, :], stream[bass.ds(2 * r + s, 1)].rearrange("a p n -> (a p) n")
                         ).then_inc(k.sem(f"raw_loaded{s}"), 16)
    if last % 2:
        sp.wait_ge(k.sem("weights_split"), last - 2)
        sp.dma_start(k.raw[:, 0, :], stream[last - 1]).then_inc(k.sem("raw_loaded0"), 16)


def split_weights(k, pool, last):
    pool.wait_ge(k.sem("one32"), 1)

    def split(s, loaded, ready, started):
        pool.wait_ge(k.sem(f"raw_loaded{s}"), loaded)
        if started is not None:
            pool.wait_ge(k.sem("unit_started"), started)
        pool.tensor_tensor(k.wh[:, s, :], k.raw[:, s, :], k.one32[:, 0:1].to_broadcast([P, UNIT]), ALU.mult).then_inc(k.sem("weights_hi"), 1)
        pool.wait_ge(k.sem("weights_hi"), ready)
        pool.tensor_tensor(k.wl[:, s, :], k.raw[:, s, :], f32(k.wh[:, s, :]), ALU.subtract
                           ).then_inc(k.sem("weights_split"), 1)
    split(0, 16, 1, None)
    with pool.Fori(0, PAIRS) as i:
        for u in range(1, 5):
            split(u % 2, 32 * i + 16 * (u // 2 + 1), 4 * i + (u + 1), 4 * i + u)
        sb_pool(k, pool, i)
    assert FIRST_UNIT["merge_sb"] == 4 * PAIRS
    split(1, 16 * (2 * PAIRS + 1), 4 * PAIRS + 2, 4 * PAIRS + 1)
    with pool.Fori(2 * PAIRS + 1, last // 2) as r:
        for s in range(2):
            split(s, 16 * r + 16, 2 * r + (s + 1), 2 * r + s)
    if last % 2:
        split(0, 16 * (last // 2) + 16, last, last - 1)



class Norms:

    def __init__(self):
        self.m, self.c = 0, 0


def norm_tensor(k, pe, n, tiles, widths):
    for w in widths:
        b = 3072 + 512 * (n.c % 2)
        if n.c >= 2:
            pe.wait_ge(k.sem("stat_root"), n.c - 1)
        for i in range(tiles):
            s = n.m % 2
            pe.wait_ge(k.sem("square_split"), n.m + 1)
            pe.matmul(k.ps[:, b:b + w], k.ones[:, :], k.sqh[:, s, :w], start=i == 0, stop=False)
            pe.matmul(k.ps[:, b:b + w], k.ones[:, :], k.sql[:, s, :w], start=False, stop=i == tiles - 1
                      ).then_inc(k.sem("square_summed"), 1)
            n.m += 1
        n.c += 1


def norm_scalar(k, act, n, src, tiles, widths, features, ready=None):
    c0 = 0
    for w in widths:
        for i in range(tiles):
            if ready is not None:
                ready(act, c0)
            if n.m >= 2:
                act.wait_ge(k.sem("square_summed"), n.m - 1)
            act.activation(k.sqh[:, n.m % 2, :w], src(i, c0, w), ACT.Square).then_inc(k.sem("square_hi"), 1)
            n.m += 1
        b = 3072 + 512 * (n.c % 2)
        act.wait_ge(k.sem("square_summed"), n.m)
        if n.c >= 1:
            act.wait_ge(k.sem("stat_rstd"), n.c)
        act.activation(k.root[:, :w], k.ps[:, b:b + w], ACT.Sqrt, bias=EPS, scale=1.0 / features
                       ).then_inc(k.sem("stat_root"), 1)
        n.c += 1
        c0 += w


def norm_vector(k, dve, n, src, tiles, widths, ready=None):
    c0 = 0
    for w in widths:
        for i in range(tiles):
            if ready is not None:
                ready(dve, c0)
            if n.m >= 1:
                dve.wait_ge(k.sem("square_split"), n.m)
            dve.tensor_tensor(k.sq[:, :w], src(i, c0, w), src(i, c0, w), ALU.mult).then_inc(k.sem("square_done"), 1)
            dve.wait_ge(k.sem("square_done"), n.m + 1)
            dve.wait_ge(k.sem("square_hi"), n.m + 1)
            dve.tensor_tensor(k.sql[:, n.m % 2, :w], k.sq[:, :w], f32(k.sqh[:, n.m % 2, :w]), ALU.subtract
                              ).then_inc(k.sem("square_split"), 1)
            n.m += 1
        n.c += 1
        dve.wait_ge(k.sem("stat_root"), n.c)
        dve.reciprocal(k.rstd[:, c0:c0 + w], k.root[:, :w]).then_inc(k.sem("stat_rstd"), 1)
        c0 += w



LAG_CUM, LAG_OUT = 3, 7


def sb_tensor(k, pe):
    with pe.Fori(0, PAIRS) as i:
        for j in range(4):
            full_gemm(k, pe, at_stage("sb", "tile", i, j), at_stage("sb", "unit", i, j))
        v = at_stage("sb", "tile", i, 2)
        pe.wait_ge(k.sem(f"tile_read{v.slot}"), v.half(1))
        for t in range(NC):
            mm = pe.transpose(k.ps[:, 3072 + P * t:3072 + P * t + P], k.vy[:, P * t:P * t + P],
                              k.const[:, CONSTS["ident"]:CONSTS["ident"] + P])
        mm.then_inc(k.sem("sb_v_turned"), 1)
        for slot in range(2):
            last = at_stage("sb", "tile", i, 2 + slot)
            pe.wait_ge(k.sem(f"tile_read{last.slot}"), last.half(1))
        pe.wait_ge(k.sem("sb_v_split"), i + 1)
        for step in range(NB + LAG_OUT):
            n = step
            if n < NB:
                qc, kb, a, off = BLOCKS[n]
                if n >= 4:
                    pe.wait_ge(k.sem("sb_logits_read"), NB * i + (n - 3))
                b = (0, 512, 1536, 2048)[n % 4]
                r = slice(HD * a, HD * a + HD)
                q = slice(512 * qc + off, 512 * qc + 512)
                three(pe, k.ps[:, b + off:b + 512],
                      (k.kh[r, P * kb:P * kb + P], k.kl[r, P * kb:P * kb + P]), (k.qh[r, q], k.ql[r, q]),
                      True, True).then_inc(k.sem("sb_logits"), 1)
            n = step - LAG_CUM
            if 0 <= n < NB:
                qc, kb, a, off = BLOCKS[n]
                b = 3072 + 512 * a
                head = kb == 4 * qc + 3
                if not head:
                    o = BLOCKS[n - 2][3]
                    pe.wait_ge(k.sem("sb_sums_read"), NB * i + (n - 1))
                    for m in (k.sph, k.spl):
                        pe.matmul(k.ps[:, b + o:b + 512], k.tri[:, P:2 * P], m[:, (n - 2) % 4, o:512],
                                  start=False, stop=False, skip_group_check=True)
                elif n >= 2:
                    pe.wait_ge(k.sem("sb_sums_read"), NB * i + (n - 1))
                pe.wait_ge(k.sem("sb_softplus"), NB * i + (n + 1))
                pe.matmul(k.ps[:, b + off:b + 512], k.tri[:, 0:P], k.sph[:, n % 4, off:512],
                          start=head, stop=False, skip_group_check=True)
                pe.matmul(k.ps[:, b + off:b + 512], k.tri[:, 0:P], k.spl[:, n % 4, off:512],
                          start=False, stop=True, skip_group_check=True).then_inc(k.sem("sb_sums"), 1)
            n = step - LAG_OUT
            if n >= 0:
                qc, kb, a, off = BLOCKS[n]
                b = (1024, 2560)[a]
                if kb == 4 * qc + 3 and qc:
                    pe.wait_ge(k.sem("sb_out_read"), 4 * i + (a + 1))
                pe.wait_ge(k.sem("sb_weights"), NB * i + (n + 1))
                three(pe, k.ps[:, b + off:b + 512], (k.vh[:, kb, :], k.vl[:, kb, :]),
                      (k.ph[:, n % 2, off:512], k.pl[:, n % 2, off:512]),
                      kb == 4 * qc + 3, kb == 0, loose=True).then_inc(k.sem("sb_out"), 1)
        pe.wait_ge(k.sem("sb_sums_read"), NB * i + NB)
        pe.wait_ge(k.sem("sb_out_read"), 4 * i + 4)
        pe.wait_ge(k.sem("sb_logits_read"), NB * i + NB)


def sb_scalar(k, act):
    with act.Fori(0, PAIRS) as i:
        def tile(j):
            t = at_stage("sb", "tile", i, j)
            wait_tile(k, act, t)
            return bank(k, t)
        act.activation(k.qh[:, :], tile(0), ACT.Copy, scale=HD ** -0.5).then_inc(k.sem("sb_qk_hi"), 1)
        act.activation(k.kh[:, :], tile(1), ACT.Copy).then_inc(k.sem("sb_qk_hi"), 1)
        read_tile(k, act.activation(k.vy[:, :], tile(2), ACT.Copy), at_stage("sb", "tile", i, 2))
        read_tile(k, act.activation(k.sg[:, :], tile(3), ACT.Silu), at_stage("sb", "tile", i, 3))
        act.preload_act_table_set("natural_log_exp_and_others")
        act.wait_ge(k.sem("sb_v_turned"), i + 1)
        act.activation(k.vh[:, :, :], k.ps[:, 3072:4096].rearrange("p (t n) -> p t n", t=NC), ACT.Copy).then_inc(k.sem("sb_v_hi"), 1)
        for step in range(NB + 6):
            n = step
            if n < NB:
                off = BLOCKS[n][3]
                act.wait_ge(k.sem("sb_logits"), NB * i + (n + 1))
                if n >= NLOGIT:
                    act.wait_ge(k.sem("sb_weights"), NB * i + (n - NLOGIT + 1))
                b = (0, 512, 1536, 2048)[n % 4]
                act.activation(k.logit[:, n % NLOGIT, off:512], k.ps[:, b + off:b + 512], ACT.Copy
                               ).then_inc(k.sem("sb_logits_read"), 1)
            n = step - 1
            if 0 <= n < NB:
                off = BLOCKS[n][3]
                act.wait_ge(k.sem("sb_clamped"), NB * i + (n + 1))
                act.activation(k.ex[:, n % NEX, off:512], k.ex[:, n % NEX, off:512], ACT.Exp).then_inc(k.sem("sb_exp"), 1)
            m = step - 5
            if 0 <= m < NB:
                mo = BLOCKS[m][3]
                act.wait_ge(k.sem("sb_sums_read"), NB * i + (m + 1))
                act.activation(k.logit[:, m % NLOGIT, mo:512], k.logit[:, m % NLOGIT, mo:512], ACT.Exp).then_inc(k.sem("sb_weight"), 1)
            if 0 <= n < NB:
                act.wait_ge(k.sem("sb_exp"), NB * i + (n + 1))
                act.activation(k.ex[:, n % NEX, off:512], k.ex[:, n % NEX, off:512], ACT.Ln, bias=1.0
                               ).then_inc(k.sem("sb_log"), 1)
            if 0 <= m < NB:
                act.wait_ge(k.sem("sb_weight"), NB * i + (m + 1))
                if m >= 2:
                    act.wait_ge(k.sem("sb_out"), NB * i + (m - 1))
                act.activation(k.ph[:, m % 2, mo:512], k.logit[:, m % NLOGIT, mo:512], ACT.Copy).then_inc(k.sem("sb_weight_hi"), 1)
        act.wait_ge(k.sem("sb_out_read"), 4 * i + 4)
        act.activation(one(k.yh, i), k.vy[:, :], ACT.Copy).then_inc(k.sem("sb_y_hi"), 1)


def sb_pool(k, pool, i):
    for step in range(2, NB + 6):
        n = step - 6
        if n >= 0:
            off = BLOCKS[n][3]
            pool.wait_ge(k.sem("sb_weight_hi"), NB * i + (n + 1))
            pool.tensor_tensor(k.pl[:, n % 2, off:512], k.logit[:, n % NLOGIT, off:512],
                               f32(k.ph[:, n % 2, off:512]), ALU.subtract).then_inc(k.sem("sb_weights"), 1)
        n = step - 2
        if n < NB:
            off = BLOCKS[n][3]
            pool.wait_ge(k.sem("sb_softplus_hi"), NB * i + (n + 1))
            pool.tensor_tensor(k.spl[:, n % 4, off:512], k.ex[:, n % NEX, off:512],
                               f32(k.sph[:, n % 4, off:512]), ALU.subtract).then_inc(k.sem("sb_softplus"), 1)


def sb_vector(k, dve):
    col = CONSTS
    mask, mneg = k.const[:, col["mask"]:col["mask"] + P], k.const[:, col["mneg"]:col["mneg"] + P]
    with dve.Fori(0, PAIRS) as i:
        for j, (hi, lo, scale) in enumerate(((k.qh, k.ql, HD ** -0.5), (k.kh, k.kl, 1.0))):
            t = at_stage("sb", "tile", i, j)
            dve.wait_ge(k.sem("sb_qk_hi"), 2 * i + (j + 1))
            read_tile(k, dve.scalar_tensor_tensor(lo[:, :], bank(k, t), scale, f32(hi[:, :]), ALU.mult,
                                                  ALU.subtract), t)
        dve.wait_ge(k.sem("sb_v_hi"), i + 1)
        dve.tensor_tensor(k.vl[:, :, :], k.ps[:, 3072:4096].rearrange("p (t n) -> p t n", t=NC),
                          f32(k.vh[:, :, :]), ALU.subtract).then_inc(k.sem("sb_v_split"), 1)
        for step in range(NB + LAG_OUT):
            n = step - 2
            if 0 <= n < NB:
                off = BLOCKS[n][3]
                dve.wait_ge(k.sem("sb_log"), NB * i + (n + 1))
                dve.tensor_tensor(k.ex[:, n % NEX, off:512], k.logit[:, n % NLOGIT, off:512], k.ex[:, n % NEX, off:512], ALU.max
                                  ).then_inc(k.sem("sb_max"), 1)
            n = step - 1
            if 0 <= n < NB:
                off = BLOCKS[n][3]
                dve.wait_ge(k.sem("sb_logits_read"), NB * i + (n + 1))
                if n >= NEX:
                    dve.wait_ge(k.sem("sb_softplus"), NB * i + (n - NEX + 1))
                dve.tensor_scalar(k.ex[:, n % NEX, off:512], k.logit[:, n % NLOGIT, off:512], CLAMP, None, ALU.min
                                  ).then_inc(k.sem("sb_clamped"), 1)
            n = step - 2
            if 0 <= n < NB:
                qc, kb, a, off = BLOCKS[n]
                dve.wait_ge(k.sem("sb_max"), NB * i + (n + 1))
                d = slice(off, off + P)
                if kb >= 4 * qc:
                    dve.tensor_tensor(k.ex[:, n % NEX, d], k.ex[:, n % NEX, d], mask, ALU.mult).then_inc(k.sem("sb_masked"), 1)
                    dve.wait_ge(k.sem("sb_masked"), 16 * i + (1 + sum(b[1] >= 4 * b[0] for b in BLOCKS[:n])))
                if n >= 4:
                    dve.wait_ge(k.sem("sb_sums"), NB * i + (n - 1))
                dve.tensor_copy(k.sph[:, n % 4, off:512], k.ex[:, n % NEX, off:512]).then_inc(k.sem("sb_softplus_hi"), 1)
            m = step - 4
            if 0 <= m < NB:
                mqc, mkb, ma, moff = BLOCKS[m]
                b = 3072 + 512 * ma
                dve.wait_ge(k.sem("sb_sums"), NB * i + (m + 1))
                dve.tensor_tensor(k.logit[:, m % NLOGIT, moff:512], k.logit[:, m % NLOGIT, moff:512], k.ps[:, b + moff:b + 512],
                                  ALU.subtract).then_inc(k.sem("sb_sub" if mkb >= 4 * mqc else "sb_sums_read"), 1)
            if 0 <= m < NB and mkb >= 4 * mqc:
                d = slice(moff, moff + P)
                dve.wait_ge(k.sem("sb_sub"), 16 * i + (1 + sum(b[1] >= 4 * b[0] for b in BLOCKS[:m])))
                dve.tensor_tensor(k.logit[:, m % NLOGIT, d], k.logit[:, m % NLOGIT, d], mneg, ALU.min
                                  ).then_inc(k.sem("sb_sums_read"), 1)
            n = step - LAG_OUT
            if n >= 0 and BLOCKS[n][1] == 0:
                qc, kb, a, off = BLOCKS[n]
                b, r, q = (1024, 2560)[a], slice(HD * a, HD * a + HD), slice(512 * qc, 512 * qc + 512)
                g = at_stage("sb", "tile", i, 3)
                dve.wait_ge(k.sem(f"tile_read{g.slot}"), g.half(1))
                dve.wait_ge(k.sem("sb_out"), NB * i + (n + 1))
                dve.tensor_tensor(k.vy[r, q], k.sg[r, q], k.ps[r, b:b + 512], ALU.mult
                                  ).then_inc(k.sem("sb_out_read"), 1)
        dve.wait_ge(k.sem("sb_weights"), NB * i + NB)
        dve.wait_ge(k.sem("sb_softplus"), NB * i + NB)
        dve.wait_ge(k.sem("sb_y_hi"), i + 1)
        dve.tensor_tensor(one(k.yl, i), k.vy[:, :], f32(one(k.yh, i)), ALU.subtract
                          ).then_inc(k.sem("branch_split"), 1)



def loads_scalar(k, act, a):
    act.dma_start(k.const[:, :], a.consts).then_inc(k.sem("const_loaded"), 16)
    act.dma_start(k.params[:, :], a.params).then_inc(k.sem("params_loaded"), 16)
    for c in range(NCH):
        act.dma_start(k.x[:, :, 512 * c:512 * c + 512], a.x[:, :, 512 * c:512 * c + 512]
                      ).then_inc(k.sem(f"x_loaded{c}"), 16)


def start_scalar(k, act):
    act.wait_ge(k.sem("params_loaded"), 16)
    c = k.params[:, PARAMS["c"]:PARAMS["c"] + 2 * DT]
    act.activation(k.scf[:, :], c, ACT.Silu).then_inc(k.sem("silu_c"), 1)
    act.wait_ge(k.sem("const_loaded"), 16)
    act.activation(k.tri[:, :], k.const[:, CONSTS["tri"]:CONSTS["tri"] + 2 * P], ACT.Copy).then_inc(k.sem("start_ready"), 1)


def start_vector(k, dve):
    dve.memset(k.one32[:, :], 1.0).then_inc(k.sem("one32"), 1)
    dve.wait_ge(k.sem("one32"), 1)
    dve.tensor_copy(k.ones[:, :], k.one32[:, :]).then_inc(k.sem("ones_ready"), 1)
    for s in range(2):
        dve.memset(k.idle[:, s:s + 1], 0.0).then_inc(k.sem(f"tile_read{s}"), 1)
    for s, name in ((2, "ada_used"), (3, "ada_read")):
        dve.memset(k.idle[:, s:s + 1], 0.0).then_inc(k.sem(name), 1)


class Applies:
    def __init__(self):
        self.n = 0


def apply_scalar(k, act, ap, hi, tiles, width, bias=None, free=None, at=0):
    for c in range(0, width, 512):
        w = min(512, width - c)
        for i in range(tiles):
            act.wait_ge(k.sem("normed"), ap.n + 1)
            src = k.nt[:, ap.n % 2, :w]
            dst = hi[:, i, at + c:at + c + w]
            (act.activation(dst, src, ACT.Copy) if bias is None else
             act.activation(dst, src, ACT.Identity, bias=bias(i))).then_inc(k.sem("normed_hi"), 1)
            ap.n += 1


def apply_vector(k, dve, ap, src, gain, hi, lo, tiles, width, bias=None, at=0):
    def low(n, i, c, w):
        dve.wait_ge(k.sem("normed_hi"), n + 1)
        h, dst, t = f32(hi[:, i, at + c:at + c + w]), lo[:, i, at + c:at + c + w], k.nt[:, n % 2, :w]
        (dve.tensor_tensor(dst, t, h, ALU.subtract) if bias is None else
         dve.scalar_tensor_tensor(dst, t, bias(i), h, ALU.add, ALU.subtract)).then_inc(k.sem("normed_split"), 1)
    before = None
    for c in range(0, width, 512):
        w = min(512, width - c)
        for i in range(tiles):
            if ap.n >= 2:
                dve.wait_ge(k.sem("normed_split"), ap.n - 1)
            dve.scalar_tensor_tensor(k.nt[:, ap.n % 2, :w], src(i, c, w), gain(i), k.rstd[:, c:c + w],
                                     ALU.mult, ALU.mult).then_inc(k.sem("normed"), 1)
            if before:
                low(*before)
            before = (ap.n, i, c, w)
            ap.n += 1
    low(*before)


def tiles_of(t, at=0):
    return lambda i, c, w: t[:, i, at + c:at + c + w]


def col(k, name, i=0):
    return k.params[:, PARAMS[name] + i:PARAMS[name] + i + 1]



def merge_tensor(k, pe, stage, b):
    with pe.Fori(0, 2) as i:
        for h in range(2):
            for j in range(2):
                full_gemm(k, pe, at_stage(stage, "tile", i, 4 * h + j), at_stage(stage, "unit", i, 3 * h + j))
                ada_product(k, pe, stage, i, 2 * h + j)
            pe.wait_ge(k.sem("branch_split"), BT * (b + 1))
            for j in range(2):
                u = at_stage(stage, "unit", i, 3 * h + 2)
                gemm_tile(k, pe, at_stage(stage, "tile", i, 4 * h + 2 + j), u,
                          unit_block(k, u.slot, 2 * P, P * j), act_of(k.yh, k.yl), BT, new_unit=j == 0)


def merge_scalar(k, act, a, stage, b):
    with act.Fori(0, 2) as i:
        for h in range(2):
            for j in range(2):
                ada_load(k, act, a, stage, i, 2 * h + j)
                t = at_stage(stage, "tile", i, 4 * h + j)
                wait_tile(k, act, t)
                read_tile(k, act.activation(k.sig[:, j, :], bank(k, t), ACT.Sigmoid), t)


def merge_vector(k, dve, stage, b):
    with dve.Fori(0, 2) as i:
        for h in range(2):
            for j in range(2):
                n = 2 * h + j
                g, t = at_stage(stage, "tile", i, 4 * h + j), at_stage(stage, "tile", i, 4 * h + 2 + j)
                dve.wait_ge(k.sem(f"tile_read{g.slot}"), g.half(1))
                wait_tile(k, dve, t)
                acc = one(k.merged, 4 * i + n)
                if b == 0:
                    read_tile(k, dve.tensor_tensor(acc, k.sig[:, j, :], bank(k, t), ALU.mult), t)
                else:
                    read_tile(k, dve.tensor_tensor(k.prod[:, :], k.sig[:, j, :], bank(k, t), ALU.mult), t)
                    dve.wait_ge(k.sem(f"tile_read{t.slot}"), t.half(1))
                    dve.tensor_tensor(acc, acc, k.prod[:, :], ALU.add).then_inc(k.sem("merged_sum"), 1)
                    dve.wait_ge(k.sem("merged_sum"), 8 * (b - 1) + 4 * i + (n + 1))
        ada_store(k, dve, stage, i)



def pool_tensor(k, pe):
    with pe.Fori(0, 2) as i:
        for h in range(2):
            for j in range(2):
                full_gemm(k, pe, at_stage("pool", "tile", i, 3 * h + j), at_stage("pool", "unit", i, 3 * h + j))
                ada_product(k, pe, "pool", i, 2 * h + j)
            pe.wait_ge(k.sem("pooled_split"), 2 * i + (h + 1))
            u = at_stage("pool", "unit", i, 3 * h + 2)
            gemm_tile(k, pe, at_stage("pool", "tile", i, 3 * h + 2), u, unit_block(k, u.slot),
                      lambda _, c, w: (k.poh[:, c:c + w], k.pol[:, c:c + w]), 1)


def pool_scalar(k, act, a):
    for g in range(BT):
        ada_load(k, act, a, "pool", g // 2, 2 * (g % 2))
        t = at_stage("pool", "tile", g // 2, 3 * (g % 2))
        wait_tile(k, act, t)
        read_tile(k, act.activation(k.pv[:, :], bank(k, t), ACT.Copy), t)
        ada_load(k, act, a, "pool", g // 2, 2 * (g % 2) + 1)
        t = at_stage("pool", "tile", g // 2, 3 * (g % 2) + 1)
        wait_tile(k, act, t)
        read_tile(k, act.activation(k.psg[:, :], bank(k, t), ACT.Silu), t)
        act.wait_ge(k.sem("pooled"), g + 1)
        act.activation(k.poh[:, :], k.pa[:, :], ACT.Copy).then_inc(k.sem("pooled_hi"), 1)
        t = at_stage("pool", "tile", g // 2, 3 * (g % 2) + 2)
        act.wait_ge(k.sem(f"tile_read{t.slot}"), t.half(1))
        act.activation(k.yh[:, g, :], k.py[:, :], ACT.Copy).then_inc(k.sem("pool_y_hi"), 1)


def pool_vector(k, dve, ch):
    for g, w in enumerate(POOL_WINDOWS):
        t = at_stage("pool", "tile", g // 2, 3 * (g % 2))
        dve.wait_ge(k.sem(f"tile_read{t.slot}"), t.half(1))
        src, bufs, d = k.pv, [k.pa, k.pb], 1
        if (w.bit_length() - 1) % 2 == 0:
            bufs = [k.pb, k.pa]
        while d < w:
            dst = bufs[0]
            ch(dve.tensor_copy(dst[:, 0:d], src[:, 0:d]))
            ch(dve.tensor_tensor(dst[:, d:], src[:, d:], src[:, :S - d], ALU.add))
            src, bufs, d = dst, bufs[::-1], 2 * d
        n = CONSTS["cnt"] + 16 * g
        ch(dve.tensor_tensor(k.pa[:, 0:16], k.pa[:, 0:16], k.const[:, n:n + 16], ALU.mult))
        dve.scalar_tensor_tensor(k.pa[:, :], k.pa[:, :], 1.0 / w, k.pv[:, :], ALU.mult, ALU.subtract
                                 ).then_inc(k.sem("pooled"), 1)
        dve.wait_ge(k.sem("pooled_hi"), g + 1)
        dve.tensor_tensor(k.pol[:, :], k.pa[:, :], f32(k.poh[:, :]), ALU.subtract).then_inc(k.sem("pooled_split"), 1)
        dve.wait_ge(k.sem("pooled_split"), g + 1)
        t = at_stage("pool", "tile", g // 2, 3 * (g % 2) + 1)
        dve.wait_ge(k.sem(f"tile_read{t.slot}"), t.half(1))
        t = at_stage("pool", "tile", g // 2, 3 * (g % 2) + 2)
        wait_tile(k, dve, t)
        read_tile(k, dve.scalar_tensor_tensor(k.py[:, :], bank(k, t), col(k, "pool_scale", g), k.psg[:, :],
                                              ALU.mult, ALU.mult), t)
        dve.wait_ge(k.sem("pool_y_hi"), g + 1)
        dve.tensor_tensor(k.yl[:, g, :], k.py[:, :], f32(k.yh[:, g, :]), ALU.subtract).then_inc(k.sem("branch_split"), 1)
        if g % 2:
            ada_store(k, dve, "pool", g // 2)



def conv_tensor(k, pe):
    with pe.Fori(0, BT) as i:
        for j in range(4):
            full_gemm(k, pe, at_stage("conv", "tile", i, j), at_stage("conv", "unit", i, j))
            ada_product(k, pe, "conv", i, j)


def conv_scalar(k, act, a):
    with act.Fori(0, BT) as i:
        ada_load(k, act, a, "conv", i, 0)
        t = at_stage("conv", "tile", i, 0)
        wait_tile(k, act, t)
        read_tile(k, act.activation(k.cg[:, :], bank(k, t), ACT.Copy), t)
        for j in (1, 2, 3):
            ada_load(k, act, a, "conv", i, j)
        t = at_stage("conv", "tile", i, 3)
        wait_tile(k, act, t)
        read_tile(k, act.activation(k.csg[:, :], bank(k, t), ACT.Silu), t)
        act.wait_ge(k.sem("conv_y"), i + 1)
        act.activation(one(k.yh, i), k.cy[:, :], ACT.Copy).then_inc(k.sem("conv_y_hi"), 1)


def conv_vector(k, dve, ch):
    def param(i, j):
        return k.params[:, bass.ds(4 * i + (PARAMS["conv"] + j), 1)]
    with dve.Fori(0, BT) as i, ch.body(i, 3, BT):
        t = at_stage("conv", "tile", i, 0)
        dve.wait_ge(k.sem(f"tile_read{t.slot}"), t.half(1))
        t = at_stage("conv", "tile", i, 1)
        wait_tile(k, dve, t)
        read_tile(k, dve.tensor_tensor(k.cz[:, :], k.cg[:, :], bank(k, t), ALU.mult), t)
        dve.wait_ge(k.sem(f"tile_read{t.slot}"), t.half(1))
        ch(dve.tensor_scalar(k.cy[:, :], k.cz[:, :], param(i, 2), param(i, 3), ALU.mult, ALU.add))
        for j in range(2):
            d = 2 - j
            ch(dve.scalar_tensor_tensor(k.cy[:, d:], k.cz[:, :S - d], param(i, j), k.cy[:, d:], ALU.mult, ALU.add))
        t = at_stage("conv", "tile", i, 2)
        wait_tile(k, dve, t)
        read_tile(k, dve.tensor_tensor(k.cy[:, :], k.cy[:, :], bank(k, t), ALU.mult), t)
        dve.wait_ge(k.sem(f"tile_read{t.slot}"), t.half(1))
        t = at_stage("conv", "tile", i, 3)
        dve.wait_ge(k.sem(f"tile_read{t.slot}"), t.half(1))
        dve.tensor_tensor(k.cy[:, :], k.cy[:, :], k.csg[:, :], ALU.mult).then_inc(k.sem("conv_y"), 1)
        dve.wait_ge(k.sem("conv_y_hi"), i + 1)
        dve.tensor_tensor(one(k.yl, i), k.cy[:, :], f32(one(k.yh, i)), ALU.subtract).then_inc(k.sem("branch_split"), 1)
        ada_store(k, dve, "conv", i)



def out1_tensor(k, pe):
    for j in range(DT):
        if j == 0:
            pe.wait_ge(k.sem("merged_split"), DT)
        full_gemm(k, pe, at_stage("out1", "tile", 0, j), at_stage("out1", "unit", 0, j))


def out1_scalar(k, act):
    t = at_stage("out1", "tile", 0, 0)
    wait_tile(k, act, t.plus(-1))
    act.wait_ge(k.sem("merged_sum"), 2 * DT)
    for i in range(DT):
        act.activation(k.hh[:, i, :], k.merged[:, i, :], ACT.Copy).then_inc(k.sem("merged_hi"), 1)


def out1_copies_scalar(k, act):
    for j in range(DT):
        t = at_stage("out1", "tile", 0, j)
        wait_tile(k, act, t)
        read_tile(k, act.activation(k.outr[:, j, :], bank(k, t), ACT.Copy), t)


def out1_vector(k, dve):
    for i in range(DT):
        dve.wait_ge(k.sem("merged_hi"), i + 1)
        dve.tensor_tensor(k.hl[:, i, :], k.merged[:, i, :], f32(k.hh[:, i, :]), ALU.subtract
                          ).then_inc(k.sem("merged_split"), 1)



def enter_scalar(k, act, a, n, ap):
    act.wait_ge(k.sem("merged_split"), DT)
    for c in range(NCH):
        act.dma_start(k.x[:, :, 512 * c:512 * c + 512], a.x[:, :, 512 * c:512 * c + 512]
                      ).then_inc(k.sem(f"x_back{c}"), 16)
    act.dma_start(k.ctx[:, :, :], a.ctx).then_inc(k.sem("ctx_loaded"), 16)
    out1_copies_scalar(k, act)
    norm_scalar(k, act, n, tiles_of(k.outr), DT, [512, 512], D)
    norm_scalar(k, act, n, tiles_of(k.x), DT, [512, 512], D,
                ready=lambda e, c: e.wait_ge(k.sem("x1_done"), DT * (1 + c // 512)))
    apply_scalar(k, act, ap, k.h2h, DT, S, bias=lambda i: k.mod[:, i, 0:1])
    norm_scalar(k, act, n, tiles_of(k.ctx), DT, [CTX], D, ready=lambda e, c: e.wait_ge(k.sem("ctx_loaded"), 16))
    apply_scalar(k, act, ap, k.h2h, DT, CTX, bias=lambda i: k.mod[:, i, 1:2], at=S)
    act.dma_start(a.x1_store, k.x[:, :, :]).then_inc(k.sem("x1_stored"), 16)
    act.wait_ge(k.sem("normed_split"), ap.n)
    act.dma_start(k.lat_table[:, :], a.mla_table).then_inc(k.sem("lat_table"), 16)
    act.wait_ge(k.sem("x1_stored"), 16)


def enter_vector(k, dve, n, ap, ch):
    dve.wait_ge(k.sem("ada_read"), 6 * DT // ADA + 1)
    for v in range(2):
        ch(dve.tensor_tensor(k.mod[:, :, v], k.mod[:, :, v],
                             k.params[:, PARAMS["b_ada"]:PARAMS["b_ada"] + 6 * DT], ALU.add))
    for j, (first, v, g) in enumerate(((DT, 0, "g1"), (DT, 1, "g1"), (4 * DT, 0, "g2"))):
        ch(dve.scalar_tensor_tensor(k.gm[:, DT * j:DT * j + DT], k.mod[:, first:first + DT, v], 1.0,
                                    k.params[:, PARAMS[g]:PARAMS[g] + DT], ALU.add, ALU.mult))

    def out_ready(e, c):
        t = at_stage("out1", "tile", 0, DT - 1)
        e.wait_ge(k.sem(f"tile_read{t.slot}"), t.half(1))
        e.wait_ge(k.sem(f"tile_read{t.plus(-1).slot}"), t.plus(-1).half(1))
    norm_vector(k, dve, n, tiles_of(k.outr), DT, [512, 512], ready=out_ready)
    dve.wait_ge(k.sem("stat_rstd"), n.c)
    for c in range(NCH):
        dve.wait_ge(k.sem(f"x_back{c}"), 16)
        s = slice(512 * c, 512 * c + 512)
        for i in range(DT):
            ch(dve.scalar_tensor_tensor(k.outr[:, i, s], k.outr[:, i, s], col(k, "post_g", i), k.rstd[:, s],
                                        ALU.mult, ALU.mult))
            dve.tensor_tensor(k.x[:, i, s], k.x[:, i, s], k.outr[:, i, s], ALU.add).then_inc(k.sem("x1_done"), 1)
    dve.wait_ge(k.sem("x1_done"), NCH * DT)
    norm_vector(k, dve, n, tiles_of(k.x), DT, [512, 512])
    dve.wait_ge(k.sem("stat_rstd"), n.c)
    apply_vector(k, dve, ap, tiles_of(k.x), lambda i: k.gm[:, i:i + 1], k.h2h, k.h2l, DT, S,
                 bias=lambda i: k.mod[:, i, 0:1])
    norm_vector(k, dve, n, tiles_of(k.ctx), DT, [CTX], ready=lambda e, c: e.wait_ge(k.sem("ctx_loaded"), 16))
    dve.wait_ge(k.sem("stat_rstd"), n.c)
    apply_vector(k, dve, ap, tiles_of(k.ctx), lambda i: k.gm[:, DT + i:DT + i + 1], k.h2h, k.h2l, DT, CTX,
                 bias=lambda i: k.mod[:, i, 1:2], at=S)
    dve.wait_ge(k.sem("normed_split"), ap.n)


def enter_tensor(k, pe, n):
    norm_tensor(k, pe, n, DT, [512, 512])
    norm_tensor(k, pe, n, DT, [512, 512])
    norm_tensor(k, pe, n, DT, [CTX])



def h2_gemm(k, pe, tile, unit, width):
    gemm_tile(k, pe, tile, unit, unit_block(k, unit.slot), act_of(k.h2h, k.h2l), DT, width)


LATENTS = (S, S, SC, SC, SC)


def latents_tensor(k, pe, n_applied):
    pe.wait_ge(k.sem("normed_split"), n_applied)
    for j, width in enumerate(LATENTS):
        h2_gemm(k, pe, at_stage("latents", "tile", 0, j), at_stage("latents", "unit", 0, j), width)


def latents_scalar(k, act, a):
    for j in range(4):
        t = at_stage("latents", "tile", 0, j)
        wait_tile(k, act, t)
        dst = k.cq[:, j, :] if j < 2 else k.ckv[:, j - 2, :]
        read_tile(k, act.activation(dst, bank(k, t, LATENTS[j]), ACT.Copy), t)
    for j in (2, 3):
        t = at_stage("latents", "tile", 0, j)
        act.wait_ge(k.sem(f"tile_read{t.slot}"), t.half(1))
    act.dma_start(a.cq_store, k.cq[:, :, :]).then_inc(k.sem("latents_stored"), 16)
    act.dma_start(a.ckv_store, k.ckv[:, :, :]).then_inc(k.sem("latents_stored"), 16)
    act.wait_ge(k.sem("key_rotated"), 1)
    act.dma_start(a.kpe_store, k.kpe[64:96, :]).then_inc(k.sem("latents_stored"), 16)
    act.wait_ge(k.sem("latents_stored"), 48)
    act.dma_start(k.rtab[:, :, :], a.ret_table).then_inc(k.sem("ret_table"), 16)


def latents_vector(k, dve, ch):
    t = at_stage("latents", "tile", 0, 4)
    dve.wait_ge(k.sem("lat_table"), 16)
    wait_tile(k, dve, t)
    ch(dve.tensor_tensor(k.kpe[64:96, 0:S], k.lat_table[64:96, :], bank(k, t)[64:96, :], ALU.mult))
    ch(dve.tensor_tensor(k.kpt[64:96, :], k.lat_table[96:128, :], bank(k, t)[96:128, :], ALU.mult))
    read_tile(k, dve.tensor_copy(k.kpe[64:96, S:SC], bank(k, t, CTX, S)[64:96, :]), t)
    dve.wait_ge(k.sem(f"tile_read{t.slot}"), t.half(1))
    dve.tensor_tensor(k.kpe[64:96, 0:S], k.kpe[64:96, 0:S], k.kpt[64:96, :], ALU.add).then_inc(k.sem("key_rotated"), 1)


RK, RV, RQ, RKT, RVT, RSC, RG, RDF, RDB, RO, RM, RVAR = range(12)


def ret_tensor(k, pe):
    ident = k.const[:, CONSTS["ident"]:CONSTS["ident"] + P]
    hi_lo = lambda pair, s: (pair[0][s], pair[1][s])

    def chunk(pair, c):
        return pair[0][:, c, :], pair[1][:, c, :]

    def cols(pair, c):
        return pair[0][:, P * c:P * c + P], pair[1][:, P * c:P * c + P]

    with pe.Fori(0, RH) as i:
        tile = lambda j: at_stage("ret", "tile", i, j)

        def begin(j):
            t = tile(j)
            pe.wait_ge(k.sem(f"tile_read{t.slot}"), t.half(0))
            return tile_bank(t.slot)

        for j, width in ((RK, SC), (RV, SC), (RQ, S)):
            h2_gemm(k, pe, tile(j), at_stage("ret", "unit", i, j), width)
        for j, src, ready in ((RKT, k.rk, "ret_k_roped"), (RVT, k.rv, None)):
            b = begin(j)
            if ready:
                pe.wait_ge(k.sem(ready), i + 1)
            else:
                t = tile(RV)
                pe.wait_ge(k.sem(f"tile_read{t.slot}"), t.half(1))
            for c in range(NC + NCC):
                mm = pe.transpose(k.ps[:, b + P * c:b + P * c + P], src[:, P * c:P * c + P], ident)
            mm.then_inc(k.sem("tile_done"), 1)
        b = begin(RSC)
        pe.wait_ge(k.sem("ret_qk_split"), 2 * i + 2)
        for c in range(NC):
            mm = three(pe, k.ps[:, b + P * c:b + P * c + P], cols(k.rkf, c), cols(k.rqf, c), True, True)
        mm.then_inc(k.sem("tile_done"), 1)
        h2_gemm(k, pe, tile(RG), at_stage("ret", "unit", i, 3), S)
        t = tile(RVT)
        pe.wait_ge(k.sem(f"tile_read{t.slot}"), t.half(1))
        t = tile(RKT)
        pe.wait_ge(k.sem(f"tile_read{t.slot}"), t.half(1))
        for d, j in enumerate((RDF, RDB)):
            b = begin(j)
            for c in range(NC + NCC):
                mm = three(pe, k.ps[:, b + P * c:b + P * c + P], chunk(k.kz[d], c), chunk(k.rvt, c), True, True)
            mm.then_inc(k.sem("tile_done"), 1)
        b = begin(RO)

        def outs(c):
            return k.ps[:, b + P * c:b + P * c + P]
        pe.wait_ge(k.sem("ret_scores_split"), i + 1)
        for c in range(NC):
            three(pe, outs(c), chunk(k.rvt, c), cols(k.rqf, c), c % 4 == 0, False, loose=True)
        for d, x in enumerate((k.rxf, k.rkf)):
            pe.wait_ge(k.sem("ret_states_split"), 2 * i + (d + 1))
            pe.wait_ge(k.sem("ret_decayed_split"), 2 * i + (d + 1))
            for c in range(NC):
                mm = three(pe, outs(c), chunk(k.st[d], c), cols(x, c), False, d == 1, loose=True)
        mm.then_inc(k.sem("tile_done"), 1)
        for n, (j, pair) in enumerate(((RM, k.rxf), (RVAR, k.rkf))):
            b = begin(j)
            pe.wait_ge(k.sem("ret_stat_split"), 2 * i + (n + 1))
            for c in range(NCH):
                s = slice(512 * c, 512 * c + 512)
                pe.matmul(k.ps[:, b + 512 * c:b + 512 * c + 512], k.ones[:, :], pair[0][:, s], start=True, stop=False)
                mm = pe.matmul(k.ps[:, b + 512 * c:b + 512 * c + 512], k.ones[:, :], pair[1][:, s], start=False, stop=True)
            mm.then_inc(k.sem("tile_done"), 1)


def ret_scalar(k, act, a, ch):
    C = lambda name, w=P: k.const[:, CONSTS[name]:CONSTS[name] + w]
    ch(act.activation(k.lg[:, 0:2 * RH], k.params[:, PARAMS["decay"]:PARAMS["decay"] + 2 * RH], ACT.Exp))
    ch(act.activation(k.lg[:, 0:2 * RH], k.lg[:, 0:2 * RH], ACT.Copy, scale=-1.0))
    act.activation(k.lg[:, 2 * RH:], k.lg[:, 0:2 * RH], ACT.Exp, scale=float(P)).then_inc(k.sem("ret_gammas"), 1)
    act.wait_ge(k.sem("ret_gammas"), 1)

    with act.Fori(0, RH) as i, ch.body(i, 1, RH):
        tile = lambda j: at_stage("ret", "tile", i, j)
        lf, lb = k.lg[:, bass.ds(i, 1)], k.lg[:, bass.ds(i + RH, 1)]
        for src, dst, s in ((C("fwd"), k.dec[:, 0, :], lf), (C("bwd"), k.dec[:, 1, :], lb),
                            (C("xf"), k.dec[:, 3, :], lf), (C("xb"), k.dec[:, 4, :], lb),
                            (C("zf", 1), k.zeta[:, 0:1], lf), (C("zb", 1), k.zeta[:, 1:2], lb)):
            act.activation(dst, src, ACT.Exp, scale=s).then_inc(k.sem("ret_decays"), 1)

        def wait_read(j):
            t = tile(j)
            act.wait_ge(k.sem(f"tile_read{t.slot}"), t.half(1))
        wait_tile(k, act, tile(RV))
        read_tile(k, act.activation(k.rv[:, :], bank(k, tile(RV), SC), ACT.Copy), tile(RV))
        act.wait_ge(k.sem("ret_k_roped"), i + 1)
        act.activation(k.rkf[0][:, :], k.rk[:, 0:S], ACT.Copy, scale=RET_SCALE).then_inc(k.sem("ret_qk_hi"), 1)
        act.wait_ge(k.sem("ret_q_roped"), i + 1)
        act.activation(k.rqf[0][:, :], k.rq[:, :], ACT.Copy).then_inc(k.sem("ret_qk_hi"), 1)
        act.wait_ge(k.sem("ret_zetas"), i + 1)
        wait_tile(k, act, tile(RKT))
        for d in range(2):
            act.activation(k.kz[d][0][:, :, :], bank(k, tile(RKT), SC).rearrange("p (c n) -> p c n", n=P), ACT.Copy,
                           scale=k.zeta[:, 2 + d:3 + d]).then_inc(k.sem("ret_kz_hi"), 1)
        wait_tile(k, act, tile(RVT))
        act.activation(k.rvt[0][:, :, :], bank(k, tile(RVT), SC).rearrange("p (c n) -> p c n", n=P), ACT.Copy
                       ).then_inc(k.sem("ret_vt_hi"), 1)
        wait_read(RSC)
        act.activation(k.rqf[0][:, :], k.rt[:, :], ACT.Copy).then_inc(k.sem("ret_scores_hi"), 1)
        wait_tile(k, act, tile(RG))
        read_tile(k, act.activation(k.rg[:, :], bank(k, tile(RG)), ACT.Silu), tile(RG))
        for d, x in enumerate((k.rxf, k.rkf)):
            act.wait_ge(k.sem("ret_decayed"), 2 * i + (d + 1))
            act.activation(x[0][:, :], k.rt[:, :] if d else k.rv[:, 0:S], ACT.Copy).then_inc(k.sem("ret_decayed_hi"), 1)
            wait_read((RDF, RDB)[d])
            act.activation(k.st[d][0][:, :, :], k.rs[:, :, :], ACT.Copy).then_inc(k.sem("ret_states_hi"), 1)
        wait_tile(k, act, tile(RO))
        act.wait_ge(k.sem("ret_decayed_split"), 2 * i + 2)
        read_tile(k, act.activation(k.rq[:, :], bank(k, tile(RO)), ACT.Copy), tile(RO))
        wait_read(RO)
        act.activation(k.rxf[0][:, :], k.rq[:, :], ACT.Copy).then_inc(k.sem("ret_stat_hi"), 1)
        wait_read(RM)
        act.activation(k.rkf[0][:, :], k.rt[:, :], ACT.Square).then_inc(k.sem("ret_stat_hi"), 1)
        wait_tile(k, act, tile(RVAR))
        read_tile(k, act.activation(k.rs[:, :, :], bank(k, tile(RVAR)).rearrange("p (c n) -> p c n", n=P), ACT.Sqrt,
                                    bias=EPS, scale=1.0 / P), tile(RVAR))
        act.wait_ge(k.sem("ret_out"), i + 1)
        act.dma_start(a.o_store[:, bass.ds(i + BT, 1), :].rearrange("p a n -> p (a n)"), k.rq[:, :]
                      ).then_inc(k.sem("ret_stored"), 16)
        act.wait_ge(k.sem("ret_stored"), 16 * i + 16)
        ch(act.activation(k.idle[:, 1:2], k.idle[:, 1:2], ACT.Copy))


def ret_vector(k, dve, ch):
    PER = 26

    def rope(i, ch, j, dst, done, ctx):
        t = at_stage("ret", "tile", i, j)
        wait_tile(k, dve, t)
        ps = bank(k, t)
        ch(dve.tensor_tensor(dst[:, 0:S], k.rtab[:, 0, :], ps, ALU.mult))
        ch(dve.tensor_tensor(k.rt[0:64, :], k.rtab[64:128, 1, :], ps[64:128, :], ALU.mult))
        if ctx:
            ch(dve.tensor_copy(dst[:, S:SC], bank(k, t, CTX, S)))
        read_tile(k, dve.tensor_tensor(k.rt[64:128, :], k.rtab[0:64, 1, :], ps[0:64, :], ALU.mult), t)
        dve.wait_ge(k.sem(f"tile_read{t.slot}"), t.half(1))
        dve.tensor_tensor(dst[:, 0:S], dst[:, 0:S], k.rt[:, :], ALU.add).then_inc(k.sem(done), 1)
        dve.wait_ge(k.sem(done), i + 1)

    dve.wait_ge(k.sem("ret_table"), 16)
    dve.wait_ge(k.sem("ret_gammas"), 1)
    with dve.Fori(0, RH) as i, ch.body(i, PER, RH):
        tile = lambda j: at_stage("ret", "tile", i, j)
        dve.wait_ge(k.sem("ret_decays"), 6 * i + 6)
        ch(dve.tensor_tensor(k.dec[:, 2, :], k.dec[:, 0, :], k.dec[:, 1, :], ALU.mult))
        dve.tensor_scalar(k.zeta[:, 2:4], k.zeta[:, 0:2], RET_SCALE, None, ALU.mult).then_inc(k.sem("ret_zetas"), 1)
        rope(i, ch, RK, k.rk, "ret_k_roped", True)
        dve.wait_ge(k.sem("ret_qk_hi"), 2 * i + 1)
        dve.scalar_tensor_tensor(k.rkf[1][:, :], k.rk[:, 0:S], RET_SCALE, f32(k.rkf[0][:, :]), ALU.mult, ALU.subtract
                                 ).then_inc(k.sem("ret_qk_split"), 1)
        rope(i, ch, RQ, k.rq, "ret_q_roped", False)
        dve.wait_ge(k.sem("ret_qk_hi"), 2 * i + 2)
        dve.tensor_tensor(k.rqf[1][:, :], k.rq[:, :], f32(k.rqf[0][:, :]), ALU.subtract).then_inc(k.sem("ret_qk_split"), 1)
        kt = bank(k, tile(RKT), SC).rearrange("p (c n) -> p c n", n=P)
        dve.wait_ge(k.sem("ret_zetas"), i + 1)
        for d in range(2):
            dve.wait_ge(k.sem("ret_kz_hi"), 2 * i + 2)
            ins = dve.scalar_tensor_tensor(k.kz[d][1][:, :, :], kt, k.zeta[:, 2 + d:3 + d], f32(k.kz[d][0][:, :, :]),
                                           ALU.mult, ALU.subtract)
            read_tile(k, ins, tile(RKT)) if d else ch(ins)
        dve.wait_ge(k.sem("ret_vt_hi"), i + 1)
        read_tile(k, dve.tensor_tensor(k.rvt[1][:, :, :], bank(k, tile(RVT), SC).rearrange("p (c n) -> p c n", n=P),
                                       f32(k.rvt[0][:, :, :]), ALU.subtract), tile(RVT))
        t = tile(RSC)
        wait_tile(k, dve, t)
        read_tile(k, dve.tensor_tensor(k.rt[:, :].rearrange("p (c n) -> p c n", n=P),
                                       bank(k, t).rearrange("p (c n) -> p c n", n=P),
                                       k.dec[:, 2:3, :].to_broadcast([P, NC, P]), ALU.mult), t)
        dve.wait_ge(k.sem("ret_scores_hi"), i + 1)
        dve.tensor_tensor(k.rqf[1][:, :], k.rt[:, :], f32(k.rqf[0][:, :]), ALU.subtract).then_inc(k.sem("ret_scores_split"), 1)
        dve.wait_ge(k.sem("ret_scores_split"), i + 1)
        t = tile(RVT)
        dve.wait_ge(k.sem(f"tile_read{t.slot}"), t.half(1))
        for d, (j, x) in enumerate(((RDF, k.rxf), (RDB, k.rkf))):
            buf = k.rt[:, :] if d else k.rv[:, 0:S]
            dve.tensor_tensor(buf.rearrange("p (c n) -> p c n", n=P), k.rq[:, :].rearrange("p (c n) -> p c n", n=P),
                              k.dec[:, 3 + d:4 + d, :].to_broadcast([P, NC, P]), ALU.mult
                              ).then_inc(k.sem("ret_decayed"), 1)
            dve.wait_ge(k.sem("ret_decayed_hi"), 2 * i + (d + 1))
            dve.tensor_tensor(x[1][:, :], buf, f32(x[0][:, :]), ALU.subtract).then_inc(k.sem("ret_decayed_split"), 1)
            t = tile(j)
            wait_tile(k, dve, t)
            g = k.lg[:, bass.ds(i + (2 * RH + RH * d), 1)]
            order = list(range(NC)) if d == 0 else list(range(NC - 1, -1, -1))
            near, far = (NC + 1, NC) if d == 0 else (NC, NC + 1)
            inc = lambda c: bank(k, t, P, P * c)
            ch(dve.tensor_scalar(k.rs[:, order[0], :], inc(far), g, None, ALU.mult))
            ch(dve.tensor_tensor(k.rs[:, order[0], :], k.rs[:, order[0], :], inc(near), ALU.add))
            for p, c in zip(order, order[1:]):
                ins = dve.scalar_tensor_tensor(k.rs[:, c, :], k.rs[:, p, :], g, inc(p), ALU.mult, ALU.add)
                if c == order[-1]:
                    read_tile(k, ins, t)
                else:
                    ch(ins)
            dve.wait_ge(k.sem(f"tile_read{t.slot}"), t.half(1))
            dve.wait_ge(k.sem("ret_states_hi"), 2 * i + (d + 1))
            dve.tensor_tensor(k.st[d][1][:, :, :], k.rs[:, :, :], f32(k.st[d][0][:, :, :]), ALU.subtract
                              ).then_inc(k.sem("ret_states_split"), 1)
            dve.wait_ge(k.sem("ret_states_split"), 2 * i + (d + 1))
        dve.wait_ge(k.sem("ret_stat_hi"), 2 * i + 1)
        dve.tensor_tensor(k.rxf[1][:, :], k.rq[:, :], f32(k.rxf[0][:, :]), ALU.subtract).then_inc(k.sem("ret_stat_split"), 1)
        t = tile(RM)
        wait_tile(k, dve, t)
        read_tile(k, dve.scalar_tensor_tensor(k.rt[:, :], bank(k, t), -1.0 / P, k.rq[:, :], ALU.mult, ALU.add), t)
        dve.wait_ge(k.sem(f"tile_read{t.slot}"), t.half(1))
        ch(dve.tensor_tensor(k.rv[:, 0:S], k.rt[:, :], k.rt[:, :], ALU.mult))
        dve.wait_ge(k.sem("ret_stat_hi"), 2 * i + 2)
        dve.tensor_tensor(k.rkf[1][:, :], k.rv[:, 0:S], f32(k.rkf[0][:, :]), ALU.subtract).then_inc(k.sem("ret_stat_split"), 1)
        t = tile(RVAR)
        dve.wait_ge(k.sem(f"tile_read{t.slot}"), t.half(1))
        flat = k.rs[:, :, :].rearrange("p c n -> p (c n)")
        ch(dve.reciprocal(flat, flat))
        ch(dve.scalar_tensor_tensor(k.rt[:, :], k.rt[:, :], k.params[:, bass.ds(i + PARAMS["gret"], 1)], flat,
                                    ALU.mult, ALU.mult))
        dve.tensor_tensor(k.rq[:, :], k.rt[:, :], k.rg[:, :], ALU.mult).then_inc(k.sem("ret_out"), 1)
        dve.wait_ge(k.sem("ret_stored"), 16 * i + 16)



def latent_norms_scalar(k, act, a, n, ap):
    for src, dst, name in ((a.cq_store, k.cqr[:, :, :], "cq"), (a.ckv_store, k.ckvr[:, :, :], "ckv"),
                           (a.kpe_store, k.kpr[64:96, :], "kpe"), (a.mla_table, k.mtab[:, :], "mtab")):
        act.dma_start(dst, src).then_inc(k.sem(f"{name}_back"), 16)
    norm_scalar(k, act, n, tiles_of(k.cqr), 2, [512, 512], 2 * P, ready=lambda e, c: e.wait_ge(k.sem("cq_back"), 16))
    apply_scalar(k, act, ap, k.cqn[0], 2, S)
    norm_scalar(k, act, n, tiles_of(k.ckvr), 2, [512, 512, CTX], 2 * P,
                ready=lambda e, c: e.wait_ge(k.sem("ckv_back"), 16))
    apply_scalar(k, act, ap, k.ckvn[0], 2, SC)
    act.wait_ge(k.sem("kpe_back"), 16)
    act.activation(k.mk[0][64:96, :], k.kpr[64:96, :], ACT.Copy).then_inc(k.sem("kpe_hi"), 1)


def latent_norms_vector(k, dve, n, ap):
    norm_vector(k, dve, n, tiles_of(k.cqr), 2, [512, 512], ready=lambda e, c: e.wait_ge(k.sem("cq_back"), 16))
    dve.wait_ge(k.sem("stat_rstd"), n.c)
    apply_vector(k, dve, ap, tiles_of(k.cqr), lambda i: col(k, "gq", i), k.cqn[0], k.cqn[1], 2, S)
    norm_vector(k, dve, n, tiles_of(k.ckvr), 2, [512, 512, CTX], ready=lambda e, c: e.wait_ge(k.sem("ckv_back"), 16))
    dve.wait_ge(k.sem("stat_rstd"), n.c)
    apply_vector(k, dve, ap, tiles_of(k.ckvr), lambda i: col(k, "gkv", i), k.ckvn[0], k.ckvn[1], 2, SC)
    dve.wait_ge(k.sem("kpe_hi"), 1)
    dve.tensor_tensor(k.mk[1][64:96, :], k.kpr[64:96, :], f32(k.mk[0][64:96, :]), ALU.subtract
                      ).then_inc(k.sem("kpe_split"), 1)


def latent_norms_tensor(k, pe, n):
    norm_tensor(k, pe, n, 2, [512, 512])
    norm_tensor(k, pe, n, 2, [512, 512, CTX])


QB = S // P
HEAD_ORDER = [("S", 0)]
for _q in range(1, QB + 1):
    HEAD_ORDER += ([("S", _q)] if _q < QB else []) + [("T", _q - 1)]
    if _q % 2 == 1 and _q > 1:
        HEAD_ORDER += [("O", _q // 2 - 1)]
HEAD_ORDER += [("O", QB // 2 - 1)]
_tile = {}
for _what in HEAD_ORDER:
    if _what[0] != "O":
        _tile[_what] = 2 + len(_tile)
HEAD_TILES = 2 + len(_tile)


def mla_tensor(k, pe, n_applied):
    ident = k.const[:, CONSTS["ident"]:CONSTS["ident"] + P]
    pe.wait_ge(k.sem("normed_split"), n_applied)
    pe.wait_ge(k.sem("kpe_split"), 1)
    with pe.Fori(0, PAIRS) as i:
        for a in range(2):
            tile = lambda j: at_stage("mla", "tile", i, HEAD_TILES * a + j)
            for j, (x, width) in enumerate(((k.cqn, S), (k.ckvn, SC))):
                u = at_stage("mla", "unit", i, a)
                gemm_tile(k, pe, tile(j), u, unit_block(k, u.slot, base=2 * P * j), act_of(*x), 2, width,
                          new_unit=j == 0)
            t = tile(1)
            pe.wait_ge(k.sem(f"tile_read{t.slot}"), t.half(1))
            t = tile(0)
            pe.wait_ge(k.sem(f"tile_read{t.slot}"), t.half(1))
            for what, q in HEAD_ORDER:
                if what == "S":
                    t = tile(_tile[what, q])
                    pe.wait_ge(k.sem(f"tile_read{t.slot}"), t.half(0))
                    b = tile_bank(t.slot)
                    for c in range(0, SC, 512):
                        w = min(512, SC - c)
                        mm = three(pe, k.ps[:, b + c:b + c + w],
                                   (k.mq[0][0:96, P * q:P * q + P], k.mq[1][0:96, P * q:P * q + P]),
                                   (k.mk[0][0:96, c:c + w], k.mk[1][0:96, c:c + w]), True, True)
                    mm.then_inc(k.sem("tile_done"), 1)
                    if q == 0:
                        for c in range(NC + NCC):
                            mm = pe.transpose(k.ps[:, 3072 + HD * c:3072 + HD * c + HD],
                                              k.mvr[64:128, P * c:P * c + P], ident[64:128, 64:128])
                        mm.then_inc(k.sem("mla_v_turned"), 1)
                elif what == "T":
                    t = tile(_tile[what, q])
                    pe.wait_ge(k.sem(f"tile_read{t.slot}"), t.half(0))
                    pe.wait_ge(k.sem("mla_probs"), 16 * i + (8 * a + q + 1))
                    b = tile_bank(t.slot)
                    for c in range(NC + NCC):
                        mm = pe.transpose(k.ps[:, b + P * c:b + P * c + P], k.probs[:, q % 2, P * c:P * c + P], ident)
                    mm.then_inc(k.sem("tile_done"), 1)
                else:
                    t = tile(_tile["T", 2 * q + 1])
                    pe.wait_ge(k.sem(f"tile_read{t.slot}"), t.half(1))
                    if q == 0:
                        pe.wait_ge(k.sem("mla_v_split"), 2 * i + (a + 1))
                    elif q >= 2:
                        pe.wait_ge(k.sem("mla_out_read"), 8 * i + (4 * a + q - 1))
                    b = 3072 + 512 * (q % 2)
                    for c in range(NC + NCC):
                        mm = three(pe, k.ps[:, b:b + 2 * P], (k.mv[0][:, c, :], k.mv[1][:, c, :]),
                                   (k.pt[0][:, q % 2, c, :], k.pt[1][:, q % 2, c, :]), c == 0, c == NC + NCC - 1)
                    mm.then_inc(k.sem("mla_out"), 1)
            pe.wait_ge(k.sem("mla_out_read"), 8 * i + 4 * a + 4)


def mla_scalar(k, act, a):
    act.wait_ge(k.sem("mla_v_cleared"), 2)
    with act.Fori(0, PAIRS) as i:
        for h in range(2):
            tile = lambda j: at_stage("mla", "tile", i, HEAD_TILES * h + j)
            wait_tile(k, act, tile(0))
            act.activation(k.mqf[0:64, :], bank(k, tile(0))[0:64, :], ACT.Copy).then_inc(k.sem("mla_q_nope"), 1)
            wait_tile(k, act, tile(1))
            act.activation(k.mk[0][0:64, :], bank(k, tile(1), SC)[0:64, :], ACT.Copy).then_inc(k.sem("mla_k_hi"), 1)
            act.activation(k.mvr[64:128, :], bank(k, tile(1), SC)[64:128, :], ACT.Copy).then_inc(k.sem("mla_v_raw"), 1)
            act.wait_ge(k.sem("mla_q_roped"), 2 * i + (h + 1))
            act.activation(k.mq[0][0:96, :], k.mqf[0:96, :], ACT.Copy).then_inc(k.sem("mla_q_hi"), 1)
            act.wait_ge(k.sem("mla_v_turned"), 2 * i + (h + 1))
            act.activation(k.mv[0][:, :, HD * h:HD * h + HD],
                           k.ps[:, 3072:3072 + 10 * HD].rearrange("p (c n) -> p c n", n=HD), ACT.Copy
                           ).then_inc(k.sem("mla_v_hi"), 1)
            for what, q in HEAD_ORDER:
                n = 8 * h + q
                if what == "S":
                    t = tile(_tile[what, q])
                    act.wait_ge(k.sem("mla_max"), 16 * i + (n + 1))
                    read_tile(k, act.activation(k.probs[:, q % 2, :], bank(k, t, SC), ACT.Exp, scale=MLA_SCALE,
                                                bias=k.stat[:, 1, n:n + 1], accum_out=k.stat[:, 2, n:n + 1]), t)
                elif what == "T":
                    t = tile(_tile[what, q])
                    wait_tile(k, act, t)
                    if q >= 4 and q % 2 == 0:
                        act.wait_ge(k.sem("mla_out"), 8 * i + (4 * h + (q // 2 - 1)))
                    act.activation(k.pt[0][:, (q // 2) % 2, :, P * (q % 2):P * (q % 2) + P],
                                   bank(k, t, SC).rearrange("p (c n) -> p c n", n=P), ACT.Copy
                                   ).then_inc(k.sem("mla_probs_hi"), 1)
        act.wait_ge(k.sem("mla_out_read"), 8 * i + 8)
        act.dma_start(a.o_store[:, bass.ds(i, 1), :].rearrange("p a n -> p (a n)"), k.mo[:, :]
                      ).then_inc(k.sem("mla_stored"), 16)


def mla_vector(k, dve, ch):
    dve.wait_ge(k.sem("mtab_back"), 16)
    for m in k.mv:
        dve.memset(f32(m[:, :, :]), 0.0).then_inc(k.sem("mla_v_cleared"), 1)
    with dve.Fori(0, PAIRS) as i, ch.body(i, 2 + 32, PAIRS):
        for h in range(2):
            tile = lambda j: at_stage("mla", "tile", i, HEAD_TILES * h + j)
            t = tile(0)
            wait_tile(k, dve, t)
            dve.wait_ge(k.sem("mla_q_nope"), 2 * i + (h + 1))
            dve.tensor_tensor(k.mqf[64:96, :], k.mtab[64:96, :], bank(k, t)[64:96, :], ALU.mult
                              ).then_inc(k.sem("mla_q_cos"), 1)
            read_q = dve.tensor_tensor(k.mqt[64:96, :], k.mtab[96:128, :], bank(k, t)[96:128, :], ALU.mult)
            ch(read_q)
            dve.wait_ge(k.sem("mla_q_cos"), 2 * i + (h + 1))
            dve.tensor_tensor(k.mqf[64:96, :], k.mqf[64:96, :], k.mqt[64:96, :], ALU.add).then_inc(k.sem("mla_q_roped"), 1)
            dve.wait_ge(k.sem("mla_q_roped"), 2 * i + (h + 1))
            t1 = tile(1)
            dve.wait_ge(k.sem("mla_v_raw"), 2 * i + (h + 1))
            read_tile(k, dve.tensor_tensor(k.mk[1][0:64, :], bank(k, t1, SC)[0:64, :], f32(k.mk[0][0:64, :]),
                                           ALU.subtract), t1)
            dve.wait_ge(k.sem("mla_q_hi"), 2 * i + (h + 1))
            read_tile(k, dve.tensor_tensor(k.mq[1][0:96, :], k.mqf[0:96, :], f32(k.mq[0][0:96, :]), ALU.subtract), t)
            dve.wait_ge(k.sem("mla_v_hi"), 2 * i + (h + 1))
            dve.tensor_tensor(k.mv[1][:, :, HD * h:HD * h + HD],
                              k.ps[:, 3072:3072 + 10 * HD].rearrange("p (c n) -> p c n", n=HD),
                              f32(k.mv[0][:, :, HD * h:HD * h + HD]), ALU.subtract).then_inc(k.sem("mla_v_split"), 1)

            def normalise(q):
                n = 8 * h + q
                t = tile(_tile["S", q])
                dve.wait_ge(k.sem(f"tile_read{t.slot}"), t.half(1))
                ch(dve.reciprocal(k.stat[:, 3, n:n + 1], k.stat[:, 2, n:n + 1]))
                dve.tensor_scalar(k.probs[:, q % 2, :], k.probs[:, q % 2, :], k.stat[:, 3, n:n + 1], None, ALU.mult
                                  ).then_inc(k.sem("mla_probs"), 1)
            for what, q in HEAD_ORDER:
                n = 8 * h + q
                if what == "S":
                    t = tile(_tile[what, q])
                    wait_tile(k, dve, t)
                    ch(dve.tensor_reduce(k.stat[:, 0, n:n + 1], bank(k, t, SC), AX.X, ALU.max))
                    dve.tensor_scalar(k.stat[:, 1, n:n + 1], k.stat[:, 0, n:n + 1], -MLA_SCALE, None, ALU.mult
                                      ).then_inc(k.sem("mla_max"), 1)
                elif what == "T":
                    t2 = tile(_tile[what, q])
                    dve.wait_ge(k.sem("mla_probs_hi"), 16 * i + (n + 1))
                    ins = dve.tensor_tensor(k.pt[1][:, (q // 2) % 2, :, P * (q % 2):P * (q % 2) + P],
                                            bank(k, t2, SC).rearrange("p (c n) -> p c n", n=P),
                                            f32(k.pt[0][:, (q // 2) % 2, :, P * (q % 2):P * (q % 2) + P]), ALU.subtract)
                    read_tile(k, ins, t2)
                    if q == QB - 2:
                        normalise(QB - 1)
                else:
                    dve.wait_ge(k.sem("mla_out"), 8 * i + (4 * h + q + 1))
                    b = 3072 + 512 * (q % 2)
                    r = slice(HD * h, HD * h + HD)
                    dve.tensor_copy(k.mo[r, 2 * P * q:2 * P * q + 2 * P], k.ps[r, b:b + 2 * P]
                                    ).then_inc(k.sem("mla_out_read"), 1)
                if what == "S" and q:
                    normalise(q - 1)
        dve.wait_ge(k.sem("mla_stored"), 16 * i + 16)



def out2_scalar(k, act, a):
    act.wait_ge(k.sem("mla_stored"), 16 * PAIRS)
    act.dma_start(k.outr[:, :, :], a.o_store).then_inc(k.sem("o_back"), 16)
    act.dma_start(k.x[:, :, :], a.x1_store).then_inc(k.sem("x1_back"), 16)
    act.wait_ge(k.sem("o_back"), 16)
    for i in range(DT):
        act.activation(k.hh[:, i, :], k.outr[:, i, :], ACT.Copy).then_inc(k.sem("o_hi"), 1)


def out2_vector(k, dve):
    for i in range(DT):
        dve.wait_ge(k.sem("o_hi"), i + 1)
        dve.tensor_tensor(k.hl[:, i, :], k.outr[:, i, :], f32(k.hh[:, i, :]), ALU.subtract).then_inc(k.sem("o_split"), 1)
    dve.wait_ge(k.sem("x1_back"), 16)
    for j in range(DT):
        t = at_stage("out2", "tile", 0, j)
        wait_tile(k, dve, t)
        read_tile(k, dve.scalar_tensor_tensor(k.x[:, j, :], bank(k, t), k.mod[:, 2 * DT + j, 0:1], k.x[:, j, :],
                                              ALU.mult, ALU.add), t)


def out2_tensor(k, pe):
    pe.wait_ge(k.sem("o_split"), DT)
    for j in range(DT):
        full_gemm(k, pe, at_stage("out2", "tile", 0, j), at_stage("out2", "unit", 0, j))


def wait_out2(k, e):
    for j in (DT - 2, DT - 1):
        t = at_stage("out2", "tile", 0, j)
        e.wait_ge(k.sem(f"tile_read{t.slot}"), t.half(1))



def up_tensor(k, pe, stage, i):
    for j in range(4):
        full_gemm(k, pe, at_stage(stage, "tile", i, j), at_stage(stage, "unit", i, j))


def down_tensor(k, pe, stage, i, tile0, unit0):
    for j in range(DT):
        u = at_stage(stage, "unit", i, unit0 + j // 4)
        gemm_tile(k, pe, at_stage(stage, "tile", i, tile0 + j), u, unit_block(k, u.slot, 4 * P, P * (j % 4)),
                  act_of(k.fh, k.fl), 2, new_unit=j % 4 == 0)


def up_scalar(k, act, stage, i, step):
    if stage == "ffn":
        act.wait_ge(k.sem("ff_split"), 2 * step)
    for m in range(2):
        for j, dst in ((0, k.fa), (1, k.fg)):
            t = at_stage(stage, "tile", i, 2 * m + j)
            p = PARAMS["conv2"] + 4 * (2 * m + j)
            tap = lambda n: k.params[:, bass.ds(16 * step + (p + n), 1)]
            wait_tile(k, act, t)
            act.activation(dst[:, m, :], bank(k, t), ACT.Identity, scale=tap(1), bias=tap(3)).then_inc(k.sem("ff_middle"), 1)
        act.wait_ge(k.sem(f"tile_read{t.slot}"), t.half(1))
        act.activation(k.fs[:, :], k.fg[:, m, :], ACT.Silu).then_inc(k.sem("ff_silu"), 1)
        act.wait_ge(k.sem("ff_product"), 2 * step + (m + 1))


def up_vector(k, dve, stage, i, step):
    for m in range(2):
        for j, dst in ((0, k.fa), (1, k.fg)):
            t = at_stage(stage, "tile", i, 2 * m + j)
            p = PARAMS["conv2"] + 4 * (2 * m + j)
            tap = lambda n: k.params[:, bass.ds(16 * step + (p + n), 1)]
            dve.wait_ge(k.sem("ff_middle"), 4 * step + (2 * m + j + 1))
            ps = bank(k, t)
            dve.scalar_tensor_tensor(dst[:, m, 1:], ps[:, :S - 1], tap(0), dst[:, m, 1:], ALU.mult, ALU.add
                                     ).then_inc(k.sem("ff_back"), 1)
            dve.wait_ge(k.sem("ff_back"), 4 * step + (2 * m + j + 1))
            read_tile(k, dve.scalar_tensor_tensor(dst[:, m, :S - 1], ps[:, 1:], tap(2), dst[:, m, :S - 1],
                                                  ALU.mult, ALU.add), t)
            dve.wait_ge(k.sem(f"tile_read{t.slot}"), t.half(1))
        dve.wait_ge(k.sem("ff_silu"), 2 * step + (m + 1))
        dve.tensor_tensor(k.fa[:, m, :], k.fa[:, m, :], k.fs[:, :], ALU.mult).then_inc(k.sem("ff_product"), 1)


def split_scalar(k, act, step, last_tile):
    wait_tile(k, act, last_tile)
    for m in range(2):
        act.wait_ge(k.sem("ff_product"), 2 * step + (m + 1))
        act.activation(k.fh[:, m, :], k.fa[:, m, :], ACT.Copy).then_inc(k.sem("ff_hi"), 1)


def split_vector(k, dve, step):
    for m in range(2):
        dve.wait_ge(k.sem("ff_hi"), 2 * step + (m + 1))
        dve.tensor_tensor(k.fl[:, m, :], k.fa[:, m, :], f32(k.fh[:, m, :]), ALU.subtract).then_inc(k.sem("ff_split"), 1)
    dve.wait_ge(k.sem("ff_split"), 2 * step + 2)


def down_vector(k, dve, stage, i, tile0):
    for j in range(DT):
        t = at_stage(stage, "tile", i, tile0 + j)
        wait_tile(k, dve, t)
        read_tile(k, dve.scalar_tensor_tensor(k.x[:, j, :], bank(k, t), k.mod[:, 5 * DT + j, 0:1], k.x[:, j, :],
                                              ALU.mult, ALU.add), t)


LAST = FT // 2 - 1


def ffn_tensor(k, pe, n_applied):
    pe.wait_ge(k.sem("normed_split"), n_applied)
    up_tensor(k, pe, "up0", 0)
    with pe.Fori(0, LAST) as i:
        up_tensor(k, pe, "ffn", i)
        pe.wait_ge(k.sem("ff_split"), 2 * i + 2)
        down_tensor(k, pe, "ffn", i, 4, 4)
    pe.wait_ge(k.sem("ff_split"), 2 * LAST + 2)
    down_tensor(k, pe, "down", 0, 0, 0)


def ffn_scalar(k, act):
    up_scalar(k, act, "up0", 0, 0)
    split_scalar(k, act, 0, at_stage("up0", "tile", 0, 3))
    with act.Fori(0, LAST) as i:
        up_scalar(k, act, "ffn", i, i + 1)
        split_scalar(k, act, i + 1, at_stage("ffn", "tile", i, 11))


def ffn_vector(k, dve):
    up_vector(k, dve, "up0", 0, 0)
    split_vector(k, dve, 0)
    with dve.Fori(0, LAST) as i:
        up_vector(k, dve, "ffn", i, i + 1)
        down_vector(k, dve, "ffn", i, 4)
        split_vector(k, dve, i + 1)
    down_vector(k, dve, "down", 0, 0)



def end_scalar(k, act, n, last_tiles):
    last_tiles(act)
    norm_scalar(k, act, n, tiles_of(k.x), DT, [512, 512], D)


def end_vector(k, dve, n, last_tiles):
    last_tiles(dve)
    norm_vector(k, dve, n, tiles_of(k.x), DT, [512, 512])
    dve.wait_ge(k.sem("stat_rstd"), n.c)
    for c in range(NCH):
        s = slice(512 * c, 512 * c + 512)
        for i in range(DT):
            dve.scalar_tensor_tensor(k.outr[:, i, s], k.x[:, i, s], col(k, "gfin", i), k.rstd[:, s], ALU.mult, ALU.mult
                                     ).then_inc(k.sem("finished"), 1)


def end_sync(k, sp, a):
    for c in range(NCH):
        s = slice(512 * c, 512 * c + 512)
        sp.wait_ge(k.sem("finished"), DT * (c + 1))
        sp.dma_start(a.out[:, :, s], k.outr[:, :, s]).then_inc(k.sem("out_stored"), 16)
    sp.wait_ge(k.sem("out_stored"), 16 * NCH)



class Arrays:
    pass


def two_blocks_program(nc, stream, w_ada, x, context, params, consts, ret_table, mla_table, out):
    a = Arrays()
    a.w_ada, a.x, a.ctx, a.ret_table, a.mla_table, a.out, a.params, a.consts = w_ada, x, context, ret_table, mla_table, out, params, consts
    a.x1_store = nc.dram_tensor("x1_store", (P, DT, S), F32).ap()
    a.cq_store = nc.dram_tensor("cq_store", (P, 2, S), F32).ap()
    a.ckv_store = nc.dram_tensor("ckv_store", (P, 2, SC), F32).ap()
    a.kpe_store = nc.dram_tensor("kpe_store", (32, SC), F32).ap()
    a.o_store = nc.dram_tensor("o_store", (P, DT, S), F32).ap()
    with ExitStack() as ctx:
        k = lay_out(nc, ctx)
        block = ctx.enter_context(nc.Block())

        @block.sync
        def _(sp):
            load_weights(k, sp, stream, NUNITS)
            end_sync(k, sp, a)

        @block.gpsimd
        def _(pool):
            split_weights(k, pool, NUNITS)

        @block.scalar
        def _(act):
            ch = Chain(act, k.sem("scalar_steps"))
            n, ap = Norms(), Applies()
            loads_scalar(k, act, a)
            start_scalar(k, act)
            norm_scalar(k, act, n, tiles_of(k.x), DT, [512, 512], D, ready=k.x_ready)
            apply_scalar(k, act, ap, k.hh, DT, S)
            sb_scalar(k, act)
            merge_scalar(k, act, a, "merge_sb", 0)
            pool_scalar(k, act, a)
            merge_scalar(k, act, a, "merge_pool", 1)
            conv_scalar(k, act, a)
            merge_scalar(k, act, a, "merge_conv", 2)
            out1_scalar(k, act)
            enter_scalar(k, act, a, n, ap)
            latents_scalar(k, act, a)
            ret_scalar(k, act, a, ch)
            latent_norms_scalar(k, act, a, n, ap)
            mla_scalar(k, act, a)
            out2_scalar(k, act, a)
            wait_out2(k, act)
            norm_scalar(k, act, n, tiles_of(k.x), DT, [512, 512], D)
            apply_scalar(k, act, ap, k.hh, DT, S, bias=lambda i: k.mod[:, 3 * DT + i, 0:1])
            ffn_scalar(k, act)
            end_scalar(k, act, n, lambda e: wait_down(k, e))

        @block.vector
        def _(dve):
            ch = Chain(dve, k.sem("vector_steps"))
            n, ap = Norms(), Applies()
            start_vector(k, dve)
            norm_vector(k, dve, n, tiles_of(k.x), DT, [512, 512], ready=k.x_ready)
            apply_vector(k, dve, ap, tiles_of(k.x), lambda i: col(k, "pre_g", i), k.hh, k.hl, DT, S)
            sb_vector(k, dve)
            merge_vector(k, dve, "merge_sb", 0)
            pool_vector(k, dve, ch)
            merge_vector(k, dve, "merge_pool", 1)
            conv_vector(k, dve, ch)
            merge_vector(k, dve, "merge_conv", 2)
            out1_vector(k, dve)
            enter_vector(k, dve, n, ap, ch)
            latents_vector(k, dve, ch)
            ret_vector(k, dve, ch)
            latent_norms_vector(k, dve, n, ap)
            mla_vector(k, dve, ch)
            out2_vector(k, dve)
            wait_out2(k, dve)
            norm_vector(k, dve, n, tiles_of(k.x), DT, [512, 512])
            dve.wait_ge(k.sem("stat_rstd"), n.c)
            apply_vector(k, dve, ap, tiles_of(k.x), lambda i: k.gm[:, 2 * DT + i:2 * DT + i + 1], k.hh, k.hl, DT, S,
                         bias=lambda i: k.mod[:, 3 * DT + i, 0:1])
            ffn_vector(k, dve)
            end_vector(k, dve, n, lambda e: wait_down(k, e))

        @block.tensor
        def _(pe):
            n = Norms()
            applied = 2 * DT
            pe.wait_ge(k.sem("ones_ready"), 1)
            norm_tensor(k, pe, n, DT, [512, 512])
            pe.wait_ge(k.sem("start_ready"), 1)
            pe.wait_ge(k.sem("silu_c"), 1)
            pe.wait_ge(k.sem("normed_split"), applied)
            sb_tensor(k, pe)
            merge_tensor(k, pe, "merge_sb", 0)
            pool_tensor(k, pe)
            merge_tensor(k, pe, "merge_pool", 1)
            conv_tensor(k, pe)
            merge_tensor(k, pe, "merge_conv", 2)
            out1_tensor(k, pe)
            enter_tensor(k, pe, n)
            applied += 3 * DT
            latents_tensor(k, pe, applied)
            ret_tensor(k, pe)
            latent_norms_tensor(k, pe, n)
            applied += 2 * 5
            mla_tensor(k, pe, applied)
            out2_tensor(k, pe)
            norm_tensor(k, pe, n, DT, [512, 512])
            applied += 2 * DT
            ffn_tensor(k, pe, applied)
            norm_tensor(k, pe, n, DT, [512, 512])


def wait_down(k, e):
    for j in (DT - 2, DT - 1):
        t = at_stage("down", "tile", 0, j)
        e.wait_ge(k.sem(f"tile_read{t.slot}"), t.half(1))



def fm(v):
    return np.asarray(v).reshape(-1, P).T


def blocks(w, cols=P):
    kk, n = w.shape
    return w.reshape(kk // P, P, n // cols, cols).transpose(2, 1, 0, 3).reshape(n // cols, P, kk // P * cols)


def padded(u):
    return np.concatenate([u, np.zeros(u.shape[:2] + (UNIT - u.shape[2],), u.dtype)], 2)


def weight_stream(i):
    w_in, w2 = i["w_in"][0], i["w_in_2"][0]
    sec = [blocks(w_in[:, W * n:W * n + W]) for n in range(10)]
    gates = blocks(w_in[:, 10 * W:])
    out = []
    for p in range(PAIRS):
        out += [sec[6][p], sec[7][p], sec[8][p], sec[9][p]]

    def merge(b):
        g, br = gates[DT * b:DT * b + DT], blocks(i["w_branch"][0][b], 2 * P)
        for t in range(0, DT, 2):
            out.extend([g[t], g[t + 1], br[t // 2]])
    merge(2)
    for g in range(BT):
        out += [sec[0][g], sec[1][g], padded(i["pool_w"][0][g][None])[0]]
    merge(0)
    for t in range(BT):
        out += [sec[4][t], sec[2][t], sec[3][t], sec[5][t]]
    merge(1)
    out += list(blocks(i["w_out"][0]))
    lat = blocks(w2[:, :512])
    kpe = w2[:, 512:544]
    swap = np.concatenate([kpe[:, 8:16], kpe[:, :8], kpe[:, 24:32], kpe[:, 16:24]], 1)
    out += list(lat) + list(blocks(np.concatenate([np.zeros((D, 64), kpe.dtype), kpe, swap], 1)))
    r = [blocks(w2[:, 544 + W * n:544 + W * n + W]) for n in range(4)]
    for h in range(RH):
        out += [r[1][h], r[2][h], r[0][h], r[3][h]]
    uq, ukv = i["w_uq_2"][0], i["w_ukv_2"][0]
    for p in range(PAIRS):
        for h in (2 * p, 2 * p + 1):
            m = uq[:, 96 * h:96 * h + 96]
            pe = m[:, 64:]
            sw = np.concatenate([pe[:, 8:16], pe[:, :8], pe[:, 24:32], pe[:, 16:24]], 1)
            q, kv = blocks(np.concatenate([m, sw], 1))[0], blocks(ukv[:, P * h:P * h + P])[0]
            out += [padded(np.concatenate([q, kv], 1)[None])[0]]
    out += list(blocks(i["w_out_2"][0]))
    up, down = blocks(i["w_up_2"][0]), i["w_down_2"][0]

    def add_up(g):
        out.extend([up[2 * g], up[FT + 2 * g], up[2 * g + 1], up[FT + 2 * g + 1]])

    def add_down(g):
        rows = down[2 * P * g:2 * P * g + 2 * P]
        out.extend(rows.reshape(2, P, 2, W).transpose(2, 1, 0, 3).reshape(2, P, UNIT))
    add_up(0)
    for g in range(1, FT // 2):
        add_up(g)
        add_down(g - 1)
    add_down(FT // 2 - 1)
    assert len(out) == NUNITS
    return np.stack(out)


def vectors(i):
    cw2 = np.concatenate([i["conv_w_2"][0], i["conv_b_2"][0][None]])
    cw2 = cw2.reshape(4, 2, FT // 1, P).transpose(3, 2, 1, 0).reshape(P, -1)
    cw = np.concatenate([i["conv_w"][0], i["conv_b"][0][None]]).reshape(4, BT, P).transpose(2, 1, 0).reshape(P, -1)
    c = np.stack([fm(i["c_2"][0]), fm(i["c_ctx_2"])], 2).reshape(P, -1)
    parts = [fm(i["pre_norm_g"][0]), fm(i["pool_scale"][0]), cw, fm(i["post_norm_g"][0]), c, fm(i["b_ada_2"][0]),
             fm(i["g_norm1_2"][0]), fm(i["g_q_2"][0]), fm(i["g_kv_2"][0]), fm(i["g_ret_2"][0]),
             fm(i["g_norm2_2"][0]), cw2, fm(i["g_final_2"]), np.tile(i["ret_decay_2"][0].reshape(1, -1), (P, 1))]
    v = np.ascontiguousarray(np.concatenate(parts, 1))
    assert v.shape == (P, NPARAM)
    return v


def tokens_last(x):
    return np.ascontiguousarray(x.T.reshape(-1, P, x.shape[0]).transpose(1, 0, 2))



def kernel(**inputs):
    import concourse.bacc as _bacc
    from concourse.bass_utils import run_bass_kernel_spmd as _run

    i = {name: np.asarray(v) for name, v in inputs.items()}
    ret_table, mla_table = rope_tables()
    arrays = {"in_stream": weight_stream(i), "in_w_ada": np.ascontiguousarray(blocks(i["w_ada_2"][0])),
              "in_x": tokens_last(i["x"][0]), "in_context": tokens_last(i["ctx_2"][0]),
              "in_params": vectors(i), "in_consts": constants(),
              "in_ret_table": np.ascontiguousarray(ret_table.reshape(P, 2, S)), "in_mla_table": mla_table}
    nc = _bacc.Bacc("TRN2", target_bir_lowering=False, num_devices=1)
    args = [nc.dram_tensor(n, v.shape, mybir.dt.from_np(v.dtype), kind="ExternalInput").ap() for n, v in arrays.items()]
    out = nc.dram_tensor("out_0_dram", (P, DT, S), F32, kind="ExternalOutput").ap()
    two_blocks_program(nc, *args, out)
    r = _run(nc, [arrays], core_ids=[0])
    got = np.asarray(r.results[0]["out_0_dram"])
    return np.ascontiguousarray(got.transpose(2, 1, 0).reshape(1, S, D))
```

```python
from contextlib import ExitStack, contextmanager

import numpy as np
import concourse.bass as bass
from concourse import mybir

F32 = mybir.dt.float32
F32R = mybir.dt.float32r
ACT = mybir.ActivationFunctionType
ALU = mybir.AluOpType
AX = mybir.AxisListType

P = 128
S = 1024
CTX = 256
SC = S + CTX
D = 1024
DT = D // P
W = 512
BT = W // P
NCH = S // 512
UNIT = 1024
EPS = 1e-6
POOL_WINDOWS = (2, 4, 8, 16)
HD = 64
PAIRS = BT
MLA_SCALE = 96.0 ** -0.5
RET_SCALE = 128.0 ** -0.5
RH = 4
NC = S // P
NCC = CTX // P
FF = 2816
FT = FF // P
CLAMP = 30.0
BIG = 1e30

PARAMS, _n = {}, 0
for _name, _w in (("pre_g", DT), ("pool_scale", BT), ("conv", 4 * BT), ("post_g", DT), ("c", 2 * DT),
                  ("b_ada", 6 * DT), ("g1", DT), ("gq", 2), ("gkv", 2), ("gret", RH), ("g2", DT),
                  ("conv2", 4 * 2 * FT), ("gfin", DT), ("decay", 2 * RH)):
    PARAMS[_name] = _n
    _n += _w
NPARAM = _n

CONSTS, _n = {}, 0
for _name, _w in (("tri", P), ("rest", P), ("ident", P), ("mask", P), ("mneg", P), ("cnt", 16 * BT),
                  ("fwd", P), ("bwd", P), ("xf", P), ("xb", P), ("zf", 1), ("zb", 1)):
    CONSTS[_name] = _n
    _n += _w
NCONST = _n


def constants():
    c = np.zeros((P, NCONST), np.float32)
    r = np.arange(P)
    k, q = r[:, None], r[None, :]

    def put(name, a):
        a = np.broadcast_to(a, (P, a.shape[-1]))
        c[:, CONSTS[name]:CONSTS[name] + a.shape[1]] = a

    put("tri", (k >= q).astype(np.float32))
    put("rest", (k < q).astype(np.float32))
    put("ident", (k == q).astype(np.float32))
    put("mask", (k < q).astype(np.float32))
    put("mneg", np.where(k < q, BIG, -BIG).astype(np.float32))
    for g, w in enumerate(POOL_WINDOWS):
        c[:, CONSTS["cnt"] + 16 * g:CONSTS["cnt"] + 16 * g + 16] = w / np.minimum(np.arange(16) + 1, w)
    put("fwd", np.maximum(q - k, 0).astype(np.float32))
    put("bwd", np.maximum(k - q, 0).astype(np.float32))
    put("xf", (q + 1).astype(np.float32))
    put("xb", (P - q).astype(np.float32))
    put("zf", (P - 1 - k).astype(np.float32))
    put("zb", k.astype(np.float32))
    return c


def rope_tables():
    def inv(dim):
        return (np.float32(10000.0) ** (-np.arange(0, dim, 2, dtype=np.float32) / np.float32(dim))).astype(np.float32)
    pos = np.arange(S, dtype=np.float32)
    a = inv(P)[:, None] * pos[None, :]
    a = np.concatenate([a, a])
    sign = np.where(np.arange(P) < P // 2, 1.0, -1.0)[:, None]
    ret = np.stack([np.cos(a), np.sin(a) * sign], 1)
    row, col = np.floor(pos / 64), pos % 64
    half = []
    for p in (row, col):
        b = inv(16)[:, None] * p[None, :].astype(np.float32)
        half.append(np.concatenate([b, b]))
    b = np.concatenate(half)
    sgn = np.tile(np.repeat([-1.0, 1.0], 8), 2)[:, None]
    mla = np.zeros((P, S))
    mla[64:96] = np.cos(b)
    mla[96:128] = np.sin(b) * sgn
    return ret.reshape(P, 2 * S).astype(np.float32), mla.astype(np.float32)


class At:

    def __init__(self, base, per=0, i=None):
        self.base, self.per, self.i = base, per, i

    def plus(self, n):
        return At(self.base + n, self.per, self.i)

    @property
    def slot(self):
        assert self.per % 2 == 0
        return self.base % 2

    def value(self, extra=0):
        return self.base + extra if self.i is None else self.per * self.i + (self.base + extra)

    def half(self, extra=0):
        return self.base // 2 + extra if self.i is None else (self.per // 2) * self.i + (self.base // 2 + extra)


class Chain:

    def __init__(self, eng, sem):
        self.eng, self.sem, self.n, self.i, self.per, self.start = eng, sem, 0, None, 0, 0

    def value(self):
        return self.n if self.i is None else self.per * self.i + self.n

    def __call__(self, ins):
        self.n += 1
        ins.then_inc(self.sem, 1)
        self.eng.wait_ge(self.sem, self.value())

    @contextmanager
    def body(self, i, per, times):
        self.i, self.per, self.start = i, per, self.n
        yield
        assert self.n - self.start == per, f"{self.n - self.start} steps in a body of {per}"
        self.i, self.n = None, self.start + per * times


class Core:
    pass



STAGES = (
    ("sb", PAIRS, 4, 4),
    ("merge_sb", 2, 6, 8),
    ("pool", 2, 6, 6),
    ("merge_pool", 2, 6, 8),
    ("conv", BT, 4, 4),
    ("merge_conv", 2, 6, 8),
    ("out1", 1, DT, DT),
    ("latents", 1, 5, 5),
    ("ret", RH, 4, 12),
    ("mla", PAIRS, 2, 36),
    ("out2", 1, DT, DT),
    ("up0", 1, 4, 4),
    ("ffn", FT // 2 - 1, 6, 12),
    ("down", 1, 2, 8),
)
FIRST_UNIT, FIRST_TILE, _u, _t = {}, {}, 0, 2
for _name, _steps, _units, _tiles in STAGES:
    FIRST_UNIT[_name], FIRST_TILE[_name] = _u, _t
    _u, _t = _u + _steps * _units, _t + _steps * _tiles
NUNITS = _u

ADA = 4
ADA_STEP, _u = {}, 0
for _name, _steps, _, _ in STAGES:
    if _name in ("merge_sb", "pool", "merge_pool", "conv", "merge_conv"):
        ADA_STEP[_name] = _u
        _u += _steps
assert ADA * _u == 6 * DT

BLOCKS = [(qc, kb, a, max(0, kb - 4 * qc) * P)
          for qc in range(NCH) for kb in range(4 * qc + 3, -1, -1) for a in range(2)]
NB = len(BLOCKS)


NLOGIT, NEX = 7, 3
NORMED = 3


def place(nc, name, kb, shape, dt):
    if kb == 0:
        with nc.sbuf_tensor(name, shape, dt) as t:
            return t
    with nc.sbuf_tensor(f"{name}_before", [P, int(kb * 256)], F32):
        with nc.sbuf_tensor(name, shape, dt) as t:
            pass
    return t


def lay_out(nc, ctx):
    k = Core()
    k.wh = place(nc, "weights_hi", 0, [P, 2, UNIT], F32R)
    k.wl = place(nc, "weights_lo", 8, [P, 2, UNIT], F32R)
    k.raw = place(nc, "weights_raw", 16, [P, 2, UNIT], F32)
    k.const = place(nc, "constants", 24, [P, NCONST], F32)
    k.params = place(nc, "params", 29, [P, NPARAM], F32)
    k.tri = place(nc, "tri", 30.5, [P, 2 * P], F32R)
    k.ones = place(nc, "ones", 31.5, [P, P], F32R)
    k.adaw = place(nc, "modulation_weights", 202, [P, UNIT], F32)
    k.one32 = place(nc, "ones_f32", 32, [P, P], F32)
    k.mod = place(nc, "modulation", 32.5, [P, 6 * DT, 2], F32)
    k.scf = place(nc, "silu_c", 33.25, [P, 2 * DT], F32)
    k.gm = place(nc, "gains", 33.5, [P, 4 * DT], F32)
    k.idle = place(nc, "idle", 33.75, [P, 4], F32)
    B = 34
    k.hh = place(nc, "h_hi", B, [P, DT, S], F32R)
    k.hl = place(nc, "h_lo", B + 32, [P, DT, S], F32R)
    k.yh = place(nc, "branch_hi", B + 64, [P, BT, S], F32R)
    k.yl = place(nc, "branch_lo", B + 80, [P, BT, S], F32R)
    k.outr = place(nc, "mixed", B + 64, [P, DT, S], F32)
    k.merged = place(nc, "merged", B + 96, [P, DT, S], F32)
    T = B + 96
    k.x = place(nc, "x", T, [P, DT, S], F32)
    N0 = T + 32
    k.sq = place(nc, "squares", N0, [P, 2, SC], F32)
    k.acc = place(nc, "square_sums", N0 + 10, [P, SC], F32)
    k.sth = place(nc, "square_sums_hi", N0 + 15, [P, 2, 512], F32R)
    k.stl = place(nc, "square_sums_lo", N0 + 19, [P, 2, 512], F32R)
    k.rstd = place(nc, "rstd", N0 + 23, [P, SC], F32)
    k.nt = place(nc, "normed", N0 + 28, [P, NORMED, 512], F32)
    k.root = place(nc, "root", N0 + 34, [P, 512], F32)
    k.qh = place(nc, "q_hi", T, [P, S], F32R)
    k.ql = place(nc, "q_lo", T + 4, [P, S], F32R)
    k.kh = place(nc, "k_hi", T + 8, [P, S], F32R)
    k.kl = place(nc, "k_lo", T + 12, [P, S], F32R)
    k.vh = place(nc, "v_hi", T + 16, [P, NC, P], F32R)
    k.vl = place(nc, "v_lo", T + 20, [P, NC, P], F32R)
    k.sph = place(nc, "softplus_hi", T + 24, [P, 4, 512], F32R)
    k.spl = place(nc, "softplus_lo", T + 32, [P, 4, 512], F32R)
    k.ph = place(nc, "weights_of_keys_hi", T + 40, [P, 2, 512], F32R)
    k.pl = place(nc, "weights_of_keys_lo", T + 44, [P, 2, 512], F32R)
    k.logit = place(nc, "logits_then_weights", T + 48, [P, NLOGIT, 512], F32)
    k.ex = place(nc, "exps_then_softplus", T + 62, [P, NEX, 512], F32)
    k.vy = place(nc, "v_then_y", T + 68, [P, S], F32)
    k.sg = place(nc, "silu_gate", T + 72, [P, S], F32)
    T2 = T + 32
    k.pv = place(nc, "pool_v", T2, [P, S], F32)
    k.pa = place(nc, "window_a", T2 + 4, [P, S], F32)
    k.pb = place(nc, "window_b", T2 + 8, [P, S], F32)
    k.poh = place(nc, "pooled_hi", T2 + 12, [P, S], F32R)
    k.pol = place(nc, "pooled_lo", T2 + 16, [P, S], F32R)
    k.psg = place(nc, "pool_gate", T2 + 20, [P, S], F32)
    k.py = place(nc, "pool_y", T2 + 24, [P, S], F32)
    k.sig = place(nc, "merge_gate", T2 + 28, [P, 2, S], F32)
    k.prod = place(nc, "gated", T2 + 36, [P, S], F32)
    k.cg = place(nc, "conv_gate_c", T2, [P, S], F32)
    k.cz = place(nc, "conv_z", T2 + 4, [P, S], F32)
    k.cy = place(nc, "conv_y", T2 + 8, [P, S], F32)
    k.csg = place(nc, "conv_gate", T2 + 12, [P, S], F32)

    k.h2h = place(nc, "h2_hi", B, [P, DT, SC], F32R)
    k.h2l = place(nc, "h2_lo", B + 40, [P, DT, SC], F32R)
    k.ctx = place(nc, "context", 198, [P, DT, CTX], F32)
    k.cq = place(nc, "latent_q", 114, [P, 2, S], F32)
    k.ckv = place(nc, "latent_kv", 122, [P, 2, SC], F32)
    k.kpe = place(nc, "key_rotated", 148, [P, SC], F32)
    k.kpt = place(nc, "key_rotated_part", 153, [P, S], F32)
    k.lat_table = place(nc, "mla_table_early", 157, [P, S], F32)
    k.rk = place(nc, "ret_k", 114, [P, SC], F32)
    k.rv = place(nc, "ret_v", 119, [P, SC], F32)
    k.rq = place(nc, "ret_q", 124, [P, S], F32)
    k.rt = place(nc, "ret_t", 128, [P, S], F32)
    k.rs = place(nc, "ret_states", 132, [P, NC, P], F32)
    k.rg = place(nc, "ret_gate", 136, [P, S], F32)
    k.rtab = place(nc, "ret_table", 140, [P, 2, S], F32)
    k.kz = [[place(nc, f"ret_k_tokens_{d}_{p}", 148 + 10 * n + 5 * m, [P, NC + NCC, P], F32R)
             for m, p in enumerate(("hi", "lo"))] for n, d in enumerate(("fwd", "bwd"))]
    k.st = [[place(nc, f"ret_states_{d}_{p}", 148 + 10 * n + 5 * m, [P, NC, P], F32R)
             for m, p in enumerate(("hi", "lo"))] for n, d in enumerate(("fwd", "bwd"))]
    k.rvt = [place(nc, f"ret_v_tokens_{p}", 168 + 5 * m, [P, NC + NCC, P], F32R) for m, p in enumerate(("hi", "lo"))]
    k.rkf = [place(nc, f"ret_k_features_{p}", 178 + 4 * m, [P, S], F32R) for m, p in enumerate(("hi", "lo"))]
    k.rqf = [place(nc, f"ret_q_then_scores_{p}", 186 + 4 * m, [P, S], F32R) for m, p in enumerate(("hi", "lo"))]
    k.rxf = [place(nc, f"ret_q_decayed_{p}", 194 + 4 * m, [P, S], F32R) for m, p in enumerate(("hi", "lo"))]
    k.dec = place(nc, "ret_decays", 202, [P, 5, P], F32)
    k.zeta = place(nc, "ret_zeta", 204.5, [P, 4], F32)
    k.lg = place(nc, "log_gamma", 204.6875, [P, 4 * RH], F32)
    k.cqn = [place(nc, f"latent_q_{p}", 34 + 8 * m, [P, 2, S], F32R) for m, p in enumerate(("hi", "lo"))]
    k.ckvn = [place(nc, f"latent_kv_{p}", 50 + 10 * m, [P, 2, SC], F32R) for m, p in enumerate(("hi", "lo"))]
    k.cqr = place(nc, "latent_q_back", 70, [P, 2, S], F32)
    k.ckvr = place(nc, "latent_kv_back", 78, [P, 2, SC], F32)
    k.mk = [place(nc, f"mla_k_{p}", 88 + 5 * m, [P, SC], F32R) for m, p in enumerate(("hi", "lo"))]
    k.mq = [place(nc, f"mla_q_{p}", 98 + 4 * m, [P, S], F32R) for m, p in enumerate(("hi", "lo"))]
    k.mv = [place(nc, f"mla_v_{p}", 106 + 5 * m, [P, NC + NCC, P], F32R) for m, p in enumerate(("hi", "lo"))]
    k.mvr = place(nc, "mla_v_raw", 116, [P, SC], F32)
    k.mqf = place(nc, "mla_q_f32", 121, [P, S], F32)
    k.mqt = place(nc, "mla_q_part", 125, [P, S], F32)
    k.mtab = place(nc, "mla_table", 129, [P, S], F32)
    k.kpr = place(nc, "key_rotated_back", 98, [P, SC], F32)
    k.pt = [place(nc, f"probs_turned_{p}", 138 + 20 * m, [P, 2, NC + NCC, 2 * P], F32R) for m, p in enumerate(("hi", "lo"))]
    k.probs = place(nc, "probs", 183, [P, 2, SC], F32)
    k.mo = place(nc, "mla_out", 193, [P, S], F32)
    k.stat = place(nc, "softmax_stats", 197, [P, 4, 16], F32)
    k.fh = place(nc, "ff_hi", B + 64, [P, 2, S], F32R)
    k.fl = place(nc, "ff_lo", B + 72, [P, 2, S], F32R)
    k.fa = place(nc, "ff_a", 162, [P, 2, S], F32)
    k.fg = place(nc, "ff_g", 170, [P, 2, S], F32)
    k.fs = place(nc, "ff_silu", 178, [P, S], F32)

    k.ps = ctx.enter_context(nc.psum_tensor("psum", [P, 8 * 512], F32))

    k.sems = {}

    def sem(name):
        if name not in k.sems:
            k.sems[name] = ctx.enter_context(nc.semaphore(name))
        return k.sems[name]
    k.sem = sem
    k.T, k.B = T, B
    k.x_ready = lambda eng, c: eng.wait_ge(sem(f"x_loaded{c // 512}"), 16)
    return k


def tile_bank(slot):
    return 1536 * slot


def one(t, i):
    return t[:, bass.ds(i, 1), :].rearrange("p a n -> p (a n)")


def f32(ap):
    return ap.bitcast(F32)


def three(pe, out, lhs, rhs, start, stop, loose=False, first=None):
    (lh, ll), (rh, rl) = lhs, rhs
    mm = pe.matmul(out, lh, rh, start=start, stop=False, skip_group_check=loose)
    if first is not None:
        mm.then_inc(first, 1)
    pe.matmul(out, lh, rl, start=False, stop=False, skip_group_check=loose)
    return pe.matmul(out, ll, rh, start=False, stop=stop, skip_group_check=loose)


def gemm_tile(k, pe, tile, unit, lhs, rhs, depth, width=S, new_unit=True, ready=None, by_chunk=False):
    if new_unit:
        pe.wait_ge(k.sem("weights_split"), unit.value(1))
    pe.wait_ge(k.sem(f"tile_read{tile.slot}"), tile.half(0))
    c0 = tile_bank(tile.slot)
    first = k.sem("unit_started") if new_unit else None
    chunks = [(c, min(512, width - c)) for c in range(0, width, 512)]
    if by_chunk:
        for n, (c, w) in enumerate(chunks):
            for i in range(depth):
                ready(i, n)
                mm = three(pe, k.ps[:, c0 + c:c0 + c + w], lhs(i), rhs(i, c, w), i == 0, i == depth - 1, first=first)
                first = None
        mm.then_inc(k.sem("tile_done"), 1)
        return
    for i in range(depth):
        if ready is not None:
            ready(i, 0)
        for c, w in chunks:
            (lh, ll), (rh, rl) = lhs(i), rhs(i, c, w)
            mm = pe.matmul(k.ps[:, c0 + c:c0 + c + w], lh, rh, start=i == 0, stop=False)
            if first is not None:
                mm.then_inc(first, 1)
                first = None
            pe.matmul(k.ps[:, c0 + c:c0 + c + w], lh, rl, start=False, stop=False)
        for c, w in chunks:
            (lh, ll), (rh, rl) = lhs(i), rhs(i, c, w)
            mm = pe.matmul(k.ps[:, c0 + c:c0 + c + w], ll, rh, start=False, stop=i == depth - 1)
    mm.then_inc(k.sem("tile_done"), 1)


def unit_block(k, slot, stride=P, base=0):
    return lambda i: (k.wh[:, slot, base + i * stride:base + i * stride + P],
                      k.wl[:, slot, base + i * stride:base + i * stride + P])


def act_of(h, l):
    return lambda i, c, w: (h[:, i, c:c + w], l[:, i, c:c + w])


def full_gemm(k, pe, tile, unit, **how):
    gemm_tile(k, pe, tile, unit, unit_block(k, unit.slot), act_of(k.hh, k.hl), DT, **how)


def ada_load(k, act, a, stage, i, j):
    s = ADA_STEP[stage]
    n = ADA * i + (ADA * s + j)
    act.wait_ge(k.sem("ada_used"), n + 1)
    src = a.w_ada[n] if isinstance(n, int) else a.w_ada[bass.ds(n, 1)].rearrange("a p n -> (a p) n")
    act.dma_start(k.adaw[:, :], src).then_inc(k.sem("ada_loaded"), 16)


def ada_product(k, pe, stage, i, j):
    s = ADA_STEP[stage]
    if j == 0:
        pe.wait_ge(k.sem("ada_read"), i + (s + 1))
    pe.wait_ge(k.sem("ada_loaded"), 16 * ADA * i + 16 * (ADA * s + j + 1))
    for t in range(DT):
        mm = pe.matmul(k.ps[:, 3072 + 2 * j:3074 + 2 * j], k.adaw[:, P * t:P * t + P], k.scf[:, 2 * t:2 * t + 2],
                       start=t == 0, stop=t == DT - 1)
    mm.then_inc(k.sem("ada_used"), 1)


def ada_store(k, dve, stage, i):
    s = ADA_STEP[stage]
    dve.wait_ge(k.sem("ada_used"), ADA * i + (ADA * s + ADA + 1))
    dve.tensor_copy(k.mod[:, bass.ds(ADA * i + ADA * s, ADA), :],
                    k.ps[:, 3072:3072 + 2 * ADA].rearrange("p (t n) -> p t n", n=2)).then_inc(k.sem("ada_read"), 1)


def bank(k, tile, width=S, c=0):
    b = tile_bank(tile.slot) + c
    return k.ps[:, b:b + width]


def wait_tile(k, eng, tile):
    eng.wait_ge(k.sem("tile_done"), tile.value(-1))


def read_tile(k, ins, tile):
    return ins.then_inc(k.sem(f"tile_read{tile.slot}"), 1)


def at_stage(stage, what, i, j):
    first = (FIRST_UNIT if what == "unit" else FIRST_TILE)[stage]
    per = next(s[2 if what == "unit" else 3] for s in STAGES if s[0] == stage)
    return At(first + per * i + j) if isinstance(i, int) else At(first + j, per, i)



def load_weights(k, sp, stream, first, last):
    def load(s, u, split):
        if split is not None:
            sp.wait_ge(k.sem("weights_split"), split)
        src = stream[u] if isinstance(u, int) else stream[bass.ds(u, 1)].rearrange("a p n -> (a p) n")
        sp.dma_start(k.raw[:, s, :], src).then_inc(k.sem(f"raw_loaded{s}"), 16)
    while first < last and (first < 2 or first % 2):
        load(first % 2, first, first - 1 if first >= 2 else None)
        first += 1
    if last // 2 > first // 2:
        with sp.Fori(first // 2, last // 2) as r:
            for s in range(2):
                load(s, 2 * r + s, 2 * r + (s - 1))
    if last % 2 and last > first:
        load(0, last - 1, last - 2)


def split_unit(k, pool, s, loaded, ready, started):
    pool.wait_ge(k.sem(f"raw_loaded{s}"), loaded)
    if started is not None:
        pool.wait_ge(k.sem("unit_started"), started)
    pool.tensor_tensor(k.wh[:, s, :], k.raw[:, s, :], k.one32[:, 0:1].to_broadcast([P, UNIT]), ALU.mult
                       ).then_inc(k.sem("weights_hi"), 1)
    pool.wait_ge(k.sem("weights_hi"), ready)
    pool.tensor_tensor(k.wl[:, s, :], k.raw[:, s, :], f32(k.wh[:, s, :]), ALU.subtract
                       ).then_inc(k.sem("weights_split"), 1)


def split_weights(k, pool, first, last):
    if first % 2:
        split_unit(k, pool, 1, 16 * (first // 2) + 16, first + 1, first)
        first += 1
    with pool.Fori(first // 2, last // 2) as r:
        for s in range(2):
            split_unit(k, pool, s, 16 * r + 16, 2 * r + (s + 1), 2 * r + s)
    if last % 2:
        split_unit(k, pool, 0, 16 * (last // 2) + 16, last, last - 1)


def sb_gpsimd(k, pool):
    with pool.Fori(0, PAIRS) as i:
        for u in range(1, 5):
            split_unit(k, pool, u % 2, 32 * i + 16 * (u // 2 + 1), 4 * i + (u + 1), 4 * i + u)
        sb_pool(k, pool, i)



class Norms:

    def __init__(self):
        self.q, self.a, self.c = 0, 0, 0

    def pass_over(self, squares, firsts):
        self.q, self.a = self.q + squares, self.a + squares - firsts


def square_scalar(k, act, n, src, c0, w, first, behind=0):
    if first:
        if n.c > behind:
            act.wait_ge(k.sem("stat_split"), n.c - behind)
        dst = k.acc[:, c0:c0 + w]
    else:
        if n.a >= 2:
            act.wait_ge(k.sem("square_added"), n.a - 1)
        dst = k.sq[:, n.a % 2, :w]
        n.a += 1
    act.activation(dst, src, ACT.Square).then_inc(k.sem("square_done"), 1)
    n.q += 1


def square_add(k, eng, n, c0, w, first):
    n.q += 1
    if first:
        return
    eng.wait_ge(k.sem("square_done"), n.q)
    if n.a >= 1:
        eng.wait_ge(k.sem("square_added"), n.a)
    eng.tensor_tensor(k.acc[:, c0:c0 + w], k.acc[:, c0:c0 + w], k.sq[:, n.a % 2, :w], ALU.add
                      ).then_inc(k.sem("square_added"), 1)
    n.a += 1


def stat_hi_scalar(k, act, n, chunks):
    act.wait_ge(k.sem("square_added"), n.a)
    for c, (c0, w) in enumerate(chunks, n.c):
        if c >= 2:
            act.wait_ge(k.sem("square_summed"), c - 1)
        act.activation(k.sth[:, c % 2, :w], k.acc[:, c0:c0 + w], ACT.Copy).then_inc(k.sem("stat_hi"), 1)


def stat_root_scalar(k, act, n, chunks, features):
    for c0, w in chunks:
        act.wait_ge(k.sem("square_summed"), n.c + 1)
        if n.c >= 1:
            act.wait_ge(k.sem("stat_rstd"), n.c)
        act.activation(k.root[:, :w], k.ps[:, 3072 + 512 * (n.c % 2):3072 + 512 * (n.c % 2) + w], ACT.Sqrt,
                       bias=EPS, scale=1.0 / features).then_inc(k.sem("stat_root"), 1)
        n.c += 1


def stat_lo_vector(k, dve, n, chunks):
    for c, (c0, w) in enumerate(chunks, n.c):
        dve.wait_ge(k.sem("stat_hi"), c + 1)
        dve.tensor_tensor(k.stl[:, c % 2, :w], k.acc[:, c0:c0 + w], f32(k.sth[:, c % 2, :w]), ALU.subtract
                          ).then_inc(k.sem("stat_split"), 1)


def stat_rstd_vector(k, dve, n, chunks):
    for c0, w in chunks:
        n.c += 1
        dve.wait_ge(k.sem("stat_root"), n.c)
        dve.reciprocal(k.rstd[:, c0:c0 + w], k.root[:, :w]).then_inc(k.sem("stat_rstd"), 1)
        dve.wait_ge(k.sem("stat_rstd"), n.c)


def stat_tensor(k, pe, n, chunks):
    for c0, w in chunks:
        b = 3072 + 512 * (n.c % 2)
        pe.wait_ge(k.sem("stat_split"), n.c + 1)
        if n.c >= 2:
            pe.wait_ge(k.sem("stat_root"), n.c - 1)
        pe.matmul(k.ps[:, b:b + w], k.ones[:, :], k.sth[:, n.c % 2, :w], start=True, stop=False)
        pe.matmul(k.ps[:, b:b + w], k.ones[:, :], k.stl[:, n.c % 2, :w], start=False, stop=True
                  ).then_inc(k.sem("square_summed"), 1)
        n.c += 1


HALVES = [(0, 512), (512, 512)]


class Applies:

    def __init__(self):
        self.n, self.biased = 0, 0


def apply_vector(k, dve, ap, src, gain, c0, w=512):
    if ap.n >= NORMED:
        dve.wait_ge(k.sem("normed_split"), ap.n - NORMED + 1)
    dve.scalar_tensor_tensor(k.nt[:, ap.n % NORMED, :w], src, gain, k.rstd[:, c0:c0 + w], ALU.mult, ALU.mult
                             ).then_inc(k.sem("normed"), 1)
    ap.n += 1


def apply_scalar(k, act, ap, hi, bias=None, w=512):
    t = k.nt[:, ap.n % NORMED, :w]
    ap.n += 1
    act.wait_ge(k.sem("normed"), ap.n)
    if bias is not None:
        ap.biased += 1
        act.activation(t, t, ACT.Identity, bias=bias).then_inc(k.sem("normed_biased"), 1)
        act.wait_ge(k.sem("normed_biased"), ap.biased)
    act.activation(hi, t, ACT.Copy).then_inc(k.sem("normed_hi"), 1)


def apply_low(k, pool, ap, hi, lo, w=512):
    t = k.nt[:, ap.n % NORMED, :w]
    ap.n += 1
    pool.wait_ge(k.sem("normed_hi"), ap.n)
    pool.tensor_tensor(lo, t, f32(hi), ALU.subtract).then_inc(k.sem("normed_split"), 1)



LAG_CUM, LAG_OUT = 3, 7


def sb_tensor(k, pe):
    with pe.Fori(0, PAIRS) as i:
        for j in range(4):
            full_gemm(k, pe, at_stage("sb", "tile", i, j), at_stage("sb", "unit", i, j))
        v = at_stage("sb", "tile", i, 2)
        pe.wait_ge(k.sem(f"tile_read{v.slot}"), v.half(1))
        for t in range(NC):
            mm = pe.transpose(k.ps[:, 3072 + P * t:3072 + P * t + P], k.vy[:, P * t:P * t + P],
                              k.const[:, CONSTS["ident"]:CONSTS["ident"] + P])
        mm.then_inc(k.sem("sb_v_turned"), 1)
        for slot in range(2):
            last = at_stage("sb", "tile", i, 2 + slot)
            pe.wait_ge(k.sem(f"tile_read{last.slot}"), last.half(1))
        pe.wait_ge(k.sem("sb_v_split"), i + 1)
        for step in range(NB + LAG_OUT):
            n = step
            if n < NB:
                qc, kb, a, off = BLOCKS[n]
                if n >= 4:
                    pe.wait_ge(k.sem("sb_logits_read"), NB * i + (n - 3))
                b = (0, 512, 1536, 2048)[n % 4]
                r = slice(HD * a, HD * a + HD)
                q = slice(512 * qc + off, 512 * qc + 512)
                three(pe, k.ps[:, b + off:b + 512],
                      (k.kh[r, P * kb:P * kb + P], k.kl[r, P * kb:P * kb + P]), (k.qh[r, q], k.ql[r, q]),
                      True, True).then_inc(k.sem("sb_logits"), 1)
            n = step - LAG_CUM
            if 0 <= n < NB:
                qc, kb, a, off = BLOCKS[n]
                b = 3072 + 512 * a
                head = kb == 4 * qc + 3
                if not head:
                    o = BLOCKS[n - 2][3]
                    pe.wait_ge(k.sem("sb_sums_read"), NB * i + (n - 1))
                    for m in (k.sph, k.spl):
                        pe.matmul(k.ps[:, b + o:b + 512], k.tri[:, P:2 * P], m[:, (n - 2) % 4, o:512],
                                  start=False, stop=False, skip_group_check=True)
                elif n >= 2:
                    pe.wait_ge(k.sem("sb_sums_read"), NB * i + (n - 1))
                pe.wait_ge(k.sem("sb_softplus"), NB * i + (n + 1))
                pe.matmul(k.ps[:, b + off:b + 512], k.tri[:, 0:P], k.sph[:, n % 4, off:512],
                          start=head, stop=False, skip_group_check=True)
                pe.matmul(k.ps[:, b + off:b + 512], k.tri[:, 0:P], k.spl[:, n % 4, off:512],
                          start=False, stop=True, skip_group_check=True).then_inc(k.sem("sb_sums"), 1)
            n = step - LAG_OUT
            if n >= 0:
                qc, kb, a, off = BLOCKS[n]
                b = (1024, 2560)[a]
                if kb == 4 * qc + 3 and qc:
                    pe.wait_ge(k.sem("sb_out_read"), 4 * i + (a + 1))
                pe.wait_ge(k.sem("sb_weights"), NB * i + (n + 1))
                three(pe, k.ps[:, b + off:b + 512], (k.vh[:, kb, :], k.vl[:, kb, :]),
                      (k.ph[:, n % 2, off:512], k.pl[:, n % 2, off:512]),
                      kb == 4 * qc + 3, kb == 0, loose=True).then_inc(k.sem("sb_out"), 1)
        pe.wait_ge(k.sem("sb_sums_read"), NB * i + NB)
        pe.wait_ge(k.sem("sb_out_read"), 4 * i + 4)
        pe.wait_ge(k.sem("sb_logits_read"), NB * i + NB)


def sb_scalar(k, act):
    with act.Fori(0, PAIRS) as i:
        def tile(j):
            t = at_stage("sb", "tile", i, j)
            wait_tile(k, act, t)
            return bank(k, t)
        act.activation(k.qh[:, :], tile(0), ACT.Copy, scale=HD ** -0.5).then_inc(k.sem("sb_qk_hi"), 1)
        act.activation(k.kh[:, :], tile(1), ACT.Copy).then_inc(k.sem("sb_qk_hi"), 1)
        read_tile(k, act.activation(k.vy[:, :], tile(2), ACT.Copy), at_stage("sb", "tile", i, 2))
        read_tile(k, act.activation(k.sg[:, :], tile(3), ACT.Silu), at_stage("sb", "tile", i, 3))
        act.preload_act_table_set("natural_log_exp_and_others")
        act.wait_ge(k.sem("sb_v_turned"), i + 1)
        act.activation(k.vh[:, :, :], k.ps[:, 3072:4096].rearrange("p (t n) -> p t n", t=NC), ACT.Copy).then_inc(k.sem("sb_v_hi"), 1)
        for step in range(NB + 6):
            n = step
            if n < NB:
                off = BLOCKS[n][3]
                act.wait_ge(k.sem("sb_logits"), NB * i + (n + 1))
                if n >= NLOGIT:
                    act.wait_ge(k.sem("sb_weights"), NB * i + (n - NLOGIT + 1))
                b = (0, 512, 1536, 2048)[n % 4]
                act.activation(k.logit[:, n % NLOGIT, off:512], k.ps[:, b + off:b + 512], ACT.Copy
                               ).then_inc(k.sem("sb_logits_read"), 1)
            n = step - 1
            if 0 <= n < NB:
                off = BLOCKS[n][3]
                act.wait_ge(k.sem("sb_clamped"), NB * i + (n + 1))
                act.activation(k.ex[:, n % NEX, off:512], k.ex[:, n % NEX, off:512], ACT.Exp).then_inc(k.sem("sb_exp"), 1)
            m = step - 5
            if 0 <= m < NB:
                mo = BLOCKS[m][3]
                act.wait_ge(k.sem("sb_sums_read"), NB * i + (m + 1))
                act.activation(k.logit[:, m % NLOGIT, mo:512], k.logit[:, m % NLOGIT, mo:512], ACT.Exp).then_inc(k.sem("sb_weight"), 1)
            if 0 <= n < NB:
                act.wait_ge(k.sem("sb_exp"), NB * i + (n + 1))
                act.activation(k.ex[:, n % NEX, off:512], k.ex[:, n % NEX, off:512], ACT.Ln, bias=1.0
                               ).then_inc(k.sem("sb_log"), 1)
            if 0 <= m < NB:
                act.wait_ge(k.sem("sb_weight"), NB * i + (m + 1))
                if m >= 2:
                    act.wait_ge(k.sem("sb_out"), NB * i + (m - 1))
                act.activation(k.ph[:, m % 2, mo:512], k.logit[:, m % NLOGIT, mo:512], ACT.Copy).then_inc(k.sem("sb_weight_hi"), 1)
        act.wait_ge(k.sem("sb_out_read"), 4 * i + 4)
        act.activation(one(k.yh, i), k.vy[:, :], ACT.Copy).then_inc(k.sem("sb_y_hi"), 1)


def sb_pool(k, pool, i):
    for step in range(2, NB + 6):
        n = step - 6
        if n >= 0:
            off = BLOCKS[n][3]
            pool.wait_ge(k.sem("sb_weight_hi"), NB * i + (n + 1))
            pool.tensor_tensor(k.pl[:, n % 2, off:512], k.logit[:, n % NLOGIT, off:512],
                               f32(k.ph[:, n % 2, off:512]), ALU.subtract).then_inc(k.sem("sb_weights"), 1)
        n = step - 2
        if n < NB:
            off = BLOCKS[n][3]
            pool.wait_ge(k.sem("sb_softplus_hi"), NB * i + (n + 1))
            pool.tensor_tensor(k.spl[:, n % 4, off:512], k.ex[:, n % NEX, off:512],
                               f32(k.sph[:, n % 4, off:512]), ALU.subtract).then_inc(k.sem("sb_softplus"), 1)


def sb_vector(k, dve):
    col = CONSTS
    mask, mneg = k.const[:, col["mask"]:col["mask"] + P], k.const[:, col["mneg"]:col["mneg"] + P]
    with dve.Fori(0, PAIRS) as i:
        for j, (hi, lo, scale) in enumerate(((k.qh, k.ql, HD ** -0.5), (k.kh, k.kl, 1.0))):
            t = at_stage("sb", "tile", i, j)
            dve.wait_ge(k.sem("sb_qk_hi"), 2 * i + (j + 1))
            read_tile(k, dve.scalar_tensor_tensor(lo[:, :], bank(k, t), scale, f32(hi[:, :]), ALU.mult,
                                                  ALU.subtract), t)
        dve.wait_ge(k.sem("sb_v_hi"), i + 1)
        dve.tensor_tensor(k.vl[:, :, :], k.ps[:, 3072:4096].rearrange("p (t n) -> p t n", t=NC),
                          f32(k.vh[:, :, :]), ALU.subtract).then_inc(k.sem("sb_v_split"), 1)
        for step in range(NB + LAG_OUT):
            n = step - 2
            if 0 <= n < NB:
                off = BLOCKS[n][3]
                dve.wait_ge(k.sem("sb_log"), NB * i + (n + 1))
                dve.tensor_tensor(k.ex[:, n % NEX, off:512], k.logit[:, n % NLOGIT, off:512], k.ex[:, n % NEX, off:512], ALU.max
                                  ).then_inc(k.sem("sb_max"), 1)
            n = step - 1
            if 0 <= n < NB:
                off = BLOCKS[n][3]
                dve.wait_ge(k.sem("sb_logits_read"), NB * i + (n + 1))
                if n >= NEX:
                    dve.wait_ge(k.sem("sb_softplus"), NB * i + (n - NEX + 1))
                dve.tensor_scalar(k.ex[:, n % NEX, off:512], k.logit[:, n % NLOGIT, off:512], CLAMP, None, ALU.min
                                  ).then_inc(k.sem("sb_clamped"), 1)
            n = step - 2
            if 0 <= n < NB:
                qc, kb, a, off = BLOCKS[n]
                dve.wait_ge(k.sem("sb_max"), NB * i + (n + 1))
                d = slice(off, off + P)
                if kb >= 4 * qc:
                    dve.tensor_tensor(k.ex[:, n % NEX, d], k.ex[:, n % NEX, d], mask, ALU.mult).then_inc(k.sem("sb_masked"), 1)
                    dve.wait_ge(k.sem("sb_masked"), 16 * i + (1 + sum(b[1] >= 4 * b[0] for b in BLOCKS[:n])))
                if n >= 4:
                    dve.wait_ge(k.sem("sb_sums"), NB * i + (n - 1))
                dve.tensor_copy(k.sph[:, n % 4, off:512], k.ex[:, n % NEX, off:512]).then_inc(k.sem("sb_softplus_hi"), 1)
            m = step - 4
            if 0 <= m < NB:
                mqc, mkb, ma, moff = BLOCKS[m]
                b = 3072 + 512 * ma
                dve.wait_ge(k.sem("sb_sums"), NB * i + (m + 1))
                dve.tensor_tensor(k.logit[:, m % NLOGIT, moff:512], k.logit[:, m % NLOGIT, moff:512], k.ps[:, b + moff:b + 512],
                                  ALU.subtract).then_inc(k.sem("sb_sub" if mkb >= 4 * mqc else "sb_sums_read"), 1)
            if 0 <= m < NB and mkb >= 4 * mqc:
                d = slice(moff, moff + P)
                dve.wait_ge(k.sem("sb_sub"), 16 * i + (1 + sum(b[1] >= 4 * b[0] for b in BLOCKS[:m])))
                dve.tensor_tensor(k.logit[:, m % NLOGIT, d], k.logit[:, m % NLOGIT, d], mneg, ALU.min
                                  ).then_inc(k.sem("sb_sums_read"), 1)
            n = step - LAG_OUT
            if n >= 0 and BLOCKS[n][1] == 0:
                qc, kb, a, off = BLOCKS[n]
                b, r, q = (1024, 2560)[a], slice(HD * a, HD * a + HD), slice(512 * qc, 512 * qc + 512)
                g = at_stage("sb", "tile", i, 3)
                dve.wait_ge(k.sem(f"tile_read{g.slot}"), g.half(1))
                dve.wait_ge(k.sem("sb_out"), NB * i + (n + 1))
                dve.tensor_tensor(k.vy[r, q], k.sg[r, q], k.ps[r, b:b + 512], ALU.mult
                                  ).then_inc(k.sem("sb_out_read"), 1)
        dve.wait_ge(k.sem("sb_weights"), NB * i + NB)
        dve.wait_ge(k.sem("sb_softplus"), NB * i + NB)
        dve.wait_ge(k.sem("sb_y_hi"), i + 1)
        dve.tensor_tensor(one(k.yl, i), k.vy[:, :], f32(one(k.yh, i)), ALU.subtract
                          ).then_inc(k.sem("branch_split"), 1)



def loads_scalar(k, act, a):
    for c in range(NCH):
        s = slice(512 * c, 512 * c + 512)
        for h in range(2):
            act.dma_start(k.x[:, 4 * h:4 * h + 4, s], a.x[:, 4 * h:4 * h + 4, s]).then_inc(k.sem(f"x_loaded{c}{h}"), 16)
        if c == 0:
            act.dma_start(k.params[:, :], a.params).then_inc(k.sem("params_loaded"), 16)
    act.dma_start(k.const[:, :], a.consts).then_inc(k.sem("const_loaded"), 16)


def start_scalar(k, act, n, ap):
    for c, chunk in enumerate(HALVES):
        s = slice(512 * c, 512 * c + 512)
        for i in range(DT):
            act.wait_ge(k.sem(f"x_loaded{c}{i // 4}"), 16)
            square_scalar(k, act, n, k.x[:, i, s], *chunk, i == 0, behind=c)
        stat_hi_scalar(k, act, n, [chunk])
        stat_root_scalar(k, act, n, [chunk], D)
        for i in range(DT):
            apply_scalar(k, act, ap, k.hh[:, i, s])
    act.wait_ge(k.sem("params_loaded"), 16)
    act.activation(k.scf[:, :], k.params[:, PARAMS["c"]:PARAMS["c"] + 2 * DT], ACT.Silu).then_inc(k.sem("silu_c"), 1)
    act.wait_ge(k.sem("const_loaded"), 16)
    act.activation(k.tri[:, :], k.const[:, CONSTS["tri"]:CONSTS["tri"] + 2 * P], ACT.Copy).then_inc(k.sem("start_ready"), 1)


def start_vector(k, dve, n, ap):
    dve.memset(k.one32[:, :], 1.0).then_inc(k.sem("one32"), 1)
    dve.wait_ge(k.sem("one32"), 1)
    dve.tensor_copy(k.ones[:, :], k.one32[:, :]).then_inc(k.sem("ones_ready"), 1)
    for s in range(2):
        dve.memset(k.idle[:, s:s + 1], 0.0).then_inc(k.sem(f"tile_read{s}"), 1)
    for s, name in ((2, "ada_used"), (3, "ada_read")):
        dve.memset(k.idle[:, s:s + 1], 0.0).then_inc(k.sem(name), 1)


    dve.wait_ge(k.sem("params_loaded"), 16)
    for c, chunk in enumerate(HALVES):
        s = slice(512 * c, 512 * c + 512)
        for i in range(DT):
            square_add(k, dve, n, *chunk, i == 0)
        stat_lo_vector(k, dve, n, [chunk])
        stat_rstd_vector(k, dve, n, [chunk])
        for i in range(DT):
            dve.wait_ge(k.sem(f"x_loaded{c}{i // 4}"), 16)
            apply_vector(k, dve, ap, k.x[:, i, s], col(k, "pre_g", i), *chunk)
    dve.wait_ge(k.sem("normed"), ap.n)


def start_tensor(k, pe, n):
    pe.wait_ge(k.sem("ones_ready"), 1)
    for chunk in HALVES:
        stat_tensor(k, pe, n, [chunk])


def low_parts(k, pool, ap, hi, lo):
    for c in range(NCH):
        s = slice(512 * c, 512 * c + 512)
        for i in range(DT):
            apply_low(k, pool, ap, hi[:, i, s], lo[:, i, s])


def col(k, name, i=0):
    return k.params[:, PARAMS[name] + i:PARAMS[name] + i + 1]



def merge_tensor(k, pe, stage, b):
    with pe.Fori(0, 2) as i:
        for h in range(2):
            for j in range(2):
                full_gemm(k, pe, at_stage(stage, "tile", i, 4 * h + j), at_stage(stage, "unit", i, 3 * h + j))
                ada_product(k, pe, stage, i, 2 * h + j)
            pe.wait_ge(k.sem("branch_split"), BT * (b + 1))
            for j in range(2):
                u = at_stage(stage, "unit", i, 3 * h + 2)
                gemm_tile(k, pe, at_stage(stage, "tile", i, 4 * h + 2 + j), u,
                          unit_block(k, u.slot, 2 * P, P * j), act_of(k.yh, k.yl), BT, new_unit=j == 0)


def merge_scalar(k, act, a, stage, b):
    with act.Fori(0, 2) as i:
        for h in range(2):
            for j in range(2):
                ada_load(k, act, a, stage, i, 2 * h + j)
                t = at_stage(stage, "tile", i, 4 * h + j)
                wait_tile(k, act, t)
                read_tile(k, act.activation(k.sig[:, j, :], bank(k, t), ACT.Sigmoid), t)


def merge_vector(k, dve, stage, b):
    with dve.Fori(0, 2) as i:
        for h in range(2):
            for j in range(2):
                n = 2 * h + j
                g, t = at_stage(stage, "tile", i, 4 * h + j), at_stage(stage, "tile", i, 4 * h + 2 + j)
                dve.wait_ge(k.sem(f"tile_read{g.slot}"), g.half(1))
                wait_tile(k, dve, t)
                acc = one(k.merged, 4 * i + n)
                if b == 0:
                    read_tile(k, dve.tensor_tensor(acc, k.sig[:, j, :], bank(k, t), ALU.mult), t)
                else:
                    read_tile(k, dve.tensor_tensor(k.prod[:, :], k.sig[:, j, :], bank(k, t), ALU.mult), t)
                    dve.wait_ge(k.sem(f"tile_read{t.slot}"), t.half(1))
                    dve.tensor_tensor(acc, acc, k.prod[:, :], ALU.add).then_inc(k.sem("merged_sum"), 1)
                    dve.wait_ge(k.sem("merged_sum"), 8 * (b - 1) + 4 * i + (n + 1))
        ada_store(k, dve, stage, i)



def pool_tensor(k, pe):
    with pe.Fori(0, 2) as i:
        for h in range(2):
            for j in range(2):
                full_gemm(k, pe, at_stage("pool", "tile", i, 3 * h + j), at_stage("pool", "unit", i, 3 * h + j))
                ada_product(k, pe, "pool", i, 2 * h + j)
            pe.wait_ge(k.sem("pooled_split"), 2 * i + (h + 1))
            u = at_stage("pool", "unit", i, 3 * h + 2)
            gemm_tile(k, pe, at_stage("pool", "tile", i, 3 * h + 2), u, unit_block(k, u.slot),
                      lambda _, c, w: (k.poh[:, c:c + w], k.pol[:, c:c + w]), 1)


def pool_scalar(k, act, a):
    for g in range(BT):
        ada_load(k, act, a, "pool", g // 2, 2 * (g % 2))
        t = at_stage("pool", "tile", g // 2, 3 * (g % 2))
        wait_tile(k, act, t)
        read_tile(k, act.activation(k.pv[:, :], bank(k, t), ACT.Copy), t)
        ada_load(k, act, a, "pool", g // 2, 2 * (g % 2) + 1)
        t = at_stage("pool", "tile", g // 2, 3 * (g % 2) + 1)
        wait_tile(k, act, t)
        read_tile(k, act.activation(k.psg[:, :], bank(k, t), ACT.Silu), t)
        act.wait_ge(k.sem("pooled"), g + 1)
        act.activation(k.poh[:, :], k.pa[:, :], ACT.Copy).then_inc(k.sem("pooled_hi"), 1)
        t = at_stage("pool", "tile", g // 2, 3 * (g % 2) + 2)
        act.wait_ge(k.sem(f"tile_read{t.slot}"), t.half(1))
        act.activation(k.yh[:, g, :], k.py[:, :], ACT.Copy).then_inc(k.sem("pool_y_hi"), 1)


def pool_vector(k, dve, ch):
    for g, w in enumerate(POOL_WINDOWS):
        t = at_stage("pool", "tile", g // 2, 3 * (g % 2))
        dve.wait_ge(k.sem(f"tile_read{t.slot}"), t.half(1))
        src, bufs, d = k.pv, [k.pa, k.pb], 1
        if (w.bit_length() - 1) % 2 == 0:
            bufs = [k.pb, k.pa]
        while d < w:
            dst = bufs[0]
            ch(dve.tensor_copy(dst[:, 0:d], src[:, 0:d]))
            ch(dve.tensor_tensor(dst[:, d:], src[:, d:], src[:, :S - d], ALU.add))
            src, bufs, d = dst, bufs[::-1], 2 * d
        n = CONSTS["cnt"] + 16 * g
        ch(dve.tensor_tensor(k.pa[:, 0:16], k.pa[:, 0:16], k.const[:, n:n + 16], ALU.mult))
        dve.scalar_tensor_tensor(k.pa[:, :], k.pa[:, :], 1.0 / w, k.pv[:, :], ALU.mult, ALU.subtract
                                 ).then_inc(k.sem("pooled"), 1)
        dve.wait_ge(k.sem("pooled_hi"), g + 1)
        dve.tensor_tensor(k.pol[:, :], k.pa[:, :], f32(k.poh[:, :]), ALU.subtract).then_inc(k.sem("pooled_split"), 1)
        dve.wait_ge(k.sem("pooled_split"), g + 1)
        t = at_stage("pool", "tile", g // 2, 3 * (g % 2) + 1)
        dve.wait_ge(k.sem(f"tile_read{t.slot}"), t.half(1))
        t = at_stage("pool", "tile", g // 2, 3 * (g % 2) + 2)
        wait_tile(k, dve, t)
        read_tile(k, dve.scalar_tensor_tensor(k.py[:, :], bank(k, t), col(k, "pool_scale", g), k.psg[:, :],
                                              ALU.mult, ALU.mult), t)
        dve.wait_ge(k.sem("pool_y_hi"), g + 1)
        dve.tensor_tensor(k.yl[:, g, :], k.py[:, :], f32(k.yh[:, g, :]), ALU.subtract).then_inc(k.sem("branch_split"), 1)
        if g % 2:
            ada_store(k, dve, "pool", g // 2)



def conv_tensor(k, pe):
    with pe.Fori(0, BT) as i:
        for j in range(4):
            full_gemm(k, pe, at_stage("conv", "tile", i, j), at_stage("conv", "unit", i, j))
            ada_product(k, pe, "conv", i, j)


def conv_scalar(k, act, a):
    with act.Fori(0, BT) as i:
        ada_load(k, act, a, "conv", i, 0)
        t = at_stage("conv", "tile", i, 0)
        wait_tile(k, act, t)
        read_tile(k, act.activation(k.cg[:, :], bank(k, t), ACT.Copy), t)
        for j in (1, 2, 3):
            ada_load(k, act, a, "conv", i, j)
        t = at_stage("conv", "tile", i, 3)
        wait_tile(k, act, t)
        read_tile(k, act.activation(k.csg[:, :], bank(k, t), ACT.Silu), t)
        act.wait_ge(k.sem("conv_y"), i + 1)
        act.activation(one(k.yh, i), k.cy[:, :], ACT.Copy).then_inc(k.sem("conv_y_hi"), 1)


def conv_vector(k, dve, ch):
    def param(i, j):
        return k.params[:, bass.ds(4 * i + (PARAMS["conv"] + j), 1)]
    with dve.Fori(0, BT) as i, ch.body(i, 3, BT):
        t = at_stage("conv", "tile", i, 0)
        dve.wait_ge(k.sem(f"tile_read{t.slot}"), t.half(1))
        t = at_stage("conv", "tile", i, 1)
        wait_tile(k, dve, t)
        read_tile(k, dve.tensor_tensor(k.cz[:, :], k.cg[:, :], bank(k, t), ALU.mult), t)
        dve.wait_ge(k.sem(f"tile_read{t.slot}"), t.half(1))
        ch(dve.tensor_scalar(k.cy[:, :], k.cz[:, :], param(i, 2), param(i, 3), ALU.mult, ALU.add))
        for j in range(2):
            d = 2 - j
            ch(dve.scalar_tensor_tensor(k.cy[:, d:], k.cz[:, :S - d], param(i, j), k.cy[:, d:], ALU.mult, ALU.add))
        t = at_stage("conv", "tile", i, 2)
        wait_tile(k, dve, t)
        read_tile(k, dve.tensor_tensor(k.cy[:, :], k.cy[:, :], bank(k, t), ALU.mult), t)
        dve.wait_ge(k.sem(f"tile_read{t.slot}"), t.half(1))
        t = at_stage("conv", "tile", i, 3)
        dve.wait_ge(k.sem(f"tile_read{t.slot}"), t.half(1))
        dve.tensor_tensor(k.cy[:, :], k.cy[:, :], k.csg[:, :], ALU.mult).then_inc(k.sem("conv_y"), 1)
        dve.wait_ge(k.sem("conv_y_hi"), i + 1)
        dve.tensor_tensor(one(k.yl, i), k.cy[:, :], f32(one(k.yh, i)), ALU.subtract).then_inc(k.sem("branch_split"), 1)
        ada_store(k, dve, "conv", i)



def out1_tensor(k, pe, n):
    def ready(i, _):
        pe.wait_ge(k.sem("merged_split"), i + 1)
    for j in range(DT):
        full_gemm(k, pe, at_stage("out1", "tile", 0, j), at_stage("out1", "unit", 0, j), ready=None if j else ready)
        if j == CTX_AFTER:
            stat_tensor(k, pe, n, [(S, CTX)])


CTX_AFTER = 4


def out1_scalar(k, act, a, n):
    t = at_stage("out1", "tile", 0, 0)
    wait_tile(k, act, t.plus(-1))
    act.wait_ge(k.sem("merged_sum"), 2 * DT)
    for i in range(DT):
        act.activation(k.hh[:, i, :], k.merged[:, i, :], ACT.Copy).then_inc(k.sem("merged_hi"), 1)
    act.wait_ge(k.sem("ada_used"), 6 * DT + 1)
    act.dma_start(k.ctx[:, :, :], a.ctx).then_inc(k.sem("ctx_loaded"), 16)
    act.wait_ge(k.sem("merged_split"), DT)
    for c in range(NCH):
        act.dma_start(k.x[:, :, 512 * c:512 * c + 512], a.x[:, :, 512 * c:512 * c + 512]
                      ).then_inc(k.sem(f"x_back{c}"), 16)
    for j in range(DT):
        t = at_stage("out1", "tile", 0, j)
        wait_tile(k, act, t)
        read_tile(k, act.activation(k.outr[:, j, :], bank(k, t), ACT.Copy), t)
        act.wait_ge(k.sem(f"tile_read{t.slot}"), t.half(1))
        square_scalar(k, act, n, k.outr[:, j, :], 0, S, j == 0)
        if j == CTX_AFTER - 1:
            act.wait_ge(k.sem("ctx_loaded"), 16)
            for i in range(DT):
                square_scalar(k, act, n, k.ctx[:, i, :], S, CTX, i == 0)
            stat_hi_scalar(k, act, n, [(S, CTX)])
        if j == CTX_AFTER:
            stat_root_scalar(k, act, n, [(S, CTX)], D)
    for i in range(DT):
        act.wait_ge(k.sem("ctx_normed"), i + 1)
        act.activation(k.ctx[:, i, :], k.ctx[:, i, :], ACT.Identity, bias=k.mod[:, i, 1:2]).then_inc(k.sem("ctx_biased"), 1)


def out1_vector(k, dve, n, ch):
    for i in range(DT):
        dve.wait_ge(k.sem("merged_hi"), i + 1)
        dve.tensor_tensor(k.hl[:, i, :], k.merged[:, i, :], f32(k.hh[:, i, :]), ALU.subtract
                          ).then_inc(k.sem("merged_split"), 1)
    dve.wait_ge(k.sem("ada_read"), 6 * DT // ADA + 1)
    for v in range(2):
        ch(dve.tensor_tensor(k.mod[:, :, v], k.mod[:, :, v],
                             k.params[:, PARAMS["b_ada"]:PARAMS["b_ada"] + 6 * DT], ALU.add))
    for j, (first, v, g) in enumerate(((DT, 0, "g1"), (DT, 1, "g1"), (4 * DT, 0, "g2"))):
        ch(dve.scalar_tensor_tensor(k.gm[:, DT * j:DT * j + DT], k.mod[:, first:first + DT, v], 1.0,
                                    k.params[:, PARAMS[g]:PARAMS[g] + DT], ALU.add, ALU.mult))
    for j in range(DT):
        square_add(k, dve, n, 0, S, j == 0)
        if j == CTX_AFTER - 1:
            for i in range(DT):
                square_add(k, dve, n, S, CTX, i == 0)
            stat_lo_vector(k, dve, n, [(S, CTX)])
        if j == CTX_AFTER:
            stat_rstd_vector(k, dve, n, [(S, CTX)])
            for i in range(DT):
                dve.scalar_tensor_tensor(k.ctx[:, i, :], k.ctx[:, i, :], k.gm[:, DT + i:DT + i + 1], k.rstd[:, S:SC],
                                         ALU.mult, ALU.mult).then_inc(k.sem("ctx_normed"), 1)



def enter_scalar(k, act, a, n, ap):
    c0, c1 = HALVES
    stat_hi_scalar(k, act, n, HALVES)
    stat_root_scalar(k, act, n, HALVES, D)

    def squares(c, tiles):
        for i in tiles:
            act.wait_ge(k.sem("x1_done"), DT * c + i + 1)
            square_scalar(k, act, n, k.x[:, i, 512 * c:512 * c + 512], *HALVES[c], i == 0, behind=c)

    def apply(c, tiles):
        for i in tiles:
            apply_scalar(k, act, ap, k.h2h[:, i, 512 * c:512 * c + 512], bias=k.mod[:, i, 0:1])
    squares(0, range(DT))
    stat_hi_scalar(k, act, n, [c0])
    squares(1, range(DT - 2))
    stat_root_scalar(k, act, n, [c0], D)
    squares(1, range(DT - 2, DT))
    stat_hi_scalar(k, act, n, [c1])
    apply(0, range(4))
    stat_root_scalar(k, act, n, [c1], D)
    apply(0, range(4, DT))
    act.wait_ge(k.sem("x1_done"), NCH * DT)
    act.dma_start(a.x1_store, k.x[:, :, :]).then_inc(k.sem("x1_stored"), 16)
    apply(1, range(DT))
    act.wait_ge(k.sem("ctx_biased"), DT)
    act.activation(k.h2h[:, :, S:SC], k.ctx[:, :, :], ACT.Copy).then_inc(k.sem("ctx_hi"), 1)


def enter_vector(k, dve, n, ap, ch):
    c0, c1 = HALVES
    stat_lo_vector(k, dve, n, HALVES)
    stat_rstd_vector(k, dve, n, HALVES)

    def x1(c, tiles):
        s = slice(512 * c, 512 * c + 512)
        dve.wait_ge(k.sem(f"x_back{c}"), 16)
        for i in tiles:
            ch(dve.scalar_tensor_tensor(k.outr[:, i, s], k.outr[:, i, s], col(k, "post_g", i), k.rstd[:, s],
                                        ALU.mult, ALU.mult))
            dve.tensor_tensor(k.x[:, i, s], k.x[:, i, s], k.outr[:, i, s], ALU.add).then_inc(k.sem("x1_done"), 1)

    def apply(c, tiles):
        for i in tiles:
            apply_vector(k, dve, ap, k.x[:, i, 512 * c:512 * c + 512], k.gm[:, i:i + 1], *HALVES[c])
    x1(0, range(DT))
    x1(1, range(4))
    stat_lo_vector(k, dve, n, [c0])
    x1(1, range(4, DT))
    stat_rstd_vector(k, dve, n, [c0])
    dve.wait_ge(k.sem("x1_done"), NCH * DT)
    apply(0, range(4))
    stat_lo_vector(k, dve, n, [c1])
    apply(0, range(4, DT))
    stat_rstd_vector(k, dve, n, [c1])
    apply(1, range(DT))
    dve.wait_ge(k.sem("ctx_hi"), 1)
    dve.tensor_tensor(k.h2l[:, :, S:SC], k.ctx[:, :, :], f32(k.h2h[:, :, S:SC]), ALU.subtract
                      ).then_inc(k.sem("ctx_split"), 1)
    dve.wait_ge(k.sem("normed"), ap.n)


def enter_tensor(k, pe, n):
    stat_tensor(k, pe, n, HALVES)
    stat_tensor(k, pe, n, HALVES)


def enter_gpsimd(k, pool, n, ap):
    for chunk in HALVES:
        for i in range(DT):
            square_add(k, pool, n, *chunk, i == 0)
    low_parts(k, pool, ap, k.h2h, k.h2l)



def h2_gemm(k, pe, tile, unit, width, **how):
    gemm_tile(k, pe, tile, unit, unit_block(k, unit.slot), act_of(k.h2h, k.h2l), DT, width, **how)


LATENTS = (S, S, SC, SC, SC)
KV_CHUNKS = HALVES + [(S, CTX)]


def latents_tensor(k, pe, n, n_applied):
    def ready(i, c):
        pe.wait_ge(k.sem("normed_split"), n_applied + DT * c + i + 1)
    for j, width in enumerate(LATENTS):
        if j == 2:
            pe.wait_ge(k.sem("ctx_split"), 1)
        h2_gemm(k, pe, at_stage("latents", "tile", 0, j), at_stage("latents", "unit", 0, j), width,
                ready=None if j else ready, by_chunk=j == 0)
        if j == 2:
            stat_tensor(k, pe, n, HALVES)
    stat_tensor(k, pe, n, KV_CHUNKS)


def latents_scalar(k, act, a, n):
    act.wait_ge(k.sem("x1_stored"), 16)
    act.dma_start(k.lat_table[:, :], a.mla_table).then_inc(k.sem("lat_table"), 16)
    act.dma_start(k.rtab[:, :, :], a.ret_table).then_inc(k.sem("ret_table"), 16)

    def evacuate(j):
        t = at_stage("latents", "tile", 0, j)
        wait_tile(k, act, t)
        dst = k.cq[:, j, :] if j < 2 else k.ckv[:, j - 2, :]
        read_tile(k, act.activation(dst, bank(k, t, LATENTS[j]), ACT.Copy), t)
        act.wait_ge(k.sem(f"tile_read{t.slot}"), t.half(1))
        return dst
    for j in range(2):
        square_scalar(k, act, n, evacuate(j), 0, S, j == 0)
    stat_hi_scalar(k, act, n, HALVES)
    kv = evacuate(2)
    stat_root_scalar(k, act, n, HALVES, 2 * P)
    square_scalar(k, act, n, kv, 0, SC, True)
    square_scalar(k, act, n, evacuate(3), 0, SC, False)
    stat_hi_scalar(k, act, n, KV_CHUNKS)
    act.wait_ge(k.sem("latent_normed"), 2)
    act.dma_start(a.cq_store, k.cq[:, :, :]).then_inc(k.sem("latents_stored"), 16)
    stat_root_scalar(k, act, n, KV_CHUNKS, 2 * P)
    act.wait_ge(k.sem("latent_normed"), 4)
    act.dma_start(a.ckv_store, k.ckv[:, :, :]).then_inc(k.sem("latents_stored"), 16)
    act.wait_ge(k.sem("key_rotated"), 1)
    act.dma_start(a.kpe_store, k.kpe[64:96, :]).then_inc(k.sem("latents_stored"), 16)
    act.wait_ge(k.sem("latents_stored"), 48)


def latents_vector(k, dve, n, ch):
    def normed(t, gain, w):
        for j in range(2):
            dve.scalar_tensor_tensor(t[:, j, :], t[:, j, :], col(k, gain, j), k.rstd[:, :w], ALU.mult, ALU.mult
                                     ).then_inc(k.sem("latent_normed"), 1)
    for j in range(2):
        square_add(k, dve, n, 0, S, j == 0)
    stat_lo_vector(k, dve, n, HALVES)
    stat_rstd_vector(k, dve, n, HALVES)
    normed(k.cq, "gq", S)
    dve.wait_ge(k.sem("latent_normed"), 2)
    for j in range(2):
        square_add(k, dve, n, 0, SC, j == 0)
    stat_lo_vector(k, dve, n, KV_CHUNKS)
    stat_rstd_vector(k, dve, n, KV_CHUNKS)
    normed(k.ckv, "gkv", SC)
    t = at_stage("latents", "tile", 0, 4)
    dve.wait_ge(k.sem("lat_table"), 16)
    wait_tile(k, dve, t)
    ch(dve.tensor_tensor(k.kpe[64:96, 0:S], k.lat_table[64:96, :], bank(k, t)[64:96, :], ALU.mult))
    ch(dve.tensor_tensor(k.kpt[64:96, :], k.lat_table[96:128, :], bank(k, t)[96:128, :], ALU.mult))
    read_tile(k, dve.tensor_copy(k.kpe[64:96, S:SC], bank(k, t, CTX, S)[64:96, :]), t)
    dve.wait_ge(k.sem(f"tile_read{t.slot}"), t.half(1))
    dve.tensor_tensor(k.kpe[64:96, 0:S], k.kpe[64:96, 0:S], k.kpt[64:96, :], ALU.add).then_inc(k.sem("key_rotated"), 1)
    dve.wait_ge(k.sem("latents_stored"), 48)


RK, RV, RQ, RKT, RVT, RSC, RG, RDF, RDB, RO, RM, RVAR = range(12)


def ret_tensor(k, pe):
    ident = k.const[:, CONSTS["ident"]:CONSTS["ident"] + P]
    hi_lo = lambda pair, s: (pair[0][s], pair[1][s])

    def chunk(pair, c):
        return pair[0][:, c, :], pair[1][:, c, :]

    def cols(pair, c):
        return pair[0][:, P * c:P * c + P], pair[1][:, P * c:P * c + P]

    with pe.Fori(0, RH) as i:
        tile = lambda j: at_stage("ret", "tile", i, j)

        def begin(j):
            t = tile(j)
            pe.wait_ge(k.sem(f"tile_read{t.slot}"), t.half(0))
            return tile_bank(t.slot)

        for j, width in ((RK, SC), (RV, SC), (RQ, S)):
            h2_gemm(k, pe, tile(j), at_stage("ret", "unit", i, j), width)
        for j, src, ready in ((RKT, k.rk, "ret_k_roped"), (RVT, k.rv, None)):
            b = begin(j)
            if ready:
                pe.wait_ge(k.sem(ready), i + 1)
            else:
                t = tile(RV)
                pe.wait_ge(k.sem(f"tile_read{t.slot}"), t.half(1))
            for c in range(NC + NCC):
                mm = pe.transpose(k.ps[:, b + P * c:b + P * c + P], src[:, P * c:P * c + P], ident)
            mm.then_inc(k.sem("tile_done"), 1)
        b = begin(RSC)
        pe.wait_ge(k.sem("ret_qk_split"), 2 * i + 2)
        for c in range(NC):
            mm = three(pe, k.ps[:, b + P * c:b + P * c + P], cols(k.rkf, c), cols(k.rqf, c), True, True)
        mm.then_inc(k.sem("tile_done"), 1)
        h2_gemm(k, pe, tile(RG), at_stage("ret", "unit", i, 3), S)
        t = tile(RVT)
        pe.wait_ge(k.sem(f"tile_read{t.slot}"), t.half(1))
        t = tile(RKT)
        pe.wait_ge(k.sem(f"tile_read{t.slot}"), t.half(1))
        for d, j in enumerate((RDF, RDB)):
            b = begin(j)
            for c in range(NC + NCC):
                mm = three(pe, k.ps[:, b + P * c:b + P * c + P], chunk(k.kz[d], c), chunk(k.rvt, c), True, True)
            mm.then_inc(k.sem("tile_done"), 1)
        b = begin(RO)

        def outs(c):
            return k.ps[:, b + P * c:b + P * c + P]
        pe.wait_ge(k.sem("ret_scores_split"), i + 1)
        for c in range(NC):
            three(pe, outs(c), chunk(k.rvt, c), cols(k.rqf, c), c % 4 == 0, False, loose=True)
        for d, x in enumerate((k.rxf, k.rkf)):
            pe.wait_ge(k.sem("ret_states_split"), 2 * i + (d + 1))
            pe.wait_ge(k.sem("ret_decayed_split"), 2 * i + (d + 1))
            for c in range(NC):
                mm = three(pe, outs(c), chunk(k.st[d], c), cols(x, c), False, d == 1, loose=True)
        mm.then_inc(k.sem("tile_done"), 1)
        for n, (j, pair) in enumerate(((RM, k.rxf), (RVAR, k.rkf))):
            b = begin(j)
            pe.wait_ge(k.sem("ret_stat_split"), 2 * i + (n + 1))
            for c in range(NCH):
                s = slice(512 * c, 512 * c + 512)
                pe.matmul(k.ps[:, b + 512 * c:b + 512 * c + 512], k.ones[:, :], pair[0][:, s], start=True, stop=False)
                mm = pe.matmul(k.ps[:, b + 512 * c:b + 512 * c + 512], k.ones[:, :], pair[1][:, s], start=False, stop=True)
            mm.then_inc(k.sem("tile_done"), 1)


def ret_scalar(k, act, a, ch):
    C = lambda name, w=P: k.const[:, CONSTS[name]:CONSTS[name] + w]
    ch(act.activation(k.lg[:, 0:2 * RH], k.params[:, PARAMS["decay"]:PARAMS["decay"] + 2 * RH], ACT.Exp))
    ch(act.activation(k.lg[:, 0:2 * RH], k.lg[:, 0:2 * RH], ACT.Copy, scale=-1.0))
    act.activation(k.lg[:, 2 * RH:], k.lg[:, 0:2 * RH], ACT.Exp, scale=float(P)).then_inc(k.sem("ret_gammas"), 1)
    act.wait_ge(k.sem("ret_gammas"), 1)

    with act.Fori(0, RH) as i, ch.body(i, 1, RH):
        tile = lambda j: at_stage("ret", "tile", i, j)
        lf, lb = k.lg[:, bass.ds(i, 1)], k.lg[:, bass.ds(i + RH, 1)]
        for src, dst, s in ((C("fwd"), k.dec[:, 0, :], lf), (C("bwd"), k.dec[:, 1, :], lb),
                            (C("xf"), k.dec[:, 3, :], lf), (C("xb"), k.dec[:, 4, :], lb),
                            (C("zf", 1), k.zeta[:, 0:1], lf), (C("zb", 1), k.zeta[:, 1:2], lb)):
            act.activation(dst, src, ACT.Exp, scale=s).then_inc(k.sem("ret_decays"), 1)

        def wait_read(j):
            t = tile(j)
            act.wait_ge(k.sem(f"tile_read{t.slot}"), t.half(1))
        wait_tile(k, act, tile(RV))
        read_tile(k, act.activation(k.rv[:, :], bank(k, tile(RV), SC), ACT.Copy), tile(RV))
        act.wait_ge(k.sem("ret_k_roped"), i + 1)
        act.activation(k.rkf[0][:, :], k.rk[:, 0:S], ACT.Copy, scale=RET_SCALE).then_inc(k.sem("ret_qk_hi"), 1)
        act.wait_ge(k.sem("ret_q_roped"), i + 1)
        act.activation(k.rqf[0][:, :], k.rq[:, :], ACT.Copy).then_inc(k.sem("ret_qk_hi"), 1)
        act.wait_ge(k.sem("ret_zetas"), i + 1)
        wait_tile(k, act, tile(RKT))
        for d in range(2):
            act.activation(k.kz[d][0][:, :, :], bank(k, tile(RKT), SC).rearrange("p (c n) -> p c n", n=P), ACT.Copy,
                           scale=k.zeta[:, 2 + d:3 + d]).then_inc(k.sem("ret_kz_hi"), 1)
        wait_tile(k, act, tile(RVT))
        act.activation(k.rvt[0][:, :, :], bank(k, tile(RVT), SC).rearrange("p (c n) -> p c n", n=P), ACT.Copy
                       ).then_inc(k.sem("ret_vt_hi"), 1)
        wait_read(RSC)
        act.activation(k.rqf[0][:, :], k.rt[:, :], ACT.Copy).then_inc(k.sem("ret_scores_hi"), 1)
        wait_tile(k, act, tile(RG))
        read_tile(k, act.activation(k.rg[:, :], bank(k, tile(RG)), ACT.Silu), tile(RG))
        for d, x in enumerate((k.rxf, k.rkf)):
            act.wait_ge(k.sem("ret_decayed"), 2 * i + (d + 1))
            act.activation(x[0][:, :], k.rt[:, :] if d else k.rv[:, 0:S], ACT.Copy).then_inc(k.sem("ret_decayed_hi"), 1)
            wait_read((RDF, RDB)[d])
            act.activation(k.st[d][0][:, :, :], k.rs[:, :, :], ACT.Copy).then_inc(k.sem("ret_states_hi"), 1)
        wait_tile(k, act, tile(RO))
        act.wait_ge(k.sem("ret_decayed_split"), 2 * i + 2)
        read_tile(k, act.activation(k.rq[:, :], bank(k, tile(RO)), ACT.Copy), tile(RO))
        wait_read(RO)
        act.activation(k.rxf[0][:, :], k.rq[:, :], ACT.Copy).then_inc(k.sem("ret_stat_hi"), 1)
        wait_read(RM)
        act.activation(k.rkf[0][:, :], k.rt[:, :], ACT.Square).then_inc(k.sem("ret_stat_hi"), 1)
        wait_tile(k, act, tile(RVAR))
        read_tile(k, act.activation(k.rs[:, :, :], bank(k, tile(RVAR)).rearrange("p (c n) -> p c n", n=P), ACT.Sqrt,
                                    bias=EPS, scale=1.0 / P), tile(RVAR))
        act.wait_ge(k.sem("ret_out"), i + 1)
        act.dma_start(a.o_store[:, bass.ds(i + BT, 1), :].rearrange("p a n -> p (a n)"), k.rq[:, :]
                      ).then_inc(k.sem("ret_stored"), 16)
        act.wait_ge(k.sem("ret_stored"), 16 * i + 16)
        ch(act.activation(k.idle[:, 1:2], k.idle[:, 1:2], ACT.Copy))


def ret_vector(k, dve, ch):
    PER = 26

    def rope(i, ch, j, dst, done, ctx):
        t = at_stage("ret", "tile", i, j)
        wait_tile(k, dve, t)
        ps = bank(k, t)
        ch(dve.tensor_tensor(dst[:, 0:S], k.rtab[:, 0, :], ps, ALU.mult))
        ch(dve.tensor_tensor(k.rt[0:64, :], k.rtab[64:128, 1, :], ps[64:128, :], ALU.mult))
        if ctx:
            ch(dve.tensor_copy(dst[:, S:SC], bank(k, t, CTX, S)))
        read_tile(k, dve.tensor_tensor(k.rt[64:128, :], k.rtab[0:64, 1, :], ps[0:64, :], ALU.mult), t)
        dve.wait_ge(k.sem(f"tile_read{t.slot}"), t.half(1))
        dve.tensor_tensor(dst[:, 0:S], dst[:, 0:S], k.rt[:, :], ALU.add).then_inc(k.sem(done), 1)
        dve.wait_ge(k.sem(done), i + 1)

    dve.wait_ge(k.sem("ret_table"), 16)
    dve.wait_ge(k.sem("ret_gammas"), 1)
    with dve.Fori(0, RH) as i, ch.body(i, PER, RH):
        tile = lambda j: at_stage("ret", "tile", i, j)
        dve.wait_ge(k.sem("ret_decays"), 6 * i + 6)
        ch(dve.tensor_tensor(k.dec[:, 2, :], k.dec[:, 0, :], k.dec[:, 1, :], ALU.mult))
        dve.tensor_scalar(k.zeta[:, 2:4], k.zeta[:, 0:2], RET_SCALE, None, ALU.mult).then_inc(k.sem("ret_zetas"), 1)
        rope(i, ch, RK, k.rk, "ret_k_roped", True)
        dve.wait_ge(k.sem("ret_qk_hi"), 2 * i + 1)
        dve.scalar_tensor_tensor(k.rkf[1][:, :], k.rk[:, 0:S], RET_SCALE, f32(k.rkf[0][:, :]), ALU.mult, ALU.subtract
                                 ).then_inc(k.sem("ret_qk_split"), 1)
        rope(i, ch, RQ, k.rq, "ret_q_roped", False)
        dve.wait_ge(k.sem("ret_qk_hi"), 2 * i + 2)
        dve.tensor_tensor(k.rqf[1][:, :], k.rq[:, :], f32(k.rqf[0][:, :]), ALU.subtract).then_inc(k.sem("ret_qk_split"), 1)
        kt = bank(k, tile(RKT), SC).rearrange("p (c n) -> p c n", n=P)
        dve.wait_ge(k.sem("ret_zetas"), i + 1)
        for d in range(2):
            dve.wait_ge(k.sem("ret_kz_hi"), 2 * i + 2)
            ins = dve.scalar_tensor_tensor(k.kz[d][1][:, :, :], kt, k.zeta[:, 2 + d:3 + d], f32(k.kz[d][0][:, :, :]),
                                           ALU.mult, ALU.subtract)
            read_tile(k, ins, tile(RKT)) if d else ch(ins)
        dve.wait_ge(k.sem("ret_vt_hi"), i + 1)
        read_tile(k, dve.tensor_tensor(k.rvt[1][:, :, :], bank(k, tile(RVT), SC).rearrange("p (c n) -> p c n", n=P),
                                       f32(k.rvt[0][:, :, :]), ALU.subtract), tile(RVT))
        t = tile(RSC)
        wait_tile(k, dve, t)
        read_tile(k, dve.tensor_tensor(k.rt[:, :].rearrange("p (c n) -> p c n", n=P),
                                       bank(k, t).rearrange("p (c n) -> p c n", n=P),
                                       k.dec[:, 2:3, :].to_broadcast([P, NC, P]), ALU.mult), t)
        dve.wait_ge(k.sem("ret_scores_hi"), i + 1)
        dve.tensor_tensor(k.rqf[1][:, :], k.rt[:, :], f32(k.rqf[0][:, :]), ALU.subtract).then_inc(k.sem("ret_scores_split"), 1)
        dve.wait_ge(k.sem("ret_scores_split"), i + 1)
        t = tile(RVT)
        dve.wait_ge(k.sem(f"tile_read{t.slot}"), t.half(1))
        for d, (j, x) in enumerate(((RDF, k.rxf), (RDB, k.rkf))):
            buf = k.rt[:, :] if d else k.rv[:, 0:S]
            dve.tensor_tensor(buf.rearrange("p (c n) -> p c n", n=P), k.rq[:, :].rearrange("p (c n) -> p c n", n=P),
                              k.dec[:, 3 + d:4 + d, :].to_broadcast([P, NC, P]), ALU.mult
                              ).then_inc(k.sem("ret_decayed"), 1)
            dve.wait_ge(k.sem("ret_decayed_hi"), 2 * i + (d + 1))
            dve.tensor_tensor(x[1][:, :], buf, f32(x[0][:, :]), ALU.subtract).then_inc(k.sem("ret_decayed_split"), 1)
            t = tile(j)
            wait_tile(k, dve, t)
            g = k.lg[:, bass.ds(i + (2 * RH + RH * d), 1)]
            order = list(range(NC)) if d == 0 else list(range(NC - 1, -1, -1))
            near, far = (NC + 1, NC) if d == 0 else (NC, NC + 1)
            inc = lambda c: bank(k, t, P, P * c)
            ch(dve.tensor_scalar(k.rs[:, order[0], :], inc(far), g, None, ALU.mult))
            ch(dve.tensor_tensor(k.rs[:, order[0], :], k.rs[:, order[0], :], inc(near), ALU.add))
            for p, c in zip(order, order[1:]):
                ins = dve.scalar_tensor_tensor(k.rs[:, c, :], k.rs[:, p, :], g, inc(p), ALU.mult, ALU.add)
                if c == order[-1]:
                    read_tile(k, ins, t)
                else:
                    ch(ins)
            dve.wait_ge(k.sem(f"tile_read{t.slot}"), t.half(1))
            dve.wait_ge(k.sem("ret_states_hi"), 2 * i + (d + 1))
            dve.tensor_tensor(k.st[d][1][:, :, :], k.rs[:, :, :], f32(k.st[d][0][:, :, :]), ALU.subtract
                              ).then_inc(k.sem("ret_states_split"), 1)
            dve.wait_ge(k.sem("ret_states_split"), 2 * i + (d + 1))
        dve.wait_ge(k.sem("ret_stat_hi"), 2 * i + 1)
        dve.tensor_tensor(k.rxf[1][:, :], k.rq[:, :], f32(k.rxf[0][:, :]), ALU.subtract).then_inc(k.sem("ret_stat_split"), 1)
        t = tile(RM)
        wait_tile(k, dve, t)
        read_tile(k, dve.scalar_tensor_tensor(k.rt[:, :], bank(k, t), -1.0 / P, k.rq[:, :], ALU.mult, ALU.add), t)
        dve.wait_ge(k.sem(f"tile_read{t.slot}"), t.half(1))
        ch(dve.tensor_tensor(k.rv[:, 0:S], k.rt[:, :], k.rt[:, :], ALU.mult))
        dve.wait_ge(k.sem("ret_stat_hi"), 2 * i + 2)
        dve.tensor_tensor(k.rkf[1][:, :], k.rv[:, 0:S], f32(k.rkf[0][:, :]), ALU.subtract).then_inc(k.sem("ret_stat_split"), 1)
        t = tile(RVAR)
        dve.wait_ge(k.sem(f"tile_read{t.slot}"), t.half(1))
        flat = k.rs[:, :, :].rearrange("p c n -> p (c n)")
        ch(dve.reciprocal(flat, flat))
        ch(dve.scalar_tensor_tensor(k.rt[:, :], k.rt[:, :], k.params[:, bass.ds(i + PARAMS["gret"], 1)], flat,
                                    ALU.mult, ALU.mult))
        dve.tensor_tensor(k.rq[:, :], k.rt[:, :], k.rg[:, :], ALU.mult).then_inc(k.sem("ret_out"), 1)
        dve.wait_ge(k.sem("ret_stored"), 16 * i + 16)



def latents_back_sync(k, sp, a):
    t = at_stage("ret", "tile", RH - 1, RG)
    wait_tile(k, sp, t)
    sp.wait_ge(k.sem("latents_stored"), 48)
    for dst, src, name in ((k.cqr[:, :, :], a.cq_store, "cq"), (k.ckvr[:, :, :], a.ckv_store, "ckv"),
                           (k.kpr[64:96, :], a.kpe_store, "kpe")):
        sp.dma_start(dst, src).then_inc(k.sem(f"{name}_back"), 16)


def latents_back_gpsimd(k, pool):
    pieces = [(k.cqr[:, j, :], [m[:, j, :] for m in k.cqn], "cq", S, P) for j in range(2)]
    pieces += [(k.ckvr[:, j, :], [m[:, j, :] for m in k.ckvn], "ckv", SC, P) for j in range(2)]
    pieces += [(k.kpr[64:96, :], [m[64:96, :] for m in k.mk], "kpe", SC, 32)]
    for n, (src, (hi, lo), name, w, rows) in enumerate(pieces):
        pool.wait_ge(k.sem(f"{name}_back"), 16)
        if rows != P:
            pool.wait_ge(k.sem("latents_split"), n)
        one = k.one32[:, 0:1] if rows == P else k.one32[64:96, 0:1]
        pool.tensor_tensor(hi, src, one.to_broadcast([rows, w]), ALU.mult).then_inc(k.sem("latents_hi"), 1)
        pool.wait_ge(k.sem("latents_hi"), n + 1)
        pool.tensor_tensor(lo, src, f32(hi), ALU.subtract).then_inc(k.sem("latents_split"), 1)
    pool.wait_ge(k.sem("latents_split"), len(pieces))


QB = S // P
HEAD_ORDER = [("S", 0)]
for _q in range(1, QB + 1):
    HEAD_ORDER += ([("S", _q)] if _q < QB else []) + [("T", _q - 1)]
    if _q % 2 == 1 and _q > 1:
        HEAD_ORDER += [("O", _q // 2 - 1)]
HEAD_ORDER += [("O", QB // 2 - 1)]
_tile = {}
for _what in HEAD_ORDER:
    if _what[0] != "O":
        _tile[_what] = 2 + len(_tile)
HEAD_TILES = 2 + len(_tile)


def mla_tensor(k, pe):
    ident = k.const[:, CONSTS["ident"]:CONSTS["ident"] + P]
    pe.wait_ge(k.sem("latents_split"), 5)
    with pe.Fori(0, PAIRS) as i:
        for a in range(2):
            tile = lambda j: at_stage("mla", "tile", i, HEAD_TILES * a + j)
            for j, (x, width) in enumerate(((k.cqn, S), (k.ckvn, SC))):
                u = at_stage("mla", "unit", i, a)
                gemm_tile(k, pe, tile(j), u, unit_block(k, u.slot, base=2 * P * j), act_of(*x), 2, width,
                          new_unit=j == 0)
            t = tile(1)
            pe.wait_ge(k.sem(f"tile_read{t.slot}"), t.half(1))
            t = tile(0)
            pe.wait_ge(k.sem(f"tile_read{t.slot}"), t.half(1))
            for what, q in HEAD_ORDER:
                if what == "S":
                    t = tile(_tile[what, q])
                    pe.wait_ge(k.sem(f"tile_read{t.slot}"), t.half(0))
                    b = tile_bank(t.slot)
                    for c in range(0, SC, 512):
                        w = min(512, SC - c)
                        mm = three(pe, k.ps[:, b + c:b + c + w],
                                   (k.mq[0][0:96, P * q:P * q + P], k.mq[1][0:96, P * q:P * q + P]),
                                   (k.mk[0][0:96, c:c + w], k.mk[1][0:96, c:c + w]), True, True)
                    mm.then_inc(k.sem("tile_done"), 1)
                    if q == 0:
                        for c in range(NC + NCC):
                            mm = pe.transpose(k.ps[:, 3072 + HD * c:3072 + HD * c + HD],
                                              k.mvr[64:128, P * c:P * c + P], ident[64:128, 64:128])
                        mm.then_inc(k.sem("mla_v_turned"), 1)
                elif what == "T":
                    t = tile(_tile[what, q])
                    pe.wait_ge(k.sem(f"tile_read{t.slot}"), t.half(0))
                    pe.wait_ge(k.sem("mla_probs"), 16 * i + (8 * a + q + 1))
                    b = tile_bank(t.slot)
                    for c in range(NC + NCC):
                        mm = pe.transpose(k.ps[:, b + P * c:b + P * c + P], k.probs[:, q % 2, P * c:P * c + P], ident)
                    mm.then_inc(k.sem("tile_done"), 1)
                else:
                    t = tile(_tile["T", 2 * q + 1])
                    pe.wait_ge(k.sem(f"tile_read{t.slot}"), t.half(1))
                    if q == 0:
                        pe.wait_ge(k.sem("mla_v_split"), 2 * i + (a + 1))
                    elif q >= 2:
                        pe.wait_ge(k.sem("mla_out_read"), 8 * i + (4 * a + q - 1))
                    b = 3072 + 512 * (q % 2)
                    for c in range(NC + NCC):
                        mm = three(pe, k.ps[:, b:b + 2 * P], (k.mv[0][:, c, :], k.mv[1][:, c, :]),
                                   (k.pt[0][:, q % 2, c, :], k.pt[1][:, q % 2, c, :]), c == 0, c == NC + NCC - 1)
                    mm.then_inc(k.sem("mla_out"), 1)
            pe.wait_ge(k.sem("mla_out_read"), 8 * i + 4 * a + 4)


def mla_scalar(k, act, a):
    act.dma_start(k.mtab[:, :], a.mla_table).then_inc(k.sem("mtab_back"), 16)
    act.wait_ge(k.sem("mla_v_cleared"), 2)
    with act.Fori(0, PAIRS) as i:
        for h in range(2):
            tile = lambda j: at_stage("mla", "tile", i, HEAD_TILES * h + j)
            wait_tile(k, act, tile(0))
            act.activation(k.mqf[0:64, :], bank(k, tile(0))[0:64, :], ACT.Copy).then_inc(k.sem("mla_q_nope"), 1)
            wait_tile(k, act, tile(1))
            act.activation(k.mk[0][0:64, :], bank(k, tile(1), SC)[0:64, :], ACT.Copy).then_inc(k.sem("mla_k_hi"), 1)
            act.activation(k.mvr[64:128, :], bank(k, tile(1), SC)[64:128, :], ACT.Copy).then_inc(k.sem("mla_v_raw"), 1)
            act.wait_ge(k.sem("mla_q_roped"), 2 * i + (h + 1))
            act.activation(k.mq[0][0:96, :], k.mqf[0:96, :], ACT.Copy).then_inc(k.sem("mla_q_hi"), 1)
            act.wait_ge(k.sem("mla_v_turned"), 2 * i + (h + 1))
            act.activation(k.mv[0][:, :, HD * h:HD * h + HD],
                           k.ps[:, 3072:3072 + 10 * HD].rearrange("p (c n) -> p c n", n=HD), ACT.Copy
                           ).then_inc(k.sem("mla_v_hi"), 1)
            for what, q in HEAD_ORDER:
                n = 8 * h + q
                if what == "S":
                    t = tile(_tile[what, q])
                    act.wait_ge(k.sem("mla_max"), 16 * i + (n + 1))
                    read_tile(k, act.activation(k.probs[:, q % 2, :], bank(k, t, SC), ACT.Exp, scale=MLA_SCALE,
                                                bias=k.stat[:, 1, n:n + 1], accum_out=k.stat[:, 2, n:n + 1]), t)
                elif what == "T":
                    t = tile(_tile[what, q])
                    wait_tile(k, act, t)
                    if q >= 4 and q % 2 == 0:
                        act.wait_ge(k.sem("mla_out"), 8 * i + (4 * h + (q // 2 - 1)))
                    act.activation(k.pt[0][:, (q // 2) % 2, :, P * (q % 2):P * (q % 2) + P],
                                   bank(k, t, SC).rearrange("p (c n) -> p c n", n=P), ACT.Copy
                                   ).then_inc(k.sem("mla_probs_hi"), 1)
        act.wait_ge(k.sem("mla_out_read"), 8 * i + 8)
        act.dma_start(a.o_store[:, bass.ds(i, 1), :].rearrange("p a n -> p (a n)"), k.mo[:, :]
                      ).then_inc(k.sem("mla_stored"), 16)


def mla_vector(k, dve, ch):
    for m in k.mv:
        dve.memset(f32(m[:, :, :]), 0.0).then_inc(k.sem("mla_v_cleared"), 1)
    dve.wait_ge(k.sem("mtab_back"), 16)
    with dve.Fori(0, PAIRS) as i, ch.body(i, 2 + 32, PAIRS):
        for h in range(2):
            tile = lambda j: at_stage("mla", "tile", i, HEAD_TILES * h + j)
            t = tile(0)
            wait_tile(k, dve, t)
            dve.wait_ge(k.sem("mla_q_nope"), 2 * i + (h + 1))
            dve.tensor_tensor(k.mqf[64:96, :], k.mtab[64:96, :], bank(k, t)[64:96, :], ALU.mult
                              ).then_inc(k.sem("mla_q_cos"), 1)
            read_q = dve.tensor_tensor(k.mqt[64:96, :], k.mtab[96:128, :], bank(k, t)[96:128, :], ALU.mult)
            ch(read_q)
            dve.wait_ge(k.sem("mla_q_cos"), 2 * i + (h + 1))
            dve.tensor_tensor(k.mqf[64:96, :], k.mqf[64:96, :], k.mqt[64:96, :], ALU.add).then_inc(k.sem("mla_q_roped"), 1)
            dve.wait_ge(k.sem("mla_q_roped"), 2 * i + (h + 1))
            t1 = tile(1)
            dve.wait_ge(k.sem("mla_v_raw"), 2 * i + (h + 1))
            read_tile(k, dve.tensor_tensor(k.mk[1][0:64, :], bank(k, t1, SC)[0:64, :], f32(k.mk[0][0:64, :]),
                                           ALU.subtract), t1)
            dve.wait_ge(k.sem("mla_q_hi"), 2 * i + (h + 1))
            read_tile(k, dve.tensor_tensor(k.mq[1][0:96, :], k.mqf[0:96, :], f32(k.mq[0][0:96, :]), ALU.subtract), t)
            dve.wait_ge(k.sem("mla_v_hi"), 2 * i + (h + 1))
            dve.tensor_tensor(k.mv[1][:, :, HD * h:HD * h + HD],
                              k.ps[:, 3072:3072 + 10 * HD].rearrange("p (c n) -> p c n", n=HD),
                              f32(k.mv[0][:, :, HD * h:HD * h + HD]), ALU.subtract).then_inc(k.sem("mla_v_split"), 1)

            def normalise(q):
                n = 8 * h + q
                t = tile(_tile["S", q])
                dve.wait_ge(k.sem(f"tile_read{t.slot}"), t.half(1))
                ch(dve.reciprocal(k.stat[:, 3, n:n + 1], k.stat[:, 2, n:n + 1]))
                dve.tensor_scalar(k.probs[:, q % 2, :], k.probs[:, q % 2, :], k.stat[:, 3, n:n + 1], None, ALU.mult
                                  ).then_inc(k.sem("mla_probs"), 1)
            for what, q in HEAD_ORDER:
                n = 8 * h + q
                if what == "S":
                    t = tile(_tile[what, q])
                    wait_tile(k, dve, t)
                    ch(dve.tensor_reduce(k.stat[:, 0, n:n + 1], bank(k, t, SC), AX.X, ALU.max))
                    dve.tensor_scalar(k.stat[:, 1, n:n + 1], k.stat[:, 0, n:n + 1], -MLA_SCALE, None, ALU.mult
                                      ).then_inc(k.sem("mla_max"), 1)
                elif what == "T":
                    t2 = tile(_tile[what, q])
                    dve.wait_ge(k.sem("mla_probs_hi"), 16 * i + (n + 1))
                    ins = dve.tensor_tensor(k.pt[1][:, (q // 2) % 2, :, P * (q % 2):P * (q % 2) + P],
                                            bank(k, t2, SC).rearrange("p (c n) -> p c n", n=P),
                                            f32(k.pt[0][:, (q // 2) % 2, :, P * (q % 2):P * (q % 2) + P]), ALU.subtract)
                    read_tile(k, ins, t2)
                    if q == QB - 2:
                        normalise(QB - 1)
                else:
                    dve.wait_ge(k.sem("mla_out"), 8 * i + (4 * h + q + 1))
                    b = 3072 + 512 * (q % 2)
                    r = slice(HD * h, HD * h + HD)
                    dve.tensor_copy(k.mo[r, 2 * P * q:2 * P * q + 2 * P], k.ps[r, b:b + 2 * P]
                                    ).then_inc(k.sem("mla_out_read"), 1)
                if what == "S" and q:
                    normalise(q - 1)
        dve.wait_ge(k.sem("mla_stored"), 16 * i + 16)



O_ORDER = list(range(BT, DT)) + list(range(BT))


def out2_scalar(k, act, a, n, ap):
    for g in (BT, BT + 2, 0, 2):
        if g == 0:
            act.wait_ge(k.sem("mla_stored"), 16 * PAIRS)
        act.dma_start(k.outr[:, g:g + 2, :], a.o_store[:, g:g + 2, :]).then_inc(k.sem(f"o_back{g}"), 16)
    act.dma_start(k.x[:, :, :], a.x1_store).then_inc(k.sem("x1_back"), 16)
    for i in O_ORDER:
        act.wait_ge(k.sem(f"o_back{i // 2 * 2}"), 16)
        act.activation(k.hh[:, i, :], k.outr[:, i, :], ACT.Copy).then_inc(k.sem("o_hi"), 1)
    for j in range(DT):
        act.wait_ge(k.sem("x2_done"), j + 1)
        square_scalar(k, act, n, k.x[:, j, :], 0, S, j == 0)
    stat_hi_scalar(k, act, n, HALVES)
    stat_root_scalar(k, act, n, HALVES, D)
    for c in range(NCH):
        for i in range(DT):
            apply_scalar(k, act, ap, k.hh[:, i, 512 * c:512 * c + 512], bias=k.mod[:, 3 * DT + i, 0:1])


def out2_vector(k, dve, n, ap):
    for m, i in enumerate(O_ORDER):
        dve.wait_ge(k.sem("o_hi"), m + 1)
        dve.tensor_tensor(k.hl[:, i, :], k.outr[:, i, :], f32(k.hh[:, i, :]), ALU.subtract).then_inc(k.sem("o_split"), 1)
    dve.wait_ge(k.sem("x1_back"), 16)
    for j in range(DT):
        t = at_stage("out2", "tile", 0, j)
        wait_tile(k, dve, t)
        dve.scalar_tensor_tensor(k.x[:, j, :], bank(k, t), k.mod[:, 2 * DT + j, 0:1], k.x[:, j, :],
                                 ALU.mult, ALU.add).then_inc(k.sem("x2_done"), 1)
        dve.wait_ge(k.sem("x2_done"), j + 1)
        read_tile(k, dve.memset(k.idle[:, 0:1], 0.0), t)
        square_add(k, dve, n, 0, S, j == 0)
    stat_lo_vector(k, dve, n, HALVES)
    stat_rstd_vector(k, dve, n, HALVES)
    for c, chunk in enumerate(HALVES):
        for i in range(DT):
            apply_vector(k, dve, ap, k.x[:, i, 512 * c:512 * c + 512], k.gm[:, 2 * DT + i:2 * DT + i + 1], *chunk)


def out2_tensor(k, pe, n):
    def ready(i, _):
        pe.wait_ge(k.sem("o_split"), i + 1)
    for j in range(DT):
        u = at_stage("out2", "unit", 0, j)
        lhs = unit_block(k, u.slot)
        gemm_tile(k, pe, at_stage("out2", "tile", 0, j), u, lambda i: lhs(O_ORDER[i]),
                  lambda i, c, w: act_of(k.hh, k.hl)(O_ORDER[i], c, w), DT, ready=None if j else ready)
    stat_tensor(k, pe, n, HALVES)



def up_tensor(k, pe, stage, i, ready=None):
    for j in range(4):
        r = ready if j == 0 else None
        full_gemm(k, pe, at_stage(stage, "tile", i, j), at_stage(stage, "unit", i, j), ready=r, by_chunk=r is not None)


def down_tensor(k, pe, stage, i, tile0, unit0):
    for j in range(DT):
        u = at_stage(stage, "unit", i, unit0 + j // 4)
        gemm_tile(k, pe, at_stage(stage, "tile", i, tile0 + j), u, unit_block(k, u.slot, 4 * P, P * (j % 4)),
                  act_of(k.fh, k.fl), 2, new_unit=j % 4 == 0)


def up_scalar(k, act, stage, i, step):
    if stage == "ffn":
        act.wait_ge(k.sem("ff_split"), 2 * step)
    for m in range(2):
        for j, dst in ((0, k.fa), (1, k.fg)):
            t = at_stage(stage, "tile", i, 2 * m + j)
            p = PARAMS["conv2"] + 4 * (2 * m + j)
            tap = lambda n: k.params[:, bass.ds(16 * step + (p + n), 1)]
            wait_tile(k, act, t)
            act.activation(dst[:, m, :], bank(k, t), ACT.Identity, scale=tap(1), bias=tap(3)).then_inc(k.sem("ff_middle"), 1)
        act.wait_ge(k.sem(f"tile_read{t.slot}"), t.half(1))
        act.activation(k.fs[:, :], k.fg[:, m, :], ACT.Silu).then_inc(k.sem("ff_silu"), 1)
        act.wait_ge(k.sem("ff_product"), 2 * step + (m + 1))


def up_vector(k, dve, stage, i, step):
    for m in range(2):
        for j, dst in ((0, k.fa), (1, k.fg)):
            t = at_stage(stage, "tile", i, 2 * m + j)
            p = PARAMS["conv2"] + 4 * (2 * m + j)
            tap = lambda n: k.params[:, bass.ds(16 * step + (p + n), 1)]
            dve.wait_ge(k.sem("ff_middle"), 4 * step + (2 * m + j + 1))
            ps = bank(k, t)
            dve.scalar_tensor_tensor(dst[:, m, 1:], ps[:, :S - 1], tap(0), dst[:, m, 1:], ALU.mult, ALU.add
                                     ).then_inc(k.sem("ff_back"), 1)
            dve.wait_ge(k.sem("ff_back"), 4 * step + (2 * m + j + 1))
            read_tile(k, dve.scalar_tensor_tensor(dst[:, m, :S - 1], ps[:, 1:], tap(2), dst[:, m, :S - 1],
                                                  ALU.mult, ALU.add), t)
            dve.wait_ge(k.sem(f"tile_read{t.slot}"), t.half(1))
        dve.wait_ge(k.sem("ff_silu"), 2 * step + (m + 1))
        dve.tensor_tensor(k.fa[:, m, :], k.fa[:, m, :], k.fs[:, :], ALU.mult).then_inc(k.sem("ff_product"), 1)


def split_scalar(k, act, step, last_tile):
    wait_tile(k, act, last_tile)
    for m in range(2):
        act.wait_ge(k.sem("ff_product"), 2 * step + (m + 1))
        act.activation(k.fh[:, m, :], k.fa[:, m, :], ACT.Copy).then_inc(k.sem("ff_hi"), 1)


def split_vector(k, dve, step):
    for m in range(2):
        dve.wait_ge(k.sem("ff_hi"), 2 * step + (m + 1))
        dve.tensor_tensor(k.fl[:, m, :], k.fa[:, m, :], f32(k.fh[:, m, :]), ALU.subtract).then_inc(k.sem("ff_split"), 1)
    dve.wait_ge(k.sem("ff_split"), 2 * step + 2)


def down_vector(k, dve, stage, i, tile0):
    for j in range(DT):
        t = at_stage(stage, "tile", i, tile0 + j)
        wait_tile(k, dve, t)
        read_tile(k, dve.scalar_tensor_tensor(k.x[:, j, :], bank(k, t), k.mod[:, 5 * DT + j, 0:1], k.x[:, j, :],
                                              ALU.mult, ALU.add), t)


LAST = FT // 2 - 1


def ffn_tensor(k, pe, n_applied):
    def ready(i, c):
        pe.wait_ge(k.sem("normed_split"), n_applied + DT * c + i + 1)
    up_tensor(k, pe, "up0", 0, ready)
    with pe.Fori(0, LAST) as i:
        up_tensor(k, pe, "ffn", i)
        pe.wait_ge(k.sem("ff_split"), 2 * i + 2)
        down_tensor(k, pe, "ffn", i, 4, 4)
    pe.wait_ge(k.sem("ff_split"), 2 * LAST + 2)
    down_tensor(k, pe, "down", 0, 0, 0)


def ffn_scalar(k, act):
    up_scalar(k, act, "up0", 0, 0)
    split_scalar(k, act, 0, at_stage("up0", "tile", 0, 3))
    with act.Fori(0, LAST) as i:
        up_scalar(k, act, "ffn", i, i + 1)
        split_scalar(k, act, i + 1, at_stage("ffn", "tile", i, 11))


def ffn_vector(k, dve):
    up_vector(k, dve, "up0", 0, 0)
    split_vector(k, dve, 0)
    with dve.Fori(0, LAST) as i:
        up_vector(k, dve, "ffn", i, i + 1)
        down_vector(k, dve, "ffn", i, 4)
        split_vector(k, dve, i + 1)



def end_scalar(k, act, n):
    for j in range(DT):
        act.wait_ge(k.sem("x3_done"), j + 1)
        square_scalar(k, act, n, k.x[:, j, :], 0, S, j == 0)
    stat_hi_scalar(k, act, n, HALVES)
    stat_root_scalar(k, act, n, HALVES, D)


def end_vector(k, dve, n):
    for j in range(DT):
        t = at_stage("down", "tile", 0, j)
        wait_tile(k, dve, t)
        dve.scalar_tensor_tensor(k.x[:, j, :], bank(k, t), k.mod[:, 5 * DT + j, 0:1], k.x[:, j, :],
                                 ALU.mult, ALU.add).then_inc(k.sem("x3_done"), 1)
        dve.wait_ge(k.sem("x3_done"), j + 1)
        read_tile(k, dve.memset(k.idle[:, 0:1], 0.0), t)
        square_add(k, dve, n, 0, S, j == 0)
    stat_lo_vector(k, dve, n, HALVES)
    stat_rstd_vector(k, dve, n, HALVES)
    for c in range(NCH):
        s = slice(512 * c, 512 * c + 512)
        for i in range(DT):
            dve.scalar_tensor_tensor(k.outr[:, i, s], k.x[:, i, s], col(k, "gfin", i), k.rstd[:, s], ALU.mult, ALU.mult
                                     ).then_inc(k.sem("finished"), 1)


def end_tensor(k, pe, n):
    stat_tensor(k, pe, n, HALVES)


def end_sync(k, sp, a):
    for c in range(NCH):
        s = slice(512 * c, 512 * c + 512)
        for h in range(2):
            sp.wait_ge(k.sem("finished"), DT * c + 4 * h + 4)
            sp.dma_start(a.out[:, 4 * h:4 * h + 4, s], k.outr[:, 4 * h:4 * h + 4, s]).then_inc(k.sem("out_stored"), 16)
    sp.wait_ge(k.sem("out_stored"), 16 * 2 * NCH)



class Arrays:
    pass


def two_blocks_program(nc, stream, w_ada, x, context, params, consts, ret_table, mla_table, out):
    a = Arrays()
    a.w_ada, a.x, a.ctx, a.ret_table, a.mla_table, a.out, a.params, a.consts = w_ada, x, context, ret_table, mla_table, out, params, consts
    a.x1_store = nc.dram_tensor("x1_store", (P, DT, S), F32).ap()
    a.cq_store = nc.dram_tensor("cq_store", (P, 2, S), F32).ap()
    a.ckv_store = nc.dram_tensor("ckv_store", (P, 2, SC), F32).ap()
    a.kpe_store = nc.dram_tensor("kpe_store", (32, SC), F32).ap()
    a.o_store = nc.dram_tensor("o_store", (P, DT, S), F32).ap()
    with ExitStack() as ctx:
        k = lay_out(nc, ctx)
        block = ctx.enter_context(nc.Block())

        @block.sync
        def _(sp):
            mla = FIRST_UNIT["mla"]
            load_weights(k, sp, stream, 0, mla + 3)
            latents_back_sync(k, sp, a)
            load_weights(k, sp, stream, mla + 3, NUNITS)
            end_sync(k, sp, a)

        @block.gpsimd
        def _(pool):
            n, ap = Norms(), Applies()
            pool.wait_ge(k.sem("one32"), 1)
            split_unit(k, pool, 0, 16, 1, None)
            low_parts(k, pool, ap, k.hh, k.hl)
            n.pass_over(2 * DT, 2)
            sb_gpsimd(k, pool)
            split_weights(k, pool, FIRST_UNIT["merge_sb"] + 1, FIRST_UNIT["latents"] + 1)
            n.pass_over(2 * DT, 2)
            enter_gpsimd(k, pool, n, ap)
            split_weights(k, pool, FIRST_UNIT["latents"] + 1, FIRST_UNIT["mla"] + 1)
            latents_back_gpsimd(k, pool)
            split_weights(k, pool, FIRST_UNIT["mla"] + 1, FIRST_UNIT["up0"] + 1)
            low_parts(k, pool, ap, k.hh, k.hl)
            split_weights(k, pool, FIRST_UNIT["up0"] + 1, NUNITS)

        @block.scalar
        def _(act):
            ch = Chain(act, k.sem("scalar_steps"))
            n, ap = Norms(), Applies()
            loads_scalar(k, act, a)
            start_scalar(k, act, n, ap)
            sb_scalar(k, act)
            merge_scalar(k, act, a, "merge_sb", 0)
            pool_scalar(k, act, a)
            merge_scalar(k, act, a, "merge_pool", 1)
            conv_scalar(k, act, a)
            merge_scalar(k, act, a, "merge_conv", 2)
            out1_scalar(k, act, a, n)
            enter_scalar(k, act, a, n, ap)
            latents_scalar(k, act, a, n)
            ret_scalar(k, act, a, ch)
            mla_scalar(k, act, a)
            out2_scalar(k, act, a, n, ap)
            ffn_scalar(k, act)
            end_scalar(k, act, n)

        @block.vector
        def _(dve):
            ch = Chain(dve, k.sem("vector_steps"))
            n, ap = Norms(), Applies()
            start_vector(k, dve, n, ap)
            sb_vector(k, dve)
            merge_vector(k, dve, "merge_sb", 0)
            pool_vector(k, dve, ch)
            merge_vector(k, dve, "merge_pool", 1)
            conv_vector(k, dve, ch)
            merge_vector(k, dve, "merge_conv", 2)
            out1_vector(k, dve, n, ch)
            enter_vector(k, dve, n, ap, ch)
            n.pass_over(2 * DT, 2)
            latents_vector(k, dve, n, ch)
            ret_vector(k, dve, ch)
            mla_vector(k, dve, ch)
            out2_vector(k, dve, n, ap)
            ffn_vector(k, dve)
            end_vector(k, dve, n)

        @block.tensor
        def _(pe):
            n = Norms()
            start_tensor(k, pe, n)
            pe.wait_ge(k.sem("start_ready"), 1)
            pe.wait_ge(k.sem("silu_c"), 1)
            pe.wait_ge(k.sem("normed_split"), NCH * DT)
            sb_tensor(k, pe)
            merge_tensor(k, pe, "merge_sb", 0)
            pool_tensor(k, pe)
            merge_tensor(k, pe, "merge_pool", 1)
            conv_tensor(k, pe)
            merge_tensor(k, pe, "merge_conv", 2)
            out1_tensor(k, pe, n)
            enter_tensor(k, pe, n)
            latents_tensor(k, pe, n, 2 * DT)
            ret_tensor(k, pe)
            mla_tensor(k, pe)
            out2_tensor(k, pe, n)
            ffn_tensor(k, pe, 4 * DT)
            end_tensor(k, pe, n)





def fm(v):
    return np.asarray(v).reshape(-1, P).T


def blocks(w, cols=P):
    kk, n = w.shape
    return w.reshape(kk // P, P, n // cols, cols).transpose(2, 1, 0, 3).reshape(n // cols, P, kk // P * cols)


def padded(u):
    return np.concatenate([u, np.zeros(u.shape[:2] + (UNIT - u.shape[2],), u.dtype)], 2)


def weight_stream(i):
    w_in, w2 = i["w_in"][0], i["w_in_2"][0]
    sec = [blocks(w_in[:, W * n:W * n + W]) for n in range(10)]
    gates = blocks(w_in[:, 10 * W:])
    out = []
    for p in range(PAIRS):
        out += [sec[6][p], sec[7][p], sec[8][p], sec[9][p]]

    def merge(b):
        g, br = gates[DT * b:DT * b + DT], blocks(i["w_branch"][0][b], 2 * P)
        for t in range(0, DT, 2):
            out.extend([g[t], g[t + 1], br[t // 2]])
    merge(2)
    for g in range(BT):
        out += [sec[0][g], sec[1][g], padded(i["pool_w"][0][g][None])[0]]
    merge(0)
    for t in range(BT):
        out += [sec[4][t], sec[2][t], sec[3][t], sec[5][t]]
    merge(1)
    out += list(blocks(i["w_out"][0]))
    lat = blocks(w2[:, :512])
    kpe = w2[:, 512:544]
    swap = np.concatenate([kpe[:, 8:16], kpe[:, :8], kpe[:, 24:32], kpe[:, 16:24]], 1)
    out += list(lat) + list(blocks(np.concatenate([np.zeros((D, 64), kpe.dtype), kpe, swap], 1)))
    r = [blocks(w2[:, 544 + W * n:544 + W * n + W]) for n in range(4)]
    for h in range(RH):
        out += [r[1][h], r[2][h], r[0][h], r[3][h]]
    uq, ukv = i["w_uq_2"][0], i["w_ukv_2"][0]
    for p in range(PAIRS):
        for h in (2 * p, 2 * p + 1):
            m = uq[:, 96 * h:96 * h + 96]
            pe = m[:, 64:]
            sw = np.concatenate([pe[:, 8:16], pe[:, :8], pe[:, 24:32], pe[:, 16:24]], 1)
            q, kv = blocks(np.concatenate([m, sw], 1))[0], blocks(ukv[:, P * h:P * h + P])[0]
            out += [padded(np.concatenate([q, kv], 1)[None])[0]]
    out += list(blocks(i["w_out_2"][0]))
    up, down = blocks(i["w_up_2"][0]), i["w_down_2"][0]

    def add_up(g):
        out.extend([up[2 * g], up[FT + 2 * g], up[2 * g + 1], up[FT + 2 * g + 1]])

    def add_down(g):
        rows = down[2 * P * g:2 * P * g + 2 * P]
        out.extend(rows.reshape(2, P, 2, W).transpose(2, 1, 0, 3).reshape(2, P, UNIT))
    add_up(0)
    for g in range(1, FT // 2):
        add_up(g)
        add_down(g - 1)
    add_down(FT // 2 - 1)
    assert len(out) == NUNITS
    return np.stack(out)


def vectors(i):
    cw2 = np.concatenate([i["conv_w_2"][0], i["conv_b_2"][0][None]])
    cw2 = cw2.reshape(4, 2, FT // 1, P).transpose(3, 2, 1, 0).reshape(P, -1)
    cw = np.concatenate([i["conv_w"][0], i["conv_b"][0][None]]).reshape(4, BT, P).transpose(2, 1, 0).reshape(P, -1)
    c = np.stack([fm(i["c_2"][0]), fm(i["c_ctx_2"])], 2).reshape(P, -1)
    parts = [fm(i["pre_norm_g"][0]), fm(i["pool_scale"][0]), cw, fm(i["post_norm_g"][0]), c, fm(i["b_ada_2"][0]),
             fm(i["g_norm1_2"][0]), fm(i["g_q_2"][0]), fm(i["g_kv_2"][0]), fm(i["g_ret_2"][0]),
             fm(i["g_norm2_2"][0]), cw2, fm(i["g_final_2"]), np.tile(i["ret_decay_2"][0].reshape(1, -1), (P, 1))]
    v = np.ascontiguousarray(np.concatenate(parts, 1))
    assert v.shape == (P, NPARAM)
    return v


def tokens_last(x):
    return np.ascontiguousarray(x.T.reshape(-1, P, x.shape[0]).transpose(1, 0, 2))



def kernel(**inputs):
    import concourse.bacc as _bacc
    from concourse.bass_utils import run_bass_kernel_spmd as _run

    i = {name: np.asarray(v) for name, v in inputs.items()}
    ret_table, mla_table = rope_tables()
    arrays = {"in_stream": weight_stream(i), "in_w_ada": np.ascontiguousarray(blocks(i["w_ada_2"][0])),
              "in_x": tokens_last(i["x"][0]), "in_context": tokens_last(i["ctx_2"][0]),
              "in_params": vectors(i), "in_consts": constants(),
              "in_ret_table": np.ascontiguousarray(ret_table.reshape(P, 2, S)), "in_mla_table": mla_table}
    nc = _bacc.Bacc("TRN2", target_bir_lowering=False, num_devices=1)
    args = [nc.dram_tensor(n, v.shape, mybir.dt.from_np(v.dtype), kind="ExternalInput").ap() for n, v in arrays.items()]
    out = nc.dram_tensor("out_0_dram", (P, DT, S), F32, kind="ExternalOutput").ap()
    two_blocks_program(nc, *args, out)
    r = _run(nc, [arrays], core_ids=[0])
    got = np.asarray(r.results[0]["out_0_dram"])
    return np.ascontiguousarray(got.transpose(2, 1, 0).reshape(1, S, D))
```

```python
from contextlib import ExitStack, contextmanager

import numpy as np
import concourse.bass as bass
from concourse import mybir

F32 = mybir.dt.float32
F32R = mybir.dt.float32r
ACT = mybir.ActivationFunctionType
ALU = mybir.AluOpType
AX = mybir.AxisListType

P = 128
S = 1024
CTX = 256
SC = S + CTX
D = 1024
DT = D // P
W = 512
BT = W // P
NCH = S // 512
UNIT = 1024
EPS = 1e-6
POOL_WINDOWS = (2, 4, 8, 16)
HD = 64
PAIRS = BT
MLA_SCALE = 96.0 ** -0.5
RET_SCALE = 128.0 ** -0.5
RH = 4
NC = S // P
NCC = CTX // P
FF = 2816
FT = FF // P
CLAMP = 30.0
BIG = 1e30

PARAMS, _n = {}, 0
for _name, _w in (("pre_g", DT), ("pool_scale", BT), ("conv", 4 * BT), ("post_g", DT), ("c", 2 * DT),
                  ("b_ada", 6 * DT), ("g1", DT), ("gq", 2), ("gkv", 2), ("gret", RH), ("g2", DT),
                  ("conv2", 4 * 2 * FT), ("gfin", DT), ("decay", 2 * RH)):
    PARAMS[_name] = _n
    _n += _w
NPARAM = _n

CONSTS, _n = {}, 0
for _name, _w in (("tri", P), ("rest", P), ("ident", P), ("mask", P), ("mneg", P), ("cnt", 16 * BT),
                  ("fwd", P), ("bwd", P), ("xf", P), ("xb", P), ("zf", 1), ("zb", 1)):
    CONSTS[_name] = _n
    _n += _w
NCONST = _n


def constants():
    c = np.zeros((P, NCONST), np.float32)
    r = np.arange(P)
    k, q = r[:, None], r[None, :]

    def put(name, a):
        a = np.broadcast_to(a, (P, a.shape[-1]))
        c[:, CONSTS[name]:CONSTS[name] + a.shape[1]] = a

    put("tri", (k >= q).astype(np.float32))
    put("rest", (k < q).astype(np.float32))
    put("ident", (k == q).astype(np.float32))
    put("mask", (k < q).astype(np.float32))
    put("mneg", np.where(k < q, BIG, -BIG).astype(np.float32))
    for g, w in enumerate(POOL_WINDOWS):
        c[:, CONSTS["cnt"] + 16 * g:CONSTS["cnt"] + 16 * g + 16] = w / np.minimum(np.arange(16) + 1, w)
    put("fwd", np.maximum(q - k, 0).astype(np.float32))
    put("bwd", np.maximum(k - q, 0).astype(np.float32))
    put("xf", (q + 1).astype(np.float32))
    put("xb", (P - q).astype(np.float32))
    put("zf", (P - 1 - k).astype(np.float32))
    put("zb", k.astype(np.float32))
    return c


def rope_tables():
    def inv(dim):
        return (np.float32(10000.0) ** (-np.arange(0, dim, 2, dtype=np.float32) / np.float32(dim))).astype(np.float32)
    pos = np.arange(S, dtype=np.float32)
    a = inv(P)[:, None] * pos[None, :]
    a = np.concatenate([a, a])
    sign = np.where(np.arange(P) < P // 2, 1.0, -1.0)[:, None]
    ret = np.stack([np.cos(a), np.sin(a) * sign], 1)
    row, col = np.floor(pos / 64), pos % 64
    half = []
    for p in (row, col):
        b = inv(16)[:, None] * p[None, :].astype(np.float32)
        half.append(np.concatenate([b, b]))
    b = np.concatenate(half)
    sgn = np.tile(np.repeat([-1.0, 1.0], 8), 2)[:, None]
    mla = np.zeros((P, S))
    mla[64:96] = np.cos(b)
    mla[96:128] = np.sin(b) * sgn
    return ret.reshape(P, 2 * S).astype(np.float32), mla.astype(np.float32)


class At:

    def __init__(self, base, per=0, i=None):
        self.base, self.per, self.i = base, per, i

    def plus(self, n):
        return At(self.base + n, self.per, self.i)

    @property
    def slot(self):
        assert self.per % 2 == 0
        return self.base % 2

    def value(self, extra=0):
        return self.base + extra if self.i is None else self.per * self.i + (self.base + extra)

    def half(self, extra=0):
        return self.base // 2 + extra if self.i is None else (self.per // 2) * self.i + (self.base // 2 + extra)


class Chain:

    def __init__(self, eng, sem):
        self.eng, self.sem, self.n, self.i, self.per, self.start = eng, sem, 0, None, 0, 0

    def value(self):
        return self.n if self.i is None else self.per * self.i + self.n

    def __call__(self, ins):
        self.n += 1
        ins.then_inc(self.sem, 1)
        self.eng.wait_ge(self.sem, self.value())

    @contextmanager
    def body(self, i, per, times):
        self.i, self.per, self.start = i, per, self.n
        yield
        assert self.n - self.start == per, f"{self.n - self.start} steps in a body of {per}"
        self.i, self.n = None, self.start + per * times


class Core:
    pass



STAGES = (
    ("sb", PAIRS, 4, 4),
    ("merge_sb", 2, 6, 8),
    ("pool", 2, 6, 6),
    ("merge_pool", 2, 6, 8),
    ("conv", BT, 4, 4),
    ("merge_conv", 2, 6, 8),
    ("out1", 1, DT, DT),
    ("latents", 1, 5, 5),
    ("ret_first", 1, 3, 3),
    ("ret", RH - 1, 4, 12),
    ("ret_last", 1, 1, 9),
    ("mla_first", 1, 1, 3),
    ("mla", PAIRS - 1, 2, 38),
    ("mla_last", 1, 1, 35),
    ("out2", 1, DT, DT),
    ("up0", 1, 4, 4),
    ("ffn", FT // 2 - 1, 6, 12),
    ("down", 1, 2, 8),
)
FIRST_UNIT, FIRST_TILE, _u, _t = {}, {}, 0, 2
for _name, _steps, _units, _tiles in STAGES:
    FIRST_UNIT[_name], FIRST_TILE[_name] = _u, _t
    _u, _t = _u + _steps * _units, _t + _steps * _tiles
NUNITS = _u

ADA = 4
ADA_STEP, _u = {}, 0
for _name, _steps, _, _ in STAGES:
    if _name in ("merge_sb", "pool", "merge_pool", "conv", "merge_conv"):
        ADA_STEP[_name] = _u
        _u += _steps
assert ADA * _u == 6 * DT

BLOCKS = [(qc, kb, a, max(0, kb - 4 * qc) * P)
          for qc in range(NCH) for kb in range(4 * qc + 3, -1, -1) for a in range(2)]
NB = len(BLOCKS)


NLOGIT, NEX = 7, 3
NPROBS = 3
NORMED = 3


def place(nc, name, kb, shape, dt):
    if kb == 0:
        with nc.sbuf_tensor(name, shape, dt) as t:
            return t
    with nc.sbuf_tensor(f"{name}_before", [P, int(kb * 256)], F32):
        with nc.sbuf_tensor(name, shape, dt) as t:
            pass
    return t


def lay_out(nc, ctx):
    k = Core()
    k.wh = place(nc, "weights_hi", 0, [P, 2, UNIT], F32R)
    k.wl = place(nc, "weights_lo", 8, [P, 2, UNIT], F32R)
    k.raw = place(nc, "weights_raw", 16, [P, 2, UNIT], F32)
    k.const = place(nc, "constants", 24, [P, NCONST], F32)
    k.params = place(nc, "params", 29, [P, NPARAM], F32)
    k.tri = place(nc, "tri", 30.5, [P, 2 * P], F32R)
    k.adaw = place(nc, "modulation_weights", 202, [P, UNIT], F32)
    k.adas = place(nc, "modulation_sums", 206, [P, 2, P], F32)
    k.one32 = place(nc, "ones_f32", 32, [P, P], F32)
    k.mod = place(nc, "modulation", 32.5, [P, 6 * DT, 2], F32)
    k.scf = place(nc, "silu_c", 33.25, [P, 2 * DT], F32)
    k.gm = place(nc, "gains", 33.5, [P, 4 * DT], F32)
    k.idle = place(nc, "idle", 33.75, [P, 16], F32)
    B = 34
    k.hh = place(nc, "h_hi", B, [P, DT, S], F32R)
    k.hl = place(nc, "h_lo", B + 32, [P, DT, S], F32R)
    k.yh = place(nc, "branch_hi", B + 64, [P, BT, S], F32R)
    k.yl = place(nc, "branch_lo", B + 80, [P, BT, S], F32R)
    k.outr = place(nc, "mixed", B + 64, [P, DT, S], F32)
    k.merged = place(nc, "merged", B + 96, [P, DT, S], F32)
    T = B + 96
    k.x = place(nc, "x", T, [P, DT, S], F32)
    N0 = T + 32
    k.sq = place(nc, "squares", N0, [P, 2, SC], F32)
    k.acc = place(nc, "square_sums", N0 + 10, [P, SC], F32)
    k.diag = place(nc, "diagonals", N0 + 15, [P, 2, 512], F32)
    k.root = place(nc, "roots_and_inverses", N0 + 19, [P, 4, 4], F32)
    k.rstd = place(nc, "rstd", N0 + 23, [P, SC], F32)
    k.nt = place(nc, "normed", N0 + 28, [P, NORMED, 512], F32)
    k.qh = place(nc, "q_hi", T, [P, S], F32R)
    k.ql = place(nc, "q_lo", T + 4, [P, S], F32R)
    k.kh = place(nc, "k_hi", T + 8, [P, S], F32R)
    k.kl = place(nc, "k_lo", T + 12, [P, S], F32R)
    k.vh = place(nc, "v_hi", T + 16, [P, NC, P], F32R)
    k.vl = place(nc, "v_lo", T + 20, [P, NC, P], F32R)
    k.sph = place(nc, "softplus_hi", T + 24, [P, 4, 512], F32R)
    k.spl = place(nc, "softplus_lo", T + 32, [P, 4, 512], F32R)
    k.ph = place(nc, "weights_of_keys_hi", T + 40, [P, 2, 512], F32R)
    k.pl = place(nc, "weights_of_keys_lo", T + 44, [P, 2, 512], F32R)
    k.logit = place(nc, "logits_then_weights", T + 48, [P, NLOGIT, 512], F32)
    k.ex = place(nc, "exps_then_softplus", T + 62, [P, NEX, 512], F32)
    k.vy = place(nc, "v_then_y", T + 68, [P, S], F32)
    k.sg = place(nc, "silu_gate", T + 72, [P, S], F32)
    T2 = T + 32
    k.pv = place(nc, "pool_v", T2, [P, S], F32)
    k.pa = place(nc, "window_a", T2 + 4, [P, S], F32)
    k.pb = place(nc, "window_b", T2 + 8, [P, S], F32)
    k.poh = place(nc, "pooled_hi", T2 + 12, [P, S], F32R)
    k.pol = place(nc, "pooled_lo", T2 + 16, [P, S], F32R)
    k.psg = place(nc, "pool_gate", T2 + 20, [P, S], F32)
    k.py = place(nc, "pool_y", T2 + 24, [P, S], F32)
    k.sig = place(nc, "merge_gate", T2 + 28, [P, 2, S], F32)
    k.prod = place(nc, "gated", T2 + 36, [P, S], F32)
    k.cg = place(nc, "conv_gate_c", T2, [P, S], F32)
    k.cz = place(nc, "conv_z", T2 + 4, [P, S], F32)
    k.cy = place(nc, "conv_y", T2 + 8, [P, S], F32)
    k.csg = place(nc, "conv_gate", T2 + 12, [P, S], F32)

    k.h2h = place(nc, "h2_hi", B, [P, DT, SC], F32R)
    k.h2l = place(nc, "h2_lo", B + 40, [P, DT, SC], F32R)
    k.ctx = place(nc, "context", 198, [P, DT, CTX], F32)
    k.cq = place(nc, "latent_q", 114, [P, 2, S], F32)
    k.ckv = place(nc, "latent_kv", 122, [P, 2, SC], F32)
    k.kpe = place(nc, "key_rotated", 148, [P, SC], F32)
    k.kpt = place(nc, "key_rotated_part", 153, [P, S], F32)
    k.lat_table = place(nc, "mla_table_early", 157, [P, S], F32)
    k.rk = place(nc, "ret_k", 114, [P, SC], F32)
    k.rv = place(nc, "ret_v", 119, [P, SC], F32)
    k.rq = place(nc, "ret_q", 124, [P, S], F32)
    k.rt = place(nc, "ret_rotated_part", 128, [P, S], F32)
    k.ro = place(nc, "ret_output", 132, [P, S], F32)
    k.rg = place(nc, "ret_gate", 136, [P, S], F32)
    k.rtab = place(nc, "ret_table", 140, [P, 2, S], F32)
    k.kz = [place(nc, f"ret_k_tokens_{d}", 148 + 5 * n, [P, NC + NCC, P], F32) for n, d in enumerate(("fwd", "bwd"))]
    k.rvt = place(nc, "ret_v_tokens", 158, [P, NC + NCC, P], F32)
    k.xq = [place(nc, f"ret_q_decayed_{d}", 163 + 4 * n, [P, S], F32) for n, d in enumerate(("fwd", "bwd"))]
    k.rsd = place(nc, "ret_scores_decayed", 171, [P, S], F32)
    k.st = [place(nc, f"ret_states_{d}", 175 + 4 * n, [P, NC, P], F32) for n, d in enumerate(("fwd", "bwd"))]
    k.cen = place(nc, "ret_centred", 183, [P, S], F32)
    k.csq = place(nc, "ret_centred_squares", 187, [P, S], F32)
    k.rroot = place(nc, "ret_root", 191, [P, S], F32)
    k.rout = place(nc, "ret_out", 198, [P, S], F32)
    k.dec = place(nc, "ret_decays", 202, [P, 5, P], F32)
    k.zeta = place(nc, "ret_zeta", 204.5, [P, 4], F32)
    k.lg = place(nc, "log_gamma", 204.6875, [P, 4 * RH], F32)
    k.cqn = [place(nc, f"latent_q_{p}", 34 + 8 * m, [P, 2, S], F32R) for m, p in enumerate(("hi", "lo"))]
    k.ckvn = [place(nc, f"latent_kv_{p}", 50 + 10 * m, [P, 2, SC], F32R) for m, p in enumerate(("hi", "lo"))]
    k.cqr = place(nc, "latent_q_back", 70, [P, 2, S], F32)
    k.ckvr = place(nc, "latent_kv_back", 78, [P, 2, SC], F32)
    k.mk = [[place(nc, f"mla_k{s}_{p}", (88, 103)[s] + 5 * m, [P, SC], F32R) for m, p in enumerate(("hi", "lo"))]
            for s in range(2)]
    k.kpr = place(nc, "key_rotated_back", 98, [P, SC], F32)
    k.mq = [[place(nc, f"mla_q{s}_{p}", (70, 124)[s] + (4, 8)[s] * m, [P, S], F32R) for m, p in enumerate(("hi", "lo"))]
            for s in range(2)]
    k.mvr = place(nc, "mla_v_raw", 78, [P, SC], F32)
    k.mqf = place(nc, "mla_q_f32", 83, [P, S], F32)
    k.mqt = place(nc, "mla_q_part", 98, [P, S], F32)
    k.mv = [place(nc, f"mla_v_{p}", 114 + 5 * m, [P, NC + NCC, P], F32R) for m, p in enumerate(("hi", "lo"))]
    k.mtab = place(nc, "mla_table", 128, [P, S], F32)
    k.pt = [place(nc, f"probs_turned_{p}", 138 + 20 * m, [P, 2, NC + NCC, 2 * P], F32R) for m, p in enumerate(("hi", "lo"))]
    k.probs = place(nc, "scores_then_probs", 183, [P, NPROBS, SC], F32)
    k.mo = place(nc, "mla_out", 198, [P, S], F32)
    k.stat = place(nc, "softmax_stats", 202, [P, 4, 16], F32)
    k.fh = place(nc, "ff_hi", B + 64, [P, 2, S], F32R)
    k.fl = place(nc, "ff_lo", B + 72, [P, 2, S], F32R)
    k.fa = place(nc, "ff_a", 162, [P, 2, S], F32)
    k.fg = place(nc, "ff_g", 170, [P, 2, S], F32)
    k.fs = place(nc, "ff_silu", 178, [P, S], F32)

    k.ps = ctx.enter_context(nc.psum_tensor("psum", [P, 8 * 512], F32))

    k.dve = nc.vector
    k.sems = {}

    def sem(name):
        if name not in k.sems:
            k.sems[name] = ctx.enter_context(nc.semaphore(name))
        return k.sems[name]
    k.sem = sem
    return k


def tile_bank(slot):
    return 1536 * slot


def one(t, i):
    return t[:, bass.ds(i, 1), :].rearrange("p a n -> p (a n)")


def f32(ap):
    return ap.bitcast(F32)


def three(pe, out, lhs, rhs, start, stop, loose=False, first=None):
    (lh, ll), (rh, rl) = lhs, rhs
    mm = pe.matmul(out, lh, rh, start=start, stop=False, skip_group_check=loose)
    if first is not None:
        mm.then_inc(first, 1)
    pe.matmul(out, lh, rl, start=False, stop=False, skip_group_check=loose)
    return pe.matmul(out, ll, rh, start=False, stop=stop, skip_group_check=loose)


def gemm_tile(k, pe, tile, unit, lhs, rhs, depth, width=S, new_unit=True, ready=None, by_chunk=False):
    if new_unit:
        pe.wait_ge(k.sem("weights_split"), unit.value(1))
    pe.wait_ge(k.sem(f"tile_read{tile.slot}"), tile.half(0))
    c0 = tile_bank(tile.slot)
    first = k.sem("unit_started") if new_unit else None
    chunks = [(c, min(512, width - c)) for c in range(0, width, 512)]
    if by_chunk:
        for n, (c, w) in enumerate(chunks):
            for i in range(depth):
                ready(i, n)
                mm = three(pe, k.ps[:, c0 + c:c0 + c + w], lhs(i), rhs(i, c, w), i == 0, i == depth - 1, first=first)
                first = None
        mm.then_inc(k.sem("tile_done"), 1)
        return
    for i in range(depth):
        if ready is not None:
            ready(i, 0)
        for c, w in chunks:
            (lh, ll), (rh, rl) = lhs(i), rhs(i, c, w)
            mm = pe.matmul(k.ps[:, c0 + c:c0 + c + w], lh, rh, start=i == 0, stop=False)
            if first is not None:
                mm.then_inc(first, 1)
                first = None
            pe.matmul(k.ps[:, c0 + c:c0 + c + w], lh, rl, start=False, stop=False)
        for c, w in chunks:
            (lh, ll), (rh, rl) = lhs(i), rhs(i, c, w)
            mm = pe.matmul(k.ps[:, c0 + c:c0 + c + w], ll, rh, start=False, stop=i == depth - 1)
    mm.then_inc(k.sem("tile_done"), 1)


def unit_block(k, slot, stride=P, base=0):
    return lambda i: (k.wh[:, slot, base + i * stride:base + i * stride + P],
                      k.wl[:, slot, base + i * stride:base + i * stride + P])


def act_of(h, l):
    return lambda i, c, w: (h[:, i, c:c + w], l[:, i, c:c + w])


def full_gemm(k, pe, tile, unit, **how):
    gemm_tile(k, pe, tile, unit, unit_block(k, unit.slot), act_of(k.hh, k.hl), DT, **how)


def ada_load(k, act, a, stage, i, j):
    s = ADA_STEP[stage]
    n = ADA * i + (ADA * s + j)
    act.wait_ge(k.sem("ada_used"), n + 1)
    src = a.w_ada[n] if isinstance(n, int) else a.w_ada[bass.ds(n, 1)].rearrange("a p n -> (a p) n")
    act.dma_start(k.adaw[:, :], src).then_inc(k.sem("ada_loaded"), 16)


def ada_sum(k, dve, stage, i, j):
    s = ADA_STEP[stage]
    n = ADA * i + (ADA * s + j)
    dve.wait_ge(k.sem("ada_loaded"), 16 * ADA * i + 16 * (ADA * s + j + 1))
    dve.wait_ge(k.sem("ada_done"), n + 1)
    for t in range(DT):
        if t:
            dve.wait_ge(k.sem("ada_term"), (DT - 1) * ADA * i + ((DT - 1) * (ADA * s + j) + t))
        for v in range(2):
            w, c, acc = k.adaw[:, P * t:P * t + P], k.scf[:, 2 * t + v:2 * t + v + 1], k.adas[:, v, :]
            ins = (dve.scalar_tensor_tensor(acc, w, c, acc, ALU.mult, ALU.add) if t else
                   dve.tensor_scalar(acc, w, c, None, ALU.mult))
            if v == 1:
                ins.then_inc(k.sem("ada_term" if t < DT - 1 else "ada_used"), 1)
            else:
                ins.then_inc(k.sem("ada_term_first"), 1)
                pending = DT * ADA * i + (DT * (ADA * s + j) + t + 1)
        dve.wait_ge(k.sem("ada_term_first"), pending)


def ada_product(k, pe, stage, i, j):
    s = ADA_STEP[stage]
    if j == 0:
        pe.wait_ge(k.sem("ada_read"), i + (s + 1))
    pe.wait_ge(k.sem("ada_used"), ADA * i + (ADA * s + j + 2))
    for v in range(2):
        mm = pe.matmul(k.ps[:, 3072 + 2 * j + v:3073 + 2 * j + v], k.adas[:, v, :], k.one32[:, 0:1],
                       start=True, stop=True)
    mm.then_inc(k.sem("ada_done"), 1)


def ada_store(k, dve, stage, i):
    s = ADA_STEP[stage]
    dve.wait_ge(k.sem("ada_done"), ADA * i + (ADA * s + ADA + 1))
    dve.tensor_copy(k.mod[:, bass.ds(ADA * i + ADA * s, ADA), :],
                    k.ps[:, 3072:3072 + 2 * ADA].rearrange("p (t n) -> p t n", n=2)).then_inc(k.sem("ada_read"), 1)


def bank(k, tile, width=S, c=0):
    b = tile_bank(tile.slot) + c
    return k.ps[:, b:b + width]


def wait_tile(k, eng, tile):
    eng.wait_ge(k.sem("tile_done"), tile.value(-1))


def read_tile(k, ins, tile):
    return ins.then_inc(k.sem(f"tile_read{tile.slot}"), 1)


def release_tile(k, eng, tile):
    ins = eng.memset(k.idle[:, 0:1], 0.0) if eng is k.dve else eng.activation(k.idle[:, 1:2], k.idle[:, 3:4], ACT.Copy)
    read_tile(k, ins, tile)


def at_stage(stage, what, i, j):
    first = (FIRST_UNIT if what == "unit" else FIRST_TILE)[stage]
    per = next(s[2 if what == "unit" else 3] for s in STAGES if s[0] == stage)
    return At(first + per * i + j) if isinstance(i, int) else At(first + j, per, i)



def load_unit(k, sp, s, src, split):
    if split is not None:
        sp.wait_ge(k.sem("weights_split"), split)
    sp.dma_start(k.raw[:, s, :], src).then_inc(k.sem(f"raw_loaded{s}"), 16)


def load_weights(k, sp, stream, first, last):
    def load(s, u, split):
        src = stream[u] if isinstance(u, int) else stream[bass.ds(u, 1)].rearrange("a p n -> (a p) n")
        load_unit(k, sp, s, src, split)
    while first < last and (first < 2 or first % 2):
        load(first % 2, first, first - 1 if first >= 2 else None)
        first += 1
    if last // 2 > first // 2:
        with sp.Fori(first // 2, last // 2) as r:
            for s in range(2):
                load(s, 2 * r + s, 2 * r + (s - 1))
    if last % 2 and last > first:
        load(0, last - 1, last - 2)


def split_unit(k, pool, s, loaded, ready, started):
    pool.wait_ge(k.sem(f"raw_loaded{s}"), loaded)
    if started is not None:
        pool.wait_ge(k.sem("unit_started"), started)
    pool.tensor_tensor(k.wh[:, s, :], k.raw[:, s, :], k.one32[:, 0:1].to_broadcast([P, UNIT]), ALU.mult
                       ).then_inc(k.sem("weights_hi"), 1)
    pool.wait_ge(k.sem("weights_hi"), ready)
    pool.tensor_tensor(k.wl[:, s, :], k.raw[:, s, :], f32(k.wh[:, s, :]), ALU.subtract
                       ).then_inc(k.sem("weights_split"), 1)


def split_weights(k, pool, first, last):
    if first % 2:
        split_unit(k, pool, 1, 16 * (first // 2) + 16, first + 1, first)
        first += 1
    with pool.Fori(first // 2, last // 2) as r:
        for s in range(2):
            split_unit(k, pool, s, 16 * r + 16, 2 * r + (s + 1), 2 * r + s)
    if last % 2:
        split_unit(k, pool, 0, 16 * (last // 2) + 16, last, last - 1)


def sb_gpsimd(k, pool):
    with pool.Fori(0, PAIRS) as i:
        for u in range(1, 5):
            split_unit(k, pool, u % 2, 32 * i + 16 * (u // 2 + 1), 4 * i + (u + 1), 4 * i + u)
        sb_pool(k, pool, i)



class Norms:

    def __init__(self):
        self.q, self.a, self.c = 0, 0, 0

    def pass_over(self, squares, firsts):
        self.q, self.a = self.q + squares, self.a + squares - firsts


def square_scalar(k, act, n, src, c0, w, first, behind=0):
    if first:
        if n.c > behind:
            act.wait_ge(k.sem("square_summed"), n.c - behind)
        dst = k.acc[:, c0:c0 + w]
    else:
        if n.a >= 2:
            act.wait_ge(k.sem("square_added"), n.a - 1)
        dst = k.sq[:, n.a % 2, :w]
        n.a += 1
    act.activation(dst, src, ACT.Square).then_inc(k.sem("square_done"), 1)
    n.q += 1


def square_add(k, eng, n, c0, w, first):
    n.q += 1
    if first:
        return
    eng.wait_ge(k.sem("square_done"), n.q)
    if n.a >= 1:
        eng.wait_ge(k.sem("square_added"), n.a)
    eng.tensor_tensor(k.acc[:, c0:c0 + w], k.acc[:, c0:c0 + w], k.sq[:, n.a % 2, :w], ALU.add
                      ).then_inc(k.sem("square_added"), 1)
    n.a += 1



def stat_bank(c):
    return 3072 + 512 * (c % 2)


def stat_sum_tensor(k, pe, n, chunks, squares=0, firsts=0):
    n.pass_over(squares, firsts)
    pe.wait_ge(k.sem("square_added"), n.a)
    for c, (c0, w) in enumerate(chunks, n.c):
        if c >= 2:
            pe.wait_ge(k.sem("stat_rstd"), c - 1)
        for m in range(w // P):
            mm = pe.matmul(k.ps[:, stat_bank(c) + m:stat_bank(c) + m + 1], k.acc[:, c0 + P * m:c0 + P * m + P],
                           k.one32[:, 0:1], start=True, stop=True)
        mm.then_inc(k.sem("square_summed"), 1)


def stat_spread_tensor(k, pe, n, chunks):
    for _, w in chunks:
        pe.wait_ge(k.sem("stat_diagonal"), n.c + 1)
        pe.matmul(k.ps[:, stat_bank(n.c):stat_bank(n.c) + w], k.one32[:, :], k.diag[:, n.c % 2, :w], start=True,
                  stop=True).then_inc(k.sem("stat_spread"), 1)
        n.c += 1


def stat_root_scalar(k, act, n, chunks, features):
    for c, (_, w) in enumerate(chunks, n.c):
        act.wait_ge(k.sem("square_summed"), c + 1)
        act.activation(k.root[:, c % 2, :w // P], k.ps[:, stat_bank(c):stat_bank(c) + w // P], ACT.Sqrt,
                       bias=EPS, scale=1.0 / features).then_inc(k.sem("stat_root"), 1)


def stat_copy_scalar(k, act, n, chunks):
    for c0, w in chunks:
        act.wait_ge(k.sem("stat_spread"), n.c + 1)
        act.activation(k.rstd[:, c0:c0 + w], k.ps[:, stat_bank(n.c):stat_bank(n.c) + w], ACT.Copy
                       ).then_inc(k.sem("stat_rstd"), 1)
        n.c += 1


def stat_vector(k, dve, n, chunks):
    ident = k.const[:, CONSTS["ident"]:CONSTS["ident"] + P].rearrange("p (a n) -> p a n", a=1)
    for _, w in chunks:
        s, m = n.c % 2, w // P
        n.c += 1
        dve.wait_ge(k.sem("stat_root"), n.c)
        dve.reciprocal(k.root[:, 2 + s, :m], k.root[:, s, :m]).then_inc(k.sem("stat_inverse"), 1)
        dve.wait_ge(k.sem("stat_inverse"), n.c)
        if n.c > 2:
            dve.wait_ge(k.sem("stat_spread"), n.c - 2)
        dve.tensor_tensor(k.diag[:, s, :w].rearrange("p (a n) -> p a n", n=P), ident.to_broadcast([P, m, P]),
                          k.root[:, 2 + s, :m].rearrange("p (a n) -> p a n", n=1).to_broadcast([P, m, P]), ALU.mult
                          ).then_inc(k.sem("stat_diagonal"), 1)


def rstd_ready(k, dve, count):
    dve.wait_ge(k.sem("stat_rstd"), count)


HALVES = [(0, 512), (512, 512)]


class Applies:

    def __init__(self):
        self.n, self.biased = 0, 0


def apply_vector(k, dve, ap, src, gain, c0, w=512):
    if ap.n >= NORMED:
        dve.wait_ge(k.sem("normed_split"), ap.n - NORMED + 1)
    dve.scalar_tensor_tensor(k.nt[:, ap.n % NORMED, :w], src, gain, k.rstd[:, c0:c0 + w], ALU.mult, ALU.mult
                             ).then_inc(k.sem("normed"), 1)
    ap.n += 1


def apply_scalar(k, act, ap, hi, bias=None, w=512):
    t = k.nt[:, ap.n % NORMED, :w]
    ap.n += 1
    act.wait_ge(k.sem("normed"), ap.n)
    if bias is not None:
        ap.biased += 1
        act.activation(t, t, ACT.Identity, bias=bias).then_inc(k.sem("normed_biased"), 1)
        act.wait_ge(k.sem("normed_biased"), ap.biased)
    act.activation(hi, t, ACT.Copy).then_inc(k.sem("normed_hi"), 1)


def apply_low(k, pool, ap, hi, lo, w=512):
    t = k.nt[:, ap.n % NORMED, :w]
    ap.n += 1
    pool.wait_ge(k.sem("normed_hi"), ap.n)
    pool.tensor_tensor(lo, t, f32(hi), ALU.subtract).then_inc(k.sem("normed_split"), 1)



LAG_CUM, LAG_OUT = 3, 7


def sb_tensor(k, pe):
    def h_ready(t, c):
        pe.wait_ge(k.sem("normed_split"), DT * c + t + 1)
    with pe.Fori(0, PAIRS) as i:
        for j in range(4):
            full_gemm(k, pe, at_stage("sb", "tile", i, j), at_stage("sb", "unit", i, j),
                      ready=None if j else h_ready, by_chunk=j == 0)
        v = at_stage("sb", "tile", i, 2)
        pe.wait_ge(k.sem("start_ready"), 1)
        pe.wait_ge(k.sem(f"tile_read{v.slot}"), v.half(1))
        for t in range(NC):
            mm = pe.transpose(k.ps[:, 3072 + P * t:3072 + P * t + P], k.vy[:, P * t:P * t + P],
                              k.const[:, CONSTS["ident"]:CONSTS["ident"] + P])
        mm.then_inc(k.sem("sb_v_turned"), 1)
        for slot in range(2):
            last = at_stage("sb", "tile", i, 2 + slot)
            pe.wait_ge(k.sem(f"tile_read{last.slot}"), last.half(1))
        pe.wait_ge(k.sem("sb_v_split"), i + 1)
        for step in range(NB + LAG_OUT):
            n = step
            if n < NB:
                qc, kb, a, off = BLOCKS[n]
                if n >= 4:
                    pe.wait_ge(k.sem("sb_logits_read"), NB * i + (n - 3))
                b = (0, 512, 1536, 2048)[n % 4]
                r = slice(HD * a, HD * a + HD)
                q = slice(512 * qc + off, 512 * qc + 512)
                three(pe, k.ps[:, b + off:b + 512],
                      (k.kh[r, P * kb:P * kb + P], k.kl[r, P * kb:P * kb + P]), (k.qh[r, q], k.ql[r, q]),
                      True, True).then_inc(k.sem("sb_logits"), 1)
            n = step - LAG_CUM
            if 0 <= n < NB:
                qc, kb, a, off = BLOCKS[n]
                b = 3072 + 512 * a
                head = kb == 4 * qc + 3
                if not head:
                    o = BLOCKS[n - 2][3]
                    pe.wait_ge(k.sem("sb_sums_read"), NB * i + (n - 1))
                    for m in (k.sph, k.spl):
                        pe.matmul(k.ps[:, b + o:b + 512], k.tri[:, P:2 * P], m[:, (n - 2) % 4, o:512],
                                  start=False, stop=False, skip_group_check=True)
                elif n >= 2:
                    pe.wait_ge(k.sem("sb_sums_read"), NB * i + (n - 1))
                pe.wait_ge(k.sem("sb_softplus"), NB * i + (n + 1))
                pe.matmul(k.ps[:, b + off:b + 512], k.tri[:, 0:P], k.sph[:, n % 4, off:512],
                          start=head, stop=False, skip_group_check=True)
                pe.matmul(k.ps[:, b + off:b + 512], k.tri[:, 0:P], k.spl[:, n % 4, off:512],
                          start=False, stop=True, skip_group_check=True).then_inc(k.sem("sb_sums"), 1)
            n = step - LAG_OUT
            if n >= 0:
                qc, kb, a, off = BLOCKS[n]
                b = (1024, 2560)[a]
                if kb == 4 * qc + 3 and qc:
                    pe.wait_ge(k.sem("sb_out_read"), 4 * i + (a + 1))
                pe.wait_ge(k.sem("sb_weights"), NB * i + (n + 1))
                three(pe, k.ps[:, b + off:b + 512], (k.vh[:, kb, :], k.vl[:, kb, :]),
                      (k.ph[:, n % 2, off:512], k.pl[:, n % 2, off:512]),
                      kb == 4 * qc + 3, kb == 0, loose=True).then_inc(k.sem("sb_out"), 1)
        pe.wait_ge(k.sem("sb_sums_read"), NB * i + NB)
        pe.wait_ge(k.sem("sb_out_read"), 4 * i + 4)
        pe.wait_ge(k.sem("sb_logits_read"), NB * i + NB)


def sb_scalar(k, act):
    with act.Fori(0, PAIRS) as i:
        def tile(j):
            t = at_stage("sb", "tile", i, j)
            wait_tile(k, act, t)
            return bank(k, t)
        act.activation(k.qh[:, :], tile(0), ACT.Copy, scale=HD ** -0.5).then_inc(k.sem("sb_qk_hi"), 1)
        act.activation(k.kh[:, :], tile(1), ACT.Copy).then_inc(k.sem("sb_qk_hi"), 1)
        read_tile(k, act.activation(k.vy[:, :], tile(2), ACT.Copy), at_stage("sb", "tile", i, 2))
        read_tile(k, act.activation(k.sg[:, :], tile(3), ACT.Silu), at_stage("sb", "tile", i, 3))
        act.preload_act_table_set("natural_log_exp_and_others")
        act.wait_ge(k.sem("sb_v_turned"), i + 1)
        act.activation(k.vh[:, :, :], k.ps[:, 3072:4096].rearrange("p (t n) -> p t n", t=NC), ACT.Copy).then_inc(k.sem("sb_v_hi"), 1)
        for step in range(NB + 6):
            n = step
            if n < NB:
                off = BLOCKS[n][3]
                act.wait_ge(k.sem("sb_logits"), NB * i + (n + 1))
                if n >= NLOGIT:
                    act.wait_ge(k.sem("sb_weights"), NB * i + (n - NLOGIT + 1))
                b = (0, 512, 1536, 2048)[n % 4]
                act.activation(k.logit[:, n % NLOGIT, off:512], k.ps[:, b + off:b + 512], ACT.Copy
                               ).then_inc(k.sem("sb_logits_read"), 1)
            n = step - 1
            if 0 <= n < NB:
                off = BLOCKS[n][3]
                act.wait_ge(k.sem("sb_clamped"), NB * i + (n + 1))
                act.activation(k.ex[:, n % NEX, off:512], k.ex[:, n % NEX, off:512], ACT.Exp).then_inc(k.sem("sb_exp"), 1)
            m = step - 5
            if 0 <= m < NB:
                mo = BLOCKS[m][3]
                act.wait_ge(k.sem("sb_sums_read"), NB * i + (m + 1))
                act.activation(k.logit[:, m % NLOGIT, mo:512], k.logit[:, m % NLOGIT, mo:512], ACT.Exp).then_inc(k.sem("sb_weight"), 1)
            if 0 <= n < NB:
                act.wait_ge(k.sem("sb_exp"), NB * i + (n + 1))
                act.activation(k.ex[:, n % NEX, off:512], k.ex[:, n % NEX, off:512], ACT.Ln, bias=1.0
                               ).then_inc(k.sem("sb_log"), 1)
            if 0 <= m < NB:
                act.wait_ge(k.sem("sb_weight"), NB * i + (m + 1))
                if m >= 2:
                    act.wait_ge(k.sem("sb_out"), NB * i + (m - 1))
                act.activation(k.ph[:, m % 2, mo:512], k.logit[:, m % NLOGIT, mo:512], ACT.Copy).then_inc(k.sem("sb_weight_hi"), 1)
        act.wait_ge(k.sem("sb_out_read"), 4 * i + 4)
        act.activation(one(k.yh, i), k.vy[:, :], ACT.Copy).then_inc(k.sem("sb_y_hi"), 1)


def sb_pool(k, pool, i):
    for step in range(2, NB + 6):
        n = step - 6
        if n >= 0:
            off = BLOCKS[n][3]
            pool.wait_ge(k.sem("sb_weight_hi"), NB * i + (n + 1))
            pool.tensor_tensor(k.pl[:, n % 2, off:512], k.logit[:, n % NLOGIT, off:512],
                               f32(k.ph[:, n % 2, off:512]), ALU.subtract).then_inc(k.sem("sb_weights"), 1)
        n = step - 2
        if n < NB:
            off = BLOCKS[n][3]
            pool.wait_ge(k.sem("sb_softplus_hi"), NB * i + (n + 1))
            pool.tensor_tensor(k.spl[:, n % 4, off:512], k.ex[:, n % NEX, off:512],
                               f32(k.sph[:, n % 4, off:512]), ALU.subtract).then_inc(k.sem("sb_softplus"), 1)


def sb_vector(k, dve):
    col = CONSTS
    mask, mneg = k.const[:, col["mask"]:col["mask"] + P], k.const[:, col["mneg"]:col["mneg"] + P]
    with dve.Fori(0, PAIRS) as i:
        for j, (hi, lo, scale) in enumerate(((k.qh, k.ql, HD ** -0.5), (k.kh, k.kl, 1.0))):
            t = at_stage("sb", "tile", i, j)
            dve.wait_ge(k.sem("sb_qk_hi"), 2 * i + (j + 1))
            read_tile(k, dve.scalar_tensor_tensor(lo[:, :], bank(k, t), scale, f32(hi[:, :]), ALU.mult,
                                                  ALU.subtract), t)
        dve.wait_ge(k.sem("sb_v_hi"), i + 1)
        dve.tensor_tensor(k.vl[:, :, :], k.ps[:, 3072:4096].rearrange("p (t n) -> p t n", t=NC),
                          f32(k.vh[:, :, :]), ALU.subtract).then_inc(k.sem("sb_v_split"), 1)
        for step in range(NB + LAG_OUT):
            n = step - 2
            if 0 <= n < NB:
                off = BLOCKS[n][3]
                dve.wait_ge(k.sem("sb_log"), NB * i + (n + 1))
                dve.tensor_tensor(k.ex[:, n % NEX, off:512], k.logit[:, n % NLOGIT, off:512], k.ex[:, n % NEX, off:512], ALU.max
                                  ).then_inc(k.sem("sb_max"), 1)
            n = step - 1
            if 0 <= n < NB:
                off = BLOCKS[n][3]
                dve.wait_ge(k.sem("sb_logits_read"), NB * i + (n + 1))
                if n >= NEX:
                    dve.wait_ge(k.sem("sb_softplus"), NB * i + (n - NEX + 1))
                dve.tensor_scalar(k.ex[:, n % NEX, off:512], k.logit[:, n % NLOGIT, off:512], CLAMP, None, ALU.min
                                  ).then_inc(k.sem("sb_clamped"), 1)
            n = step - 2
            if 0 <= n < NB:
                qc, kb, a, off = BLOCKS[n]
                dve.wait_ge(k.sem("sb_max"), NB * i + (n + 1))
                d = slice(off, off + P)
                if kb >= 4 * qc:
                    dve.tensor_tensor(k.ex[:, n % NEX, d], k.ex[:, n % NEX, d], mask, ALU.mult).then_inc(k.sem("sb_masked"), 1)
                    dve.wait_ge(k.sem("sb_masked"), 16 * i + (1 + sum(b[1] >= 4 * b[0] for b in BLOCKS[:n])))
                if n >= 4:
                    dve.wait_ge(k.sem("sb_sums"), NB * i + (n - 1))
                dve.tensor_copy(k.sph[:, n % 4, off:512], k.ex[:, n % NEX, off:512]).then_inc(k.sem("sb_softplus_hi"), 1)
            m = step - 4
            if 0 <= m < NB:
                mqc, mkb, ma, moff = BLOCKS[m]
                b = 3072 + 512 * ma
                dve.wait_ge(k.sem("sb_sums"), NB * i + (m + 1))
                dve.tensor_tensor(k.logit[:, m % NLOGIT, moff:512], k.logit[:, m % NLOGIT, moff:512], k.ps[:, b + moff:b + 512],
                                  ALU.subtract).then_inc(k.sem("sb_sub" if mkb >= 4 * mqc else "sb_sums_read"), 1)
            if 0 <= m < NB and mkb >= 4 * mqc:
                d = slice(moff, moff + P)
                dve.wait_ge(k.sem("sb_sub"), 16 * i + (1 + sum(b[1] >= 4 * b[0] for b in BLOCKS[:m])))
                dve.tensor_tensor(k.logit[:, m % NLOGIT, d], k.logit[:, m % NLOGIT, d], mneg, ALU.min
                                  ).then_inc(k.sem("sb_sums_read"), 1)
            n = step - LAG_OUT
            if n >= 0 and BLOCKS[n][1] == 0:
                qc, kb, a, off = BLOCKS[n]
                b, r, q = (1024, 2560)[a], slice(HD * a, HD * a + HD), slice(512 * qc, 512 * qc + 512)
                g = at_stage("sb", "tile", i, 3)
                dve.wait_ge(k.sem(f"tile_read{g.slot}"), g.half(1))
                dve.wait_ge(k.sem("sb_out"), NB * i + (n + 1))
                dve.tensor_tensor(k.vy[r, q], k.sg[r, q], k.ps[r, b:b + 512], ALU.mult
                                  ).then_inc(k.sem("sb_out_read"), 1)
        dve.wait_ge(k.sem("sb_weights"), NB * i + NB)
        dve.wait_ge(k.sem("sb_softplus"), NB * i + NB)
        dve.wait_ge(k.sem("sb_y_hi"), i + 1)
        dve.tensor_tensor(one(k.yl, i), k.vy[:, :], f32(one(k.yh, i)), ALU.subtract
                          ).then_inc(k.sem("branch_split"), 1)



def loads_scalar(k, act, a):
    for c in range(NCH):
        s = slice(512 * c, 512 * c + 512)
        for h in range(2):
            act.dma_start(k.x[:, 4 * h:4 * h + 4, s], a.x[:, 4 * h:4 * h + 4, s]).then_inc(k.sem(f"x_loaded{c}{h}"), 16)
        if c == 0:
            act.dma_start(k.params[:, :], a.params).then_inc(k.sem("params_loaded"), 16)
            act.dma_start(k.const[:, :], a.consts).then_inc(k.sem("const_loaded"), 16)


def start_scalar(k, act, n, ap):
    def square(c, i):
        act.wait_ge(k.sem(f"x_loaded{c}{i // 4}"), 16)
        square_scalar(k, act, n, k.x[:, i, 512 * c:512 * c + 512], *HALVES[c], i == 0, behind=c)
    for i in range(DT):
        square(0, i)
    stat_root_scalar(k, act, n, HALVES[:1], D)
    stat_copy_scalar(k, act, n, HALVES[:1])
    for i in range(DT):
        square(1, i)
        apply_scalar(k, act, ap, k.hh[:, i, 0:512])
    stat_root_scalar(k, act, n, HALVES[1:], D)
    stat_copy_scalar(k, act, n, HALVES[1:])
    for i in range(DT):
        apply_scalar(k, act, ap, k.hh[:, i, 512:S])
    act.wait_ge(k.sem("params_loaded"), 16)
    act.activation(k.scf[:, :], k.params[:, PARAMS["c"]:PARAMS["c"] + 2 * DT], ACT.Silu).then_inc(k.sem("silu_c"), 1)
    act.wait_ge(k.sem("const_loaded"), 16)
    act.activation(k.tri[:, :], k.const[:, CONSTS["tri"]:CONSTS["tri"] + 2 * P], ACT.Copy).then_inc(k.sem("start_ready"), 1)


def start_vector(k, dve, n, ap):
    dve.memset(k.one32[:, :], 1.0).then_inc(k.sem("one32"), 1)
    for s in range(2):
        dve.memset(k.idle[:, s:s + 1], 0.0).then_inc(k.sem(f"tile_read{s}"), 1)
    for s, (name, free) in enumerate((("ada_used", 1), ("ada_done", 1), ("ada_read", 1), ("ret_stored", 1), ("mla_stored", 1),
                                      ("mla_out_read", 2)), 3):
        dve.memset(k.idle[:, s:s + 1], 0.0).then_inc(k.sem(name), free)


    dve.wait_ge(k.sem("params_loaded"), 16)
    def apply(c, i):
        dve.wait_ge(k.sem(f"x_loaded{c}{i // 4}"), 16)
        apply_vector(k, dve, ap, k.x[:, i, 512 * c:512 * c + 512], col(k, "pre_g", i), *HALVES[c])
    for i in range(DT):
        square_add(k, dve, n, *HALVES[0], i == 0)
    dve.wait_ge(k.sem("const_loaded"), 16)
    stat_vector(k, dve, n, HALVES[:1])
    rstd_ready(k, dve, n.c)
    for i in range(DT):
        apply(0, i)
        square_add(k, dve, n, *HALVES[1], i == 0)
    stat_vector(k, dve, n, HALVES[1:])
    rstd_ready(k, dve, n.c)
    for i in range(DT):
        apply(1, i)
    dve.wait_ge(k.sem("normed"), ap.n)


def start_tensor(k, pe, n):
    pe.wait_ge(k.sem("one32"), 1)
    for chunk in HALVES:
        stat_sum_tensor(k, pe, n, [chunk], DT, 1)
        stat_spread_tensor(k, pe, n, [chunk])


def low_parts(k, pool, ap, hi, lo):
    for c in range(NCH):
        s = slice(512 * c, 512 * c + 512)
        for i in range(DT):
            apply_low(k, pool, ap, hi[:, i, s], lo[:, i, s])


def col(k, name, i=0):
    return k.params[:, PARAMS[name] + i:PARAMS[name] + i + 1]



def merge_tensor(k, pe, stage, b):
    with pe.Fori(0, 2) as i:
        for h in range(2):
            for j in range(2):
                full_gemm(k, pe, at_stage(stage, "tile", i, 4 * h + j), at_stage(stage, "unit", i, 3 * h + j))
                ada_product(k, pe, stage, i, 2 * h + j)
            pe.wait_ge(k.sem("branch_split"), BT * (b + 1))
            for j in range(2):
                u = at_stage(stage, "unit", i, 3 * h + 2)
                gemm_tile(k, pe, at_stage(stage, "tile", i, 4 * h + 2 + j), u,
                          unit_block(k, u.slot, 2 * P, P * j), act_of(k.yh, k.yl), BT, new_unit=j == 0)


def merge_scalar(k, act, a, stage, b):
    with act.Fori(0, 2) as i:
        for h in range(2):
            for j in range(2):
                ada_load(k, act, a, stage, i, 2 * h + j)
                t = at_stage(stage, "tile", i, 4 * h + j)
                wait_tile(k, act, t)
                read_tile(k, act.activation(k.sig[:, j, :], bank(k, t), ACT.Sigmoid), t)


def merge_vector(k, dve, stage, b):
    with dve.Fori(0, 2) as i:
        for h in range(2):
            for j in range(2):
                ada_sum(k, dve, stage, i, 2 * h + j)
            for j in range(2):
                n = 2 * h + j
                g, t = at_stage(stage, "tile", i, 4 * h + j), at_stage(stage, "tile", i, 4 * h + 2 + j)
                dve.wait_ge(k.sem(f"tile_read{g.slot}"), g.half(1))
                wait_tile(k, dve, t)
                acc = one(k.merged, 4 * i + n)
                if b == 0:
                    read_tile(k, dve.tensor_tensor(acc, k.sig[:, j, :], bank(k, t), ALU.mult), t)
                else:
                    read_tile(k, dve.tensor_tensor(k.prod[:, :], k.sig[:, j, :], bank(k, t), ALU.mult), t)
                    dve.wait_ge(k.sem(f"tile_read{t.slot}"), t.half(1))
                    dve.tensor_tensor(acc, acc, k.prod[:, :], ALU.add).then_inc(k.sem("merged_sum"), 1)
                    dve.wait_ge(k.sem("merged_sum"), 8 * (b - 1) + 4 * i + (n + 1))
        ada_store(k, dve, stage, i)



def pool_tensor(k, pe):
    with pe.Fori(0, 2) as i:
        for h in range(2):
            for j in range(2):
                full_gemm(k, pe, at_stage("pool", "tile", i, 3 * h + j), at_stage("pool", "unit", i, 3 * h + j))
                if j == 0:
                    ada_product(k, pe, "pool", i, 2 * h)
            pe.wait_ge(k.sem("pooled_split"), 2 * i + (h + 1))
            u = at_stage("pool", "unit", i, 3 * h + 2)
            gemm_tile(k, pe, at_stage("pool", "tile", i, 3 * h + 2), u, unit_block(k, u.slot),
                      lambda _, c, w: (k.poh[:, c:c + w], k.pol[:, c:c + w]), 1)
            ada_product(k, pe, "pool", i, 2 * h + 1)


def pool_scalar(k, act, a):
    for g in range(BT):
        ada_load(k, act, a, "pool", g // 2, 2 * (g % 2))
        t = at_stage("pool", "tile", g // 2, 3 * (g % 2))
        wait_tile(k, act, t)
        read_tile(k, act.activation(k.pv[:, :], bank(k, t), ACT.Copy), t)
        ada_load(k, act, a, "pool", g // 2, 2 * (g % 2) + 1)
        t = at_stage("pool", "tile", g // 2, 3 * (g % 2) + 1)
        wait_tile(k, act, t)
        read_tile(k, act.activation(k.psg[:, :], bank(k, t), ACT.Silu), t)
        act.wait_ge(k.sem("pooled"), g + 1)
        act.activation(k.poh[:, :], k.pa[:, :], ACT.Copy).then_inc(k.sem("pooled_hi"), 1)
        t = at_stage("pool", "tile", g // 2, 3 * (g % 2) + 2)
        act.wait_ge(k.sem(f"tile_read{t.slot}"), t.half(1))
        act.activation(k.yh[:, g, :], k.py[:, :], ACT.Copy).then_inc(k.sem("pool_y_hi"), 1)


def pool_vector(k, dve, ch):
    for g, w in enumerate(POOL_WINDOWS):
        ada_sum(k, dve, "pool", g // 2, 2 * (g % 2))
        t = at_stage("pool", "tile", g // 2, 3 * (g % 2))
        dve.wait_ge(k.sem(f"tile_read{t.slot}"), t.half(1))
        src, bufs, d = k.pv, [k.pa, k.pb], 1
        if (w.bit_length() - 1) % 2 == 0:
            bufs = [k.pb, k.pa]
        while d < w:
            dst = bufs[0]
            ch(dve.tensor_copy(dst[:, 0:d], src[:, 0:d]))
            ch(dve.tensor_tensor(dst[:, d:], src[:, d:], src[:, :S - d], ALU.add))
            src, bufs, d = dst, bufs[::-1], 2 * d
        n = CONSTS["cnt"] + 16 * g
        ch(dve.tensor_tensor(k.pa[:, 0:16], k.pa[:, 0:16], k.const[:, n:n + 16], ALU.mult))
        dve.scalar_tensor_tensor(k.pa[:, :], k.pa[:, :], 1.0 / w, k.pv[:, :], ALU.mult, ALU.subtract
                                 ).then_inc(k.sem("pooled"), 1)
        dve.wait_ge(k.sem("pooled_hi"), g + 1)
        dve.tensor_tensor(k.pol[:, :], k.pa[:, :], f32(k.poh[:, :]), ALU.subtract).then_inc(k.sem("pooled_split"), 1)
        dve.wait_ge(k.sem("pooled_split"), g + 1)
        ada_sum(k, dve, "pool", g // 2, 2 * (g % 2) + 1)
        t = at_stage("pool", "tile", g // 2, 3 * (g % 2) + 1)
        dve.wait_ge(k.sem(f"tile_read{t.slot}"), t.half(1))
        t = at_stage("pool", "tile", g // 2, 3 * (g % 2) + 2)
        wait_tile(k, dve, t)
        read_tile(k, dve.scalar_tensor_tensor(k.py[:, :], bank(k, t), col(k, "pool_scale", g), k.psg[:, :],
                                              ALU.mult, ALU.mult), t)
        dve.wait_ge(k.sem("pool_y_hi"), g + 1)
        dve.tensor_tensor(k.yl[:, g, :], k.py[:, :], f32(k.yh[:, g, :]), ALU.subtract).then_inc(k.sem("branch_split"), 1)
        if g % 2:
            ada_store(k, dve, "pool", g // 2)



def conv_tensor(k, pe):
    with pe.Fori(0, BT) as i:
        for j in range(4):
            full_gemm(k, pe, at_stage("conv", "tile", i, j), at_stage("conv", "unit", i, j))
            ada_product(k, pe, "conv", i, j)


def conv_scalar(k, act, a):
    with act.Fori(0, BT) as i:
        ada_load(k, act, a, "conv", i, 0)
        t = at_stage("conv", "tile", i, 0)
        wait_tile(k, act, t)
        read_tile(k, act.activation(k.cg[:, :], bank(k, t), ACT.Copy), t)
        for j in (1, 2, 3):
            ada_load(k, act, a, "conv", i, j)
        t = at_stage("conv", "tile", i, 3)
        wait_tile(k, act, t)
        read_tile(k, act.activation(k.csg[:, :], bank(k, t), ACT.Silu), t)
        act.wait_ge(k.sem("conv_y"), i + 1)
        act.activation(one(k.yh, i), k.cy[:, :], ACT.Copy).then_inc(k.sem("conv_y_hi"), 1)


def conv_vector(k, dve, ch):
    def param(i, j):
        return k.params[:, bass.ds(4 * i + (PARAMS["conv"] + j), 1)]
    with dve.Fori(0, BT) as i, ch.body(i, 3, BT):
        ada_sum(k, dve, "conv", i, 0)
        t = at_stage("conv", "tile", i, 0)
        dve.wait_ge(k.sem(f"tile_read{t.slot}"), t.half(1))
        ada_sum(k, dve, "conv", i, 1)
        t = at_stage("conv", "tile", i, 1)
        wait_tile(k, dve, t)
        read_tile(k, dve.tensor_tensor(k.cz[:, :], k.cg[:, :], bank(k, t), ALU.mult), t)
        dve.wait_ge(k.sem(f"tile_read{t.slot}"), t.half(1))
        ch(dve.tensor_scalar(k.cy[:, :], k.cz[:, :], param(i, 2), param(i, 3), ALU.mult, ALU.add))
        for j in range(2):
            d = 2 - j
            ch(dve.scalar_tensor_tensor(k.cy[:, d:], k.cz[:, :S - d], param(i, j), k.cy[:, d:], ALU.mult, ALU.add))
        ada_sum(k, dve, "conv", i, 2)
        t = at_stage("conv", "tile", i, 2)
        wait_tile(k, dve, t)
        read_tile(k, dve.tensor_tensor(k.cy[:, :], k.cy[:, :], bank(k, t), ALU.mult), t)
        dve.wait_ge(k.sem(f"tile_read{t.slot}"), t.half(1))
        ada_sum(k, dve, "conv", i, 3)
        t = at_stage("conv", "tile", i, 3)
        dve.wait_ge(k.sem(f"tile_read{t.slot}"), t.half(1))
        dve.tensor_tensor(k.cy[:, :], k.cy[:, :], k.csg[:, :], ALU.mult).then_inc(k.sem("conv_y"), 1)
        dve.wait_ge(k.sem("conv_y_hi"), i + 1)
        dve.tensor_tensor(one(k.yl, i), k.cy[:, :], f32(one(k.yh, i)), ALU.subtract).then_inc(k.sem("branch_split"), 1)
        ada_store(k, dve, "conv", i)



def out1_tensor(k, pe, n):
    def ready(i, _):
        pe.wait_ge(k.sem("merged_split"), i + 1)
    for j in range(DT):
        full_gemm(k, pe, at_stage("out1", "tile", 0, j), at_stage("out1", "unit", 0, j), ready=None if j else ready)
        if j == CTX_AFTER:
            stat_sum_tensor(k, pe, n, [(S, CTX)], CTX_AFTER + DT, 2)
        if j == CTX_AFTER + 1:
            stat_spread_tensor(k, pe, n, [(S, CTX)])


CTX_AFTER = 4


def out1_scalar(k, act, a, n):
    t = at_stage("out1", "tile", 0, 0)
    wait_tile(k, act, t.plus(-1))
    act.wait_ge(k.sem("merged_sum"), 2 * DT)
    for i in range(DT):
        act.activation(k.hh[:, i, :], k.merged[:, i, :], ACT.Copy).then_inc(k.sem("merged_hi"), 1)
    act.wait_ge(k.sem("ada_used"), 6 * DT + 1)
    act.dma_start(k.ctx[:, :, :], a.ctx).then_inc(k.sem("ctx_loaded"), 16)
    act.wait_ge(k.sem("merged_split"), DT)
    for c in range(NCH):
        act.dma_start(k.x[:, :, 512 * c:512 * c + 512], a.x[:, :, 512 * c:512 * c + 512]
                      ).then_inc(k.sem(f"x_back{c}"), 16)
    for j in range(DT):
        t = at_stage("out1", "tile", 0, j)
        wait_tile(k, act, t)
        read_tile(k, act.activation(k.outr[:, j, :], bank(k, t), ACT.Copy), t)
        act.wait_ge(k.sem(f"tile_read{t.slot}"), t.half(1))
        square_scalar(k, act, n, k.outr[:, j, :], 0, S, j == 0)
        if j == CTX_AFTER - 1:
            act.wait_ge(k.sem("ctx_loaded"), 16)
            for i in range(DT):
                square_scalar(k, act, n, k.ctx[:, i, :], S, CTX, i == 0)
        if j == CTX_AFTER:
            stat_root_scalar(k, act, n, [(S, CTX)], D)
        if j == CTX_AFTER + 1:
            stat_copy_scalar(k, act, n, [(S, CTX)])
    for i in range(DT):
        act.wait_ge(k.sem("ctx_normed"), i + 1)
        act.activation(k.ctx[:, i, :], k.ctx[:, i, :], ACT.Identity, bias=k.mod[:, i, 1:2]).then_inc(k.sem("ctx_biased"), 1)


def out1_vector(k, dve, n, ch):
    for i in range(DT):
        dve.wait_ge(k.sem("merged_hi"), i + 1)
        dve.tensor_tensor(k.hl[:, i, :], k.merged[:, i, :], f32(k.hh[:, i, :]), ALU.subtract
                          ).then_inc(k.sem("merged_split"), 1)
    dve.wait_ge(k.sem("ada_read"), 6 * DT // ADA + 1)
    for v in range(2):
        ch(dve.tensor_tensor(k.mod[:, :, v], k.mod[:, :, v],
                             k.params[:, PARAMS["b_ada"]:PARAMS["b_ada"] + 6 * DT], ALU.add))
    for j, (first, v, g) in enumerate(((DT, 0, "g1"), (DT, 1, "g1"), (4 * DT, 0, "g2"))):
        ch(dve.scalar_tensor_tensor(k.gm[:, DT * j:DT * j + DT], k.mod[:, first:first + DT, v], 1.0,
                                    k.params[:, PARAMS[g]:PARAMS[g] + DT], ALU.add, ALU.mult))
    for j in range(DT):
        square_add(k, dve, n, 0, S, j == 0)
        if j == CTX_AFTER - 1:
            for i in range(DT):
                square_add(k, dve, n, S, CTX, i == 0)
        if j == CTX_AFTER:
            stat_vector(k, dve, n, [(S, CTX)])
        if j == CTX_AFTER + 1:
            rstd_ready(k, dve, n.c)
            for i in range(DT):
                dve.scalar_tensor_tensor(k.ctx[:, i, :], k.ctx[:, i, :], k.gm[:, DT + i:DT + i + 1], k.rstd[:, S:SC],
                                         ALU.mult, ALU.mult).then_inc(k.sem("ctx_normed"), 1)



def enter_scalar(k, act, a, n, ap):
    c0, c1 = HALVES
    stat_root_scalar(k, act, n, HALVES, D)
    stat_copy_scalar(k, act, n, HALVES)

    def squares(c, tiles):
        for i in tiles:
            act.wait_ge(k.sem("x1_done"), DT * c + i + 1)
            square_scalar(k, act, n, k.x[:, i, 512 * c:512 * c + 512], *HALVES[c], i == 0, behind=c)

    def apply(c, tiles):
        for i in tiles:
            apply_scalar(k, act, ap, k.h2h[:, i, 512 * c:512 * c + 512], bias=k.mod[:, i, 0:1])
    squares(0, range(DT))
    squares(1, range(3))
    stat_root_scalar(k, act, n, [c0], D)
    squares(1, range(3, DT))
    stat_copy_scalar(k, act, n, [c0])
    apply(0, range(2))
    stat_root_scalar(k, act, n, [c1], D)
    apply(0, range(2, 5))
    stat_copy_scalar(k, act, n, [c1])
    apply(0, range(5, DT))
    act.wait_ge(k.sem("x1_done"), NCH * DT)
    act.dma_start(a.x1_store, k.x[:, :, :]).then_inc(k.sem("x1_stored"), 16)
    apply(1, range(DT))
    act.wait_ge(k.sem("ctx_biased"), DT)
    act.activation(k.h2h[:, :, S:SC], k.ctx[:, :, :], ACT.Copy).then_inc(k.sem("ctx_hi"), 1)


def enter_vector(k, dve, n, ap, ch):
    c0, c1 = HALVES
    stat_vector(k, dve, n, HALVES)
    rstd_ready(k, dve, n.c - 1)

    def x1(c, tiles):
        s = slice(512 * c, 512 * c + 512)
        dve.wait_ge(k.sem(f"x_back{c}"), 16)
        for i in tiles:
            ch(dve.scalar_tensor_tensor(k.outr[:, i, s], k.outr[:, i, s], col(k, "post_g", i), k.rstd[:, s],
                                        ALU.mult, ALU.mult))
            dve.tensor_tensor(k.x[:, i, s], k.x[:, i, s], k.outr[:, i, s], ALU.add).then_inc(k.sem("x1_done"), 1)

    def apply(c, tiles):
        for i in tiles:
            apply_vector(k, dve, ap, k.x[:, i, 512 * c:512 * c + 512], k.gm[:, i:i + 1], *HALVES[c])
    x1(0, range(DT))
    rstd_ready(k, dve, n.c)
    x1(1, range(5))
    stat_vector(k, dve, n, [c0])
    x1(1, range(5, DT))
    dve.wait_ge(k.sem("x1_done"), NCH * DT)
    rstd_ready(k, dve, n.c)
    apply(0, range(4))
    stat_vector(k, dve, n, [c1])
    apply(0, range(4, DT))
    rstd_ready(k, dve, n.c)
    apply(1, range(DT))
    dve.wait_ge(k.sem("ctx_hi"), 1)
    dve.tensor_tensor(k.h2l[:, :, S:SC], k.ctx[:, :, :], f32(k.h2h[:, :, S:SC]), ALU.subtract
                      ).then_inc(k.sem("ctx_split"), 1)
    dve.wait_ge(k.sem("normed"), ap.n)


def enter_tensor(k, pe, n):
    stat_sum_tensor(k, pe, n, HALVES, DT - CTX_AFTER, 0)
    stat_spread_tensor(k, pe, n, HALVES)
    for chunk in HALVES:
        stat_sum_tensor(k, pe, n, [chunk], DT, 1)
        stat_spread_tensor(k, pe, n, [chunk])


def enter_gpsimd(k, pool, n, ap):
    for chunk in HALVES:
        for i in range(DT):
            square_add(k, pool, n, *chunk, i == 0)
    low_parts(k, pool, ap, k.h2h, k.h2l)



def h2_gemm(k, pe, tile, unit, width, **how):
    gemm_tile(k, pe, tile, unit, unit_block(k, unit.slot), act_of(k.h2h, k.h2l), DT, width, **how)


LATENTS = (S, S, SC, SC, SC)
KV_CHUNKS = HALVES + [(S, CTX)]


def latents_tensor(k, pe, n, n_applied):
    def ready(i, c):
        pe.wait_ge(k.sem("normed_split"), n_applied + DT * c + i + 1)
    for j, width in enumerate(LATENTS):
        if j == 2:
            pe.wait_ge(k.sem("ctx_split"), 1)
        h2_gemm(k, pe, at_stage("latents", "tile", 0, j), at_stage("latents", "unit", 0, j), width,
                ready=None if j else ready, by_chunk=j == 0)
        if j == 1:
            stat_sum_tensor(k, pe, n, HALVES, 2, 1)
        if j == 2:
            stat_spread_tensor(k, pe, n, HALVES)
        if j == 3:
            stat_sum_tensor(k, pe, n, KV_CHUNKS[:2], 2, 1)
    stat_spread_tensor(k, pe, n, KV_CHUNKS[:2])
    stat_sum_tensor(k, pe, n, KV_CHUNKS[2:])
    stat_spread_tensor(k, pe, n, KV_CHUNKS[2:])


def latents_scalar(k, act, a, n):
    act.wait_ge(k.sem("x1_stored"), 16)
    act.dma_start(k.lat_table[:, :], a.mla_table).then_inc(k.sem("lat_table"), 16)
    act.dma_start(k.rtab[:, :, :], a.ret_table).then_inc(k.sem("ret_table"), 16)

    def evacuate(j):
        t = at_stage("latents", "tile", 0, j)
        wait_tile(k, act, t)
        dst = k.cq[:, j, :] if j < 2 else k.ckv[:, j - 2, :]
        read_tile(k, act.activation(dst, bank(k, t, LATENTS[j]), ACT.Copy), t)
        act.wait_ge(k.sem(f"tile_read{t.slot}"), t.half(1))
        return dst
    for j in range(2):
        square_scalar(k, act, n, evacuate(j), 0, S, j == 0)
    stat_root_scalar(k, act, n, HALVES, 2 * P)
    kv = evacuate(2)
    stat_copy_scalar(k, act, n, HALVES)
    square_scalar(k, act, n, kv, 0, SC, True)
    square_scalar(k, act, n, evacuate(3), 0, SC, False)
    act.wait_ge(k.sem("latent_normed"), 2)
    act.dma_start(a.cq_store, k.cq[:, :, :]).then_inc(k.sem("latents_stored"), 16)
    for chunks in (KV_CHUNKS[:2], KV_CHUNKS[2:]):
        stat_root_scalar(k, act, n, chunks, 2 * P)
        stat_copy_scalar(k, act, n, chunks)
    act.wait_ge(k.sem("latent_normed"), 4)
    act.dma_start(a.ckv_store, k.ckv[:, :, :]).then_inc(k.sem("latents_stored"), 16)
    act.wait_ge(k.sem("key_rotated"), 1)
    act.dma_start(a.kpe_store, k.kpe[64:96, :]).then_inc(k.sem("latents_stored"), 16)
    act.wait_ge(k.sem("latents_stored"), 48)


def latents_vector(k, dve, n, ch):
    def normed(t, gain, w):
        for j in range(2):
            dve.scalar_tensor_tensor(t[:, j, :], t[:, j, :], col(k, gain, j), k.rstd[:, :w], ALU.mult, ALU.mult
                                     ).then_inc(k.sem("latent_normed"), 1)
    for j in range(2):
        square_add(k, dve, n, 0, S, j == 0)
    stat_vector(k, dve, n, HALVES)
    rstd_ready(k, dve, n.c)
    normed(k.cq, "gq", S)
    dve.wait_ge(k.sem("latent_normed"), 2)
    for j in range(2):
        square_add(k, dve, n, 0, SC, j == 0)
    stat_vector(k, dve, n, KV_CHUNKS)
    rstd_ready(k, dve, n.c)
    normed(k.ckv, "gkv", SC)
    t = at_stage("latents", "tile", 0, 4)
    dve.wait_ge(k.sem("lat_table"), 16)
    wait_tile(k, dve, t)
    ch(dve.tensor_tensor(k.kpe[64:96, 0:S], k.lat_table[64:96, :], bank(k, t)[64:96, :], ALU.mult))
    ch(dve.tensor_tensor(k.kpt[64:96, :], k.lat_table[96:128, :], bank(k, t)[96:128, :], ALU.mult))
    read_tile(k, dve.tensor_copy(k.kpe[64:96, S:SC], bank(k, t, CTX, S)[64:96, :]), t)
    dve.wait_ge(k.sem(f"tile_read{t.slot}"), t.half(1))
    dve.tensor_tensor(k.kpe[64:96, 0:S], k.kpe[64:96, 0:S], k.kpt[64:96, :], ALU.add).then_inc(k.sem("key_rotated"), 1)
    dve.wait_ge(k.sem("latents_stored"), 48)



REST = ["RG", "RKT", "RVT", "RSC", "RDF", "RDB"]
RET_STAGES = (("ret_first", [("RK", 0), ("RV", 0), ("RQ", 0)]),
              ("ret", [(t, 0) for t in REST] + [("RK", 1), ("RO", 0), ("RV", 1), ("RM", 0), ("RQ", 1), ("RVAR", 0)]),
              ("ret_last", [(t, 0) for t in REST + ["RO", "RM", "RVAR"]]))


def ret_heads(eng, step):
    (first, o0), (mid, o1), (last, o2) = RET_STAGES
    step(first, o0, 0, 0)
    with eng.Fori(0, RH - 1) as i:
        step(mid, o1, i, i)
    step(last, o2, 0, RH - 1)


def ret_tile(stage, order, i, what):
    return at_stage(stage, "tile", i, [w for w, _ in order].index(what))


def ret_unit(stage, i, what):
    j = {"ret_first": {"RK": 0, "RV": 1, "RQ": 2}, "ret": {"RG": 0, "RK": 1, "RV": 2, "RQ": 3}, "ret_last": {"RG": 0}}
    return at_stage(stage, "unit", i, j[stage][what])


def ret_tensor(k, pe):
    ident = k.const[:, CONSTS["ident"]:CONSTS["ident"] + P]

    def cols(t, c):
        return t[:, P * c:P * c + P]

    def step(stage, order, i, head):
        for what, later in order:
            t = ret_tile(stage, order, i, what)
            h = head + later
            if what in ("RK", "RV", "RQ", "RG"):
                h2_gemm(k, pe, t, ret_unit(stage, i, what), S if what in ("RQ", "RG") else SC)
                continue
            pe.wait_ge(k.sem(f"tile_read{t.slot}"), t.half(0))
            b = tile_bank(t.slot)

            def product(c, lhs, rhs, start=True, stop=True):
                return pe.matmul(k.ps[:, b + P * c:b + P * c + P], lhs, rhs, start=start, stop=stop)
            if what in ("RKT", "RVT"):
                src = k.rk if what == "RKT" else k.rv
                pe.wait_ge(k.sem("ret_k_roped" if what == "RKT" else "ret_v_read"), h + 1)
                for c in range(NC + NCC):
                    mm = pe.transpose(k.ps[:, b + P * c:b + P * c + P], cols(src, c), ident)
            elif what == "RSC":
                pe.wait_ge(k.sem("ret_q_roped"), h + 1)
                for c in range(NC):
                    mm = product(c, cols(k.rk, c), cols(k.rq, c))
            elif what in ("RDF", "RDB"):
                if what == "RDF":
                    pe.wait_ge(k.sem("ret_k_decayed"), 2 * h + 2)
                    pe.wait_ge(k.sem("ret_v_turned"), h + 1)
                for c in range(NC + NCC):
                    mm = product(c, k.kz[what == "RDB"][:, c, :], k.rvt[:, c, :])
            elif what == "RO":
                pe.wait_ge(k.sem("ret_q_decayed"), 2 * h + 2)
                pe.wait_ge(k.sem("ret_scores"), h + 1)
                pe.wait_ge(k.sem("ret_states"), 2 * h + 2)
                for c in range(NC):
                    product(c, k.rvt[:, c, :], cols(k.rsd, c), stop=False)
                    product(c, k.st[0][:, c, :], cols(k.xq[0], c), False, False)
                    mm = product(c, k.st[1][:, c, :], cols(k.xq[1], c), False, True)
            else:
                src = k.ro if what == "RM" else k.csq
                pe.wait_ge(k.sem("ret_output" if what == "RM" else "ret_squares"), h + 1)
                for c in range(NCH):
                    s = slice(512 * c, 512 * c + 512)
                    mm = pe.matmul(k.ps[:, b + 512 * c:b + 512 * c + 512], k.one32[:, :], src[:, s], start=True, stop=True)
            mm.then_inc(k.sem("tile_done"), 1)
    ret_heads(pe, step)


def chunked(ap):
    return ap.rearrange("p (c n) -> p c n", n=P)


def ret_scalar(k, act, a, ch):
    C = lambda name, w=P: k.const[:, CONSTS[name]:CONSTS[name] + w]
    ch(act.activation(k.lg[:, 0:2 * RH], k.params[:, PARAMS["decay"]:PARAMS["decay"] + 2 * RH], ACT.Exp))
    ch(act.activation(k.lg[:, 0:2 * RH], k.lg[:, 0:2 * RH], ACT.Copy, scale=-1.0))
    act.activation(k.lg[:, 2 * RH:], k.lg[:, 0:2 * RH], ACT.Exp, scale=float(P)).then_inc(k.sem("ret_gammas"), 1)
    act.wait_ge(k.sem("ret_gammas"), 1)

    def copy(dst, t, w, **how):
        wait_tile(k, act, t)
        return act.activation(dst, bank(k, t, w), ACT.Copy, **how)

    def step(stage, order, i, head):
        for what, later in order:
            t = ret_tile(stage, order, i, what)
            h = head + later
            if what == "RG":
                if stage == "ret_last":
                    act.wait_ge(k.sem("ret_q_roped"), RH)
                    act.dma_start(k.mtab[:, :], a.mla_table).then_inc(k.sem("mtab_back"), 16)
                wait_tile(k, act, t)
                read_tile(k, act.activation(k.rg[:, :], bank(k, t), ACT.Silu), t)
            elif what == "RQ":
                lf, lb = k.lg[:, bass.ds(h, 1)], k.lg[:, bass.ds(h + RH, 1)]
                for src, dst, s in ((C("fwd"), k.dec[:, 0, :], lf), (C("bwd"), k.dec[:, 1, :], lb),
                                    (C("xf"), k.dec[:, 3, :], lf), (C("xb"), k.dec[:, 4, :], lb),
                                    (C("zf", 1), k.zeta[:, 0:1], lf), (C("zb", 1), k.zeta[:, 1:2], lb)):
                    act.activation(dst, src, ACT.Exp, scale=s).then_inc(k.sem("ret_decays"), 1)
                act.wait_ge(k.sem("ret_decays"), 6 * h + 6)
                act.activation(k.zeta[:, 2:4], k.zeta[:, 0:2], ACT.Copy, scale=RET_SCALE).then_inc(k.sem("ret_zetas"), 1)
            elif what == "RV":
                read_tile(k, copy(k.rv[:, :], t, SC), t)
                act.wait_ge(k.sem(f"tile_read{t.slot}"), t.half(1))
                act.activation(k.idle[:, 1:2], k.idle[:, 3:4], ACT.Copy).then_inc(k.sem("ret_v_read"), 1)
            elif what == "RKT":
                act.wait_ge(k.sem("ret_zetas"), h + 1)
                wait_tile(k, act, t)
                for d in range(2):
                    act.activation(k.kz[d][:, :, :], chunked(bank(k, t, SC)), ACT.Copy, scale=k.zeta[:, 2 + d:3 + d]
                                   ).then_inc(k.sem("ret_k_decayed"), 1)
                act.wait_ge(k.sem("ret_k_decayed"), 2 * h + 2)
                release_tile(k, act, t)
            elif what == "RVT":
                wait_tile(k, act, t)
                act.activation(k.rvt[:, :, :], chunked(bank(k, t, SC)), ACT.Copy).then_inc(k.sem("ret_v_turned"), 1)
                act.wait_ge(k.sem("ret_v_turned"), h + 1)
                release_tile(k, act, t)
            elif what == "RO":
                copy(k.ro[:, :], t, S).then_inc(k.sem("ret_output"), 1)
                act.wait_ge(k.sem("ret_output"), h + 1)
                release_tile(k, act, t)
            elif what == "RM":
                act.wait_ge(k.sem("ret_centred"), h + 1)
                act.activation(k.csq[:, :], k.cen[:, :], ACT.Square).then_inc(k.sem("ret_squares"), 1)
            elif what == "RVAR":
                wait_tile(k, act, t)
                read_tile(k, act.activation(k.rroot[:, :], bank(k, t), ACT.Sqrt, bias=EPS, scale=1.0 / P), t)
                if stage != "ret_last":
                    ret_store_scalar(k, act, a, h)
    ret_heads(act, step)


def ret_store_scalar(k, act, a, h):
    act.wait_ge(k.sem("ret_out"), h + 1)
    act.dma_start(a.o_store[:, bass.ds(h + BT, 1), :].rearrange("p a n -> p (a n)"), k.rout[:, :]
                  ).then_inc(k.sem("ret_stored"), 16)


def ret_vector(k, dve, ch):
    dve.wait_ge(k.sem("ret_table"), 16)
    dve.wait_ge(k.sem("ret_gammas"), 1)

    def rope(t, dst, name, h):
        wait_tile(k, dve, t)
        ps = bank(k, t)
        dve.tensor_tensor(dst[:, 0:S], k.rtab[:, 0, :], ps, ALU.mult).then_inc(k.sem(f"{name}_cos"), 1)
        if name == "ret_k":
            dve.tensor_copy(dst[:, S:SC], bank(k, t, CTX, S)).then_inc(k.sem("ret_k_context"), 1)
        dve.tensor_tensor(k.rt[0:64, :], k.rtab[64:128, 1, :], ps[64:128, :], ALU.mult).then_inc(k.sem(f"{name}_sin"), 1)
        read_tile(k, dve.tensor_tensor(k.rt[64:128, :], k.rtab[0:64, 1, :], ps[0:64, :], ALU.mult), t)
        dve.wait_ge(k.sem(f"{name}_sin"), h + 1)
        dve.wait_ge(k.sem(f"{name}_cos"), h + 1)
        dve.wait_ge(k.sem(f"tile_read{t.slot}"), t.half(1))
        dve.tensor_tensor(dst[:, 0:S], dst[:, 0:S], k.rt[:, :], ALU.add).then_inc(k.sem(f"{name}_roped"), 1)
        dve.wait_ge(k.sem(f"{name}_roped"), h + 1)

    def states(t, d, h, count):
        wait_tile(k, dve, t)
        g = k.lg[:, bass.ds(h + (2 * RH + RH * d), 1)]
        order = list(range(NC)) if d == 0 else list(range(NC - 1, -1, -1))
        near, far = (NC + 1, NC) if d == 0 else (NC, NC + 1)
        inc = lambda c: bank(k, t, P, P * c)
        st = k.st[d]
        n = count

        def chain(ins):
            nonlocal n
            n += 1
            ins.then_inc(k.sem("ret_state_steps"), 1)
            dve.wait_ge(k.sem("ret_state_steps"), 2 * (NC + 1) * h + n)
        chain(dve.tensor_scalar(st[:, order[0], :], inc(far), g, None, ALU.mult))
        chain(dve.tensor_tensor(st[:, order[0], :], st[:, order[0], :], inc(near), ALU.add))
        for p, c in zip(order, order[1:]):
            chain(dve.scalar_tensor_tensor(st[:, c, :], st[:, p, :], g, inc(p), ALU.mult, ALU.add))
        dve.memset(k.idle[:, 2:3], 0.0).then_inc(k.sem("ret_states"), 1)
        release_tile(k, dve, t)
        return n

    def step(stage, order, i, head):
        for what, later in order:
            t = ret_tile(stage, order, i, what)
            h = head + later
            if what == "RK":
                rope(t, k.rk, "ret_k", h)
                dve.wait_ge(k.sem("ret_k_context"), h + 1)
            elif what == "RQ":
                rope(t, k.rq, "ret_q", h)
            elif what == "RG":
                dve.wait_ge(k.sem("ret_decays"), 6 * h + 6)
                dve.scalar_tensor_tensor(k.dec[:, 2, :], k.dec[:, 0, :], RET_SCALE, k.dec[:, 1, :], ALU.mult, ALU.mult
                                         ).then_inc(k.sem("ret_both"), 1)
                for d in range(2):
                    dve.tensor_tensor(chunked(k.xq[d][:, :]), chunked(k.rq[:, :]),
                                      k.dec[:, 3 + d:4 + d, :].to_broadcast([P, NC, P]), ALU.mult
                                      ).then_inc(k.sem("ret_q_decayed"), 1)
            elif what == "RSC":
                wait_tile(k, dve, t)
                dve.wait_ge(k.sem("ret_both"), h + 1)
                dve.tensor_tensor(chunked(k.rsd[:, :]), chunked(bank(k, t)), k.dec[:, 2:3, :].to_broadcast([P, NC, P]),
                                  ALU.mult).then_inc(k.sem("ret_scores"), 1)
                dve.wait_ge(k.sem("ret_scores"), h + 1)
                release_tile(k, dve, t)
            elif what == "RDF":
                n = states(t, 0, h, 0)
            elif what == "RDB":
                states(t, 1, h, n)
            elif what == "RM":
                wait_tile(k, dve, t)
                dve.scalar_tensor_tensor(k.cen[:, :], bank(k, t), -1.0 / P, k.ro[:, :], ALU.mult, ALU.add
                                         ).then_inc(k.sem("ret_centred"), 1)
                dve.wait_ge(k.sem("ret_centred"), h + 1)
                release_tile(k, dve, t)
            elif what == "RVAR":
                if stage != "ret_last":
                    ret_finish_vector(k, dve, t, h)
    ret_heads(dve, step)


def ret_finish_vector(k, dve, t, h):
    dve.wait_ge(k.sem(f"tile_read{t.slot}"), t.half(1))
    dve.reciprocal(k.rroot[:, :], k.rroot[:, :]).then_inc(k.sem("ret_rstd"), 1)
    dve.wait_ge(k.sem("ret_rstd"), h + 1)
    dve.scalar_tensor_tensor(k.cen[:, :], k.cen[:, :], k.params[:, bass.ds(h + PARAMS["gret"], 1)],
                             k.rroot[:, :], ALU.mult, ALU.mult).then_inc(k.sem("ret_normed"), 1)
    dve.wait_ge(k.sem("ret_normed"), h + 1)
    dve.wait_ge(k.sem("ret_stored"), 16 * h + 1)
    dve.tensor_tensor(k.rout[:, :], k.cen[:, :], k.rg[:, :], ALU.mult).then_inc(k.sem("ret_out"), 1)





def latents_back_sync(k, sp, a):
    t = ret_tile(*RET_STAGES[2], 0, "RG")
    wait_tile(k, sp, t)
    sp.wait_ge(k.sem("latents_stored"), 48)
    for dst, src, name in ((k.cqr[:, :, :], a.cq_store, "cq"), (k.ckvr[:, :, :], a.ckv_store, "ckv"),
                           (k.kpr[64:96, :], a.kpe_store, "kpe")):
        sp.dma_start(dst, src).then_inc(k.sem(f"{name}_back"), 16)


def latents_back_gpsimd(k, pool):
    pieces = [(k.cqr[:, j, :], [m[:, j, :] for m in k.cqn], "cq", S, P) for j in range(2)]
    pieces += [(k.ckvr[:, j, :], [m[:, j, :] for m in k.ckvn], "ckv", SC, P) for j in range(2)]
    pieces += [(k.kpr[64:96, :], [m[64:96, :] for m in mk], "kpe", SC, 32) for mk in k.mk]
    for n, (src, (hi, lo), name, w, rows) in enumerate(pieces):
        pool.wait_ge(k.sem(f"{name}_back"), 16)
        if rows != P:
            pool.wait_ge(k.sem("latents_split"), n)
        one = k.one32[:, 0:1] if rows == P else k.one32[64:96, 0:1]
        pool.tensor_tensor(hi, src, one.to_broadcast([rows, w]), ALU.mult).then_inc(k.sem("latents_hi"), 1)
        pool.wait_ge(k.sem("latents_hi"), n + 1)
        pool.tensor_tensor(lo, src, f32(hi), ALU.subtract).then_inc(k.sem("latents_split"), 1)
    pool.wait_ge(k.sem("latents_split"), len(pieces))


QB = S // P


def pair_order(more):
    order = []
    for g in range(2 * QB + 2):
        if g < 2 * QB:
            order.append(("S", g))
        if g >= 2:
            order.append(("T", g - 2))
        if g >= 4:
            order.append(("OP"[g % 2], (g - 4) // 2))
        what = {3: "Q", 4: "K", 6: "V"}.get(g % QB) if g < 2 * QB else None
        if what and (g < QB or more):
            order.append((what, 1 if g < QB else 0))
    return order + [("O", QB - 1), ("P", QB - 1)]


def pair_tiles(order):
    tiles = [w for w in order if w[0] not in "OP"]
    return {w: n for n, w in enumerate(tiles)}


FIRST_ORDER = [("Q", 0), ("K", 0), ("V", 0)]
MLA_STAGES = (("mla_first", FIRST_ORDER), ("mla", pair_order(True)), ("mla_last", pair_order(False)))


def mla_pairs(eng, step):
    (first, o0), (mid, o1), (last, o2) = MLA_STAGES
    step(first, o0, 0, -1)
    with eng.Fori(0, PAIRS - 1) as i:
        step(mid, o1, i, i)
    step(last, o2, 0, PAIRS - 1)


def head_count(pair, what, head):
    return 1 if isinstance(pair, int) and pair < 0 else 2 * pair + (2 if head else 3)


def mla_tensor(k, pe):
    ident = k.const[:, CONSTS["ident"]:CONSTS["ident"] + P]
    pe.wait_ge(k.sem("latents_split"), 6)

    def step(stage, order, i, pair):
        index = pair_tiles(order)
        for what, g in order:
            if what not in "OP":
                t = at_stage(stage, "tile", i, index[what, g])
                b = tile_bank(t.slot)
            if what in "QK":
                u = at_stage(stage, "unit", i, 0 if stage != "mla" or g else 1)
                x, width = (k.cqn, S) if what == "Q" else (k.ckvn, SC)
                gemm_tile(k, pe, t, u, unit_block(k, u.slot, base=0 if what == "Q" else 2 * P), act_of(*x), 2, width,
                          new_unit=what == "Q")
                continue
            ahead = order[order.index((what, g)) + 1:][:1]
            if what == "O" and ahead and ahead[0][0] == "V":
                v = at_stage(stage, "tile", i, index[ahead[0]])
                pe.wait_ge(k.sem(f"tile_read{v.slot}"), v.half(0))
                pe.wait_ge(k.sem("mla_v_raw"), head_count(pair, *ahead[0]))
            elif what in "ST" or stage == "mla_first":
                pe.wait_ge(k.sem(f"tile_read{t.slot}"), t.half(0))
            if what == "V":
                if stage == "mla_first":
                    pe.wait_ge(k.sem("mla_v_raw"), 1)
                for c in range(NC + NCC):
                    mm = pe.transpose(k.ps[:, b + HD * c:b + HD * c + HD], k.mvr[64:128, P * c:P * c + P],
                                      ident[64:128, 64:128])
                mm.then_inc(k.sem("tile_done"), 1)
                continue
            a, q = (g // QB, g % QB) if what in "ST" else (g // (QB // 2), g % (QB // 2))
            if what == "S":
                if q == 0:
                    pe.wait_ge(k.sem("mla_q_split"), 2 * pair + (a + 1))
                    pe.wait_ge(k.sem("mla_k_split"), 2 * pair + (a + 1))
                for c in range(0, SC, 512):
                    w = min(512, SC - c)
                    mm = three(pe, k.ps[:, b + c:b + c + w],
                               (k.mq[a][0][0:96, P * q:P * q + P], k.mq[a][1][0:96, P * q:P * q + P]),
                               (k.mk[a][0][0:96, c:c + w], k.mk[a][1][0:96, c:c + w]), True, True)
                mm.then_inc(k.sem("tile_done"), 1)
            elif what == "T":
                pe.wait_ge(k.sem("mla_probs"), 16 * pair + (g + 1))
                for c in range(NC + NCC):
                    mm = pe.transpose(k.ps[:, b + P * c:b + P * c + P], k.probs[:, g % NPROBS, P * c:P * c + P], ident)
                mm.then_inc(k.sem("tile_done"), 1)
            else:
                if what == "O":
                    pe.wait_ge(k.sem("mla_probs_split"), 16 * pair + (2 * g + 2))
                    pe.wait_ge(k.sem("mla_out_read"), 8 * pair + (g + 1))
                    if q == 0:
                        pe.wait_ge(k.sem("mla_v_split"), 2 * pair + (a + 1))
                b = 3072 + 512 * (g % 2)
                v = slice(HD * a, HD * a + HD)
                half = (NC + NCC) // 2
                for c in range(half) if what == "O" else range(half, NC + NCC):
                    mm = three(pe, k.ps[0:HD, b:b + 2 * P], (k.mv[0][:, c, v], k.mv[1][:, c, v]),
                               (k.pt[0][:, g % 2, c, :], k.pt[1][:, g % 2, c, :]), c == 0, c == NC + NCC - 1)
                if what == "P":
                    mm.then_inc(k.sem("mla_out"), 1)
    mla_pairs(pe, step)


def turned(k, m, g):
    return k.pt[m][:, (g // 2) % 2, :, P * (g % 2):P * (g % 2) + P]


def mla_scalar(k, act, a):
    def step(stage, order, i, pair):
        index = pair_tiles(order)
        for what, g in order:
            if what in "OP":
                continue
            t = at_stage(stage, "tile", i, index[what, g])
            if what == "Q":
                wait_tile(k, act, t)
                act.activation(k.mqf[0:64, :], bank(k, t)[0:64, :], ACT.Copy).then_inc(k.sem("mla_q_nope"), 1)
            elif what == "K":
                act.wait_ge(k.sem("mla_q_roped"), head_count(pair, what, g))
                act.activation(k.mq[g][0][0:96, :], k.mqf[0:96, :], ACT.Copy).then_inc(k.sem("mla_q_hi"), 1)
                wait_tile(k, act, t)
                act.activation(k.mvr[64:128, :], bank(k, t, SC)[64:128, :], ACT.Copy).then_inc(k.sem("mla_v_raw"), 1)
                act.activation(k.mk[g][0][0:64, :], bank(k, t, SC)[0:64, :], ACT.Copy).then_inc(k.sem("mla_k_hi"), 1)
            elif what == "V":
                wait_tile(k, act, t)
                act.activation(k.mv[0][:, :, HD * g:HD * g + HD],
                               bank(k, t, 10 * HD).rearrange("p (c n) -> p c n", n=HD), ACT.Copy
                               ).then_inc(k.sem("mla_v_hi"), 1)
            elif what == "S":
                if g >= NPROBS:
                    wait_tile(k, act, at_stage(stage, "tile", i, index["T", g - NPROBS]))
                wait_tile(k, act, t)
                read_tile(k, act.activation(k.probs[:, g % NPROBS, :], bank(k, t, SC), ACT.Copy), t)
                if g < 2:
                    mla_exp(k, act, pair, g)
            else:
                wait_tile(k, act, t)
                if g >= 4 and g % 2 == 0:
                    act.wait_ge(k.sem("mla_out"), 8 * pair + (g // 2 - 1))
                act.activation(turned(k, 0, g), bank(k, t, SC).rearrange("p (c n) -> p c n", n=P), ACT.Copy
                               ).then_inc(k.sem("mla_probs_hi"), 1)
                if g + 2 < 2 * QB:
                    mla_exp(k, act, pair, g + 2)
        if stage == "mla_first":
            ret_store_scalar(k, act, a, RH - 1)
    mla_pairs(act, step)


def mla_exp(k, act, pair, g):
    p = k.probs[:, g % NPROBS, :]
    act.wait_ge(k.sem("mla_max"), 16 * pair + (g + 1))
    act.activation(p, p, ACT.Exp, scale=MLA_SCALE, bias=k.stat[:, 1, g:g + 1], accum_out=k.stat[:, 2, g:g + 1]
                   ).then_inc(k.sem("mla_exp"), 1)


def mla_vector(k, dve, ch):
    dve.wait_ge(k.sem("mtab_back"), 16)

    def step(stage, order, i, pair):
        index = pair_tiles(order)

        def normalise(g):
            p = k.probs[:, g % NPROBS, :]
            dve.wait_ge(k.sem("mla_exp"), 16 * pair + (g + 1))
            dve.reciprocal(k.stat[:, 3, g:g + 1], k.stat[:, 2, g:g + 1]).then_inc(k.sem("mla_share"), 1)
            dve.wait_ge(k.sem("mla_share"), 16 * pair + (g + 1))
            dve.tensor_scalar(p, p, k.stat[:, 3, g:g + 1], None, ALU.mult).then_inc(k.sem("mla_probs"), 1)

        def out(m):
            dve.wait_ge(k.sem("mla_out"), 8 * pair + (m + 1))
            if m == 0:
                dve.wait_ge(k.sem("ret_stored"), 16 * RH + 1)
                dve.wait_ge(k.sem("mla_stored"), 16 * pair + 1)
            r = slice(HD * (m // 4), HD * (m // 4) + HD)
            b, q = 3072 + 512 * (m % 2), m % 4
            dve.tensor_copy(k.mo[r, 2 * P * q:2 * P * q + 2 * P], k.ps[0:HD, b:b + 2 * P]
                            ).then_inc(k.sem("mla_out_read"), 1)
        due = None
        for what, g in order:
            if what == "O":
                continue
            if what == "P":
                if due is not None:
                    out(due)
                due = g
                if g == QB - 1:
                    out(g)
                continue
            t = at_stage(stage, "tile", i, index[what, g])
            heads = head_count(pair, what, g)
            if what == "Q":
                wait_tile(k, dve, t)
                dve.wait_ge(k.sem("mla_q_nope"), heads)
                if not (isinstance(pair, int) and pair < 0):
                    dve.wait_ge(k.sem("mla_q_split"), heads - 1)
                dve.tensor_tensor(k.mqf[64:96, :], k.mtab[64:96, :], bank(k, t)[64:96, :], ALU.mult
                                  ).then_inc(k.sem("mla_q_cos"), 1)
                read_tile(k, dve.tensor_tensor(k.mqt[64:96, :], k.mtab[96:128, :], bank(k, t)[96:128, :], ALU.mult), t)
                dve.wait_ge(k.sem("mla_q_cos"), heads)
                dve.wait_ge(k.sem(f"tile_read{t.slot}"), t.half(1))
                dve.tensor_tensor(k.mqf[64:96, :], k.mqf[64:96, :], k.mqt[64:96, :], ALU.add
                                  ).then_inc(k.sem("mla_q_roped"), 1)
            elif what == "K":
                dve.wait_ge(k.sem("mla_q_hi"), heads)
                dve.tensor_tensor(k.mq[g][1][0:96, :], k.mqf[0:96, :], f32(k.mq[g][0][0:96, :]), ALU.subtract
                                  ).then_inc(k.sem("mla_q_split"), 1)
                dve.wait_ge(k.sem("mla_k_hi"), heads)
                dve.tensor_tensor(k.mk[g][1][0:64, :], bank(k, t, SC)[0:64, :], f32(k.mk[g][0][0:64, :]),
                                  ALU.subtract).then_inc(k.sem("mla_k_split"), 1)
                dve.wait_ge(k.sem("mla_k_split"), heads)
                release_tile(k, dve, t)
            elif what == "V":
                v = slice(HD * g, HD * g + HD)
                dve.wait_ge(k.sem("mla_v_hi"), heads)
                dve.tensor_tensor(k.mv[1][:, :, v], bank(k, t, 10 * HD).rearrange("p (c n) -> p c n", n=HD),
                                  f32(k.mv[0][:, :, v]), ALU.subtract).then_inc(k.sem("mla_v_split"), 1)
                dve.wait_ge(k.sem("mla_v_split"), heads)
                release_tile(k, dve, t)
            elif what == "S":
                if g:
                    normalise(g - 1)
                if due is not None:
                    out(due)
                    due = None
                dve.wait_ge(k.sem(f"tile_read{t.slot}"), t.half(1))
                dve.tensor_reduce(k.stat[:, 0, g:g + 1], k.probs[:, g % NPROBS, :], AX.X, ALU.max
                                  ).then_inc(k.sem("mla_max_raw"), 1)
                dve.wait_ge(k.sem("mla_max_raw"), 16 * pair + (g + 1))
                dve.tensor_scalar(k.stat[:, 1, g:g + 1], k.stat[:, 0, g:g + 1], -MLA_SCALE, None, ALU.mult
                                  ).then_inc(k.sem("mla_max"), 1)
            else:
                if g == 2 * QB - 2:
                    normalise(2 * QB - 1)
                dve.wait_ge(k.sem("mla_probs_hi"), 16 * pair + (g + 1))
                dve.tensor_tensor(turned(k, 1, g), bank(k, t, SC).rearrange("p (c n) -> p c n", n=P),
                                  f32(turned(k, 0, g)), ALU.subtract).then_inc(k.sem("mla_probs_split"), 1)
                dve.wait_ge(k.sem("mla_probs_split"), 16 * pair + (g + 1))
                release_tile(k, dve, t)
        if stage == "mla_first":
            ret_finish_vector(k, dve, ret_tile(*RET_STAGES[2], 0, "RVAR"), RH - 1)
    mla_pairs(dve, step)


def mla_sync(k, sp, stream, a):
    first = FIRST_UNIT["mla_first"] + 3
    with sp.Fori(0, PAIRS) as i:
        for n in range(2):
            load_unit(k, sp, (first + n) % 2, stream[bass.ds(2 * i + (first + n), 1)].rearrange("a p n -> (a p) n"),
                      2 * i + (first + n - 1))
        sp.wait_ge(k.sem("mla_out_read"), 8 * i + 10)
        sp.dma_start(a.o_store[:, bass.ds(i, 1), :].rearrange("p a n -> p (a n)"), k.mo[:, :]
                     ).then_inc(k.sem("mla_stored"), 16)
    return first + 2 * PAIRS



O_ORDER = list(range(BT, DT)) + list(range(BT))


def out2_scalar(k, act, a, n, ap):
    act.wait_ge(k.sem("mla_out_read"), 8 * PAIRS + 2)
    for g in (BT, BT + 2, 0, 2):
        if g == 0:
            act.wait_ge(k.sem("mla_stored"), 16 * PAIRS + 1)
        else:
            act.wait_ge(k.sem("ret_stored"), 16 * RH + 1)
        act.dma_start(k.outr[:, g:g + 2, :], a.o_store[:, g:g + 2, :]).then_inc(k.sem(f"o_back{g}"), 16)
    act.dma_start(k.x[:, :, :], a.x1_store).then_inc(k.sem("x1_back"), 16)
    for i in O_ORDER:
        act.wait_ge(k.sem(f"o_back{i // 2 * 2}"), 16)
        act.activation(k.hh[:, i, :], k.outr[:, i, :], ACT.Copy).then_inc(k.sem("o_hi"), 1)
    for j in range(DT):
        act.wait_ge(k.sem("x2_done"), j + 1)
        square_scalar(k, act, n, k.x[:, j, :], 0, S, j == 0)
    stat_root_scalar(k, act, n, HALVES, D)
    stat_copy_scalar(k, act, n, HALVES)
    for c in range(NCH):
        for i in range(DT):
            apply_scalar(k, act, ap, k.hh[:, i, 512 * c:512 * c + 512], bias=k.mod[:, 3 * DT + i, 0:1])


def out2_vector(k, dve, n, ap):
    for m, i in enumerate(O_ORDER):
        dve.wait_ge(k.sem("o_hi"), m + 1)
        dve.tensor_tensor(k.hl[:, i, :], k.outr[:, i, :], f32(k.hh[:, i, :]), ALU.subtract).then_inc(k.sem("o_split"), 1)
    dve.wait_ge(k.sem("x1_back"), 16)
    for j in range(DT):
        t = at_stage("out2", "tile", 0, j)
        wait_tile(k, dve, t)
        dve.scalar_tensor_tensor(k.x[:, j, :], bank(k, t), k.mod[:, 2 * DT + j, 0:1], k.x[:, j, :],
                                 ALU.mult, ALU.add).then_inc(k.sem("x2_done"), 1)
        dve.wait_ge(k.sem("x2_done"), j + 1)
        release_tile(k, dve, t)
        square_add(k, dve, n, 0, S, j == 0)
    stat_vector(k, dve, n, HALVES)
    for c, chunk in enumerate(HALVES):
        rstd_ready(k, dve, n.c - 1 + c)
        for i in range(DT):
            apply_vector(k, dve, ap, k.x[:, i, 512 * c:512 * c + 512], k.gm[:, 2 * DT + i:2 * DT + i + 1], *chunk)


def out2_tensor(k, pe, n):
    def ready(i, _):
        pe.wait_ge(k.sem("o_split"), i + 1)
    for j in range(DT):
        u = at_stage("out2", "unit", 0, j)
        lhs = unit_block(k, u.slot)
        gemm_tile(k, pe, at_stage("out2", "tile", 0, j), u, lambda i: lhs(O_ORDER[i]),
                  lambda i, c, w: act_of(k.hh, k.hl)(O_ORDER[i], c, w), DT, ready=None if j else ready)
    stat_sum_tensor(k, pe, n, HALVES, DT, 1)
    stat_spread_tensor(k, pe, n, HALVES)



def up_tensor(k, pe, stage, i, ready=None):
    for j in range(4):
        r = ready if j == 0 else None
        full_gemm(k, pe, at_stage(stage, "tile", i, j), at_stage(stage, "unit", i, j), ready=r, by_chunk=r is not None)


def down_tensor(k, pe, stage, i, tile0, unit0):
    for j in range(DT):
        u = at_stage(stage, "unit", i, unit0 + j // 4)
        gemm_tile(k, pe, at_stage(stage, "tile", i, tile0 + j), u, unit_block(k, u.slot, 4 * P, P * (j % 4)),
                  act_of(k.fh, k.fl), 2, new_unit=j % 4 == 0)


def up_scalar(k, act, stage, i, step):
    if stage == "ffn":
        act.wait_ge(k.sem("ff_split"), 2 * step)
    for m in range(2):
        for j, dst in ((0, k.fa), (1, k.fg)):
            t = at_stage(stage, "tile", i, 2 * m + j)
            p = PARAMS["conv2"] + 4 * (2 * m + j)
            tap = lambda n: k.params[:, bass.ds(16 * step + (p + n), 1)]
            wait_tile(k, act, t)
            act.activation(dst[:, m, :], bank(k, t), ACT.Identity, scale=tap(1), bias=tap(3)).then_inc(k.sem("ff_middle"), 1)
        act.wait_ge(k.sem(f"tile_read{t.slot}"), t.half(1))
        act.activation(k.fs[:, :], k.fg[:, m, :], ACT.Silu).then_inc(k.sem("ff_silu"), 1)
        act.wait_ge(k.sem("ff_product"), 2 * step + (m + 1))


def up_vector(k, dve, stage, i, step, meanwhile=None):
    for m in range(2):
        for j, dst in ((0, k.fa), (1, k.fg)):
            t = at_stage(stage, "tile", i, 2 * m + j)
            p = PARAMS["conv2"] + 4 * (2 * m + j)
            tap = lambda n: k.params[:, bass.ds(16 * step + (p + n), 1)]
            dve.wait_ge(k.sem("ff_middle"), 4 * step + (2 * m + j + 1))
            ps = bank(k, t)
            dve.scalar_tensor_tensor(dst[:, m, 1:], ps[:, :S - 1], tap(0), dst[:, m, 1:], ALU.mult, ALU.add
                                     ).then_inc(k.sem("ff_back"), 1)
            dve.wait_ge(k.sem("ff_back"), 4 * step + (2 * m + j + 1))
            read_tile(k, dve.scalar_tensor_tensor(dst[:, m, :S - 1], ps[:, 1:], tap(2), dst[:, m, :S - 1],
                                                  ALU.mult, ALU.add), t)
            dve.wait_ge(k.sem(f"tile_read{t.slot}"), t.half(1))
        if m == 1 and meanwhile is not None:
            meanwhile()
        dve.wait_ge(k.sem("ff_silu"), 2 * step + (m + 1))
        dve.tensor_tensor(k.fa[:, m, :], k.fa[:, m, :], k.fs[:, :], ALU.mult).then_inc(k.sem("ff_product"), 1)


def split_scalar(k, act, step, last_tile):
    wait_tile(k, act, last_tile)
    for m in range(2):
        act.wait_ge(k.sem("ff_product"), 2 * step + (m + 1))
        act.activation(k.fh[:, m, :], k.fa[:, m, :], ACT.Copy).then_inc(k.sem("ff_hi"), 1)


def split_vector(k, dve, step):
    for m in range(2):
        dve.wait_ge(k.sem("ff_hi"), 2 * step + (m + 1))
        dve.tensor_tensor(k.fl[:, m, :], k.fa[:, m, :], f32(k.fh[:, m, :]), ALU.subtract).then_inc(k.sem("ff_split"), 1)
    dve.wait_ge(k.sem("ff_split"), 2 * step + 2)


def down_vector(k, dve, stage, i, tile0, tiles):
    for j in tiles:
        t = at_stage(stage, "tile", i, tile0 + j)
        wait_tile(k, dve, t)
        read_tile(k, dve.scalar_tensor_tensor(k.x[:, j, :], bank(k, t), k.mod[:, 5 * DT + j, 0:1], k.x[:, j, :],
                                              ALU.mult, ALU.add), t)


LAST = FT // 2 - 1


def ffn_tensor(k, pe, n_applied):
    def ready(i, c):
        pe.wait_ge(k.sem("normed_split"), n_applied + DT * c + i + 1)
    up_tensor(k, pe, "up0", 0, ready)
    with pe.Fori(0, LAST) as i:
        up_tensor(k, pe, "ffn", i)
        pe.wait_ge(k.sem("ff_split"), 2 * i + 2)
        down_tensor(k, pe, "ffn", i, 4, 4)
    pe.wait_ge(k.sem("ff_split"), 2 * LAST + 2)
    down_tensor(k, pe, "down", 0, 0, 0)


def ffn_scalar(k, act):
    up_scalar(k, act, "up0", 0, 0)
    split_scalar(k, act, 0, at_stage("up0", "tile", 0, 3))
    with act.Fori(0, LAST) as i:
        up_scalar(k, act, "ffn", i, i + 1)
        split_scalar(k, act, i + 1, at_stage("ffn", "tile", i, 11))


def ffn_vector(k, dve):
    up_vector(k, dve, "up0", 0, 0)
    split_vector(k, dve, 0)
    with dve.Fori(0, LAST) as i:
        up_vector(k, dve, "ffn", i, i + 1, meanwhile=lambda: down_vector(k, dve, "ffn", i, 4, range(1)))
        down_vector(k, dve, "ffn", i, 4, range(1, DT))
        split_vector(k, dve, i + 1)



def end_scalar(k, act, n):
    for j in range(DT):
        act.wait_ge(k.sem("x3_done"), j + 1)
        square_scalar(k, act, n, k.x[:, j, :], 0, S, j == 0)
    stat_root_scalar(k, act, n, HALVES, D)
    stat_copy_scalar(k, act, n, HALVES)


def end_vector(k, dve, n):
    for j in range(DT):
        t = at_stage("down", "tile", 0, j)
        wait_tile(k, dve, t)
        dve.scalar_tensor_tensor(k.x[:, j, :], bank(k, t), k.mod[:, 5 * DT + j, 0:1], k.x[:, j, :],
                                 ALU.mult, ALU.add).then_inc(k.sem("x3_done"), 1)
        dve.wait_ge(k.sem("x3_done"), j + 1)
        release_tile(k, dve, t)
        square_add(k, dve, n, 0, S, j == 0)
    stat_vector(k, dve, n, HALVES)
    for c in range(NCH):
        rstd_ready(k, dve, n.c - 1 + c)
        s = slice(512 * c, 512 * c + 512)
        for i in range(DT):
            dve.scalar_tensor_tensor(k.outr[:, i, s], k.x[:, i, s], col(k, "gfin", i), k.rstd[:, s], ALU.mult, ALU.mult
                                     ).then_inc(k.sem("finished"), 1)


def end_tensor(k, pe, n):
    stat_sum_tensor(k, pe, n, HALVES, DT, 1)
    stat_spread_tensor(k, pe, n, HALVES)


def end_sync(k, sp, a):
    for c in range(NCH):
        s = slice(512 * c, 512 * c + 512)
        for h in range(2):
            sp.wait_ge(k.sem("finished"), DT * c + 4 * h + 4)
            sp.dma_start(a.out[:, 4 * h:4 * h + 4, s], k.outr[:, 4 * h:4 * h + 4, s]).then_inc(k.sem("out_stored"), 16)
    sp.wait_ge(k.sem("out_stored"), 16 * 2 * NCH)



class Arrays:
    pass


def two_blocks_program(nc, stream, w_ada, x, context, params, consts, ret_table, mla_table, out):
    a = Arrays()
    a.w_ada, a.x, a.ctx, a.ret_table, a.mla_table, a.out, a.params, a.consts = w_ada, x, context, ret_table, mla_table, out, params, consts
    a.x1_store = nc.dram_tensor("x1_store", (P, DT, S), F32).ap()
    a.cq_store = nc.dram_tensor("cq_store", (P, 2, S), F32).ap()
    a.ckv_store = nc.dram_tensor("ckv_store", (P, 2, SC), F32).ap()
    a.kpe_store = nc.dram_tensor("kpe_store", (32, SC), F32).ap()
    a.o_store = nc.dram_tensor("o_store", (P, DT, S), F32).ap()
    with ExitStack() as ctx:
        k = lay_out(nc, ctx)
        block = ctx.enter_context(nc.Block())

        @block.sync
        def _(sp):
            mla = FIRST_UNIT["mla_first"]
            load_weights(k, sp, stream, 0, mla + 3)
            latents_back_sync(k, sp, a)
            load_weights(k, sp, stream, mla_sync(k, sp, stream, a), NUNITS)
            end_sync(k, sp, a)

        @block.gpsimd
        def _(pool):
            n, ap = Norms(), Applies()
            pool.wait_ge(k.sem("one32"), 1)
            split_unit(k, pool, 0, 16, 1, None)
            low_parts(k, pool, ap, k.hh, k.hl)
            n.pass_over(2 * DT, 2)
            sb_gpsimd(k, pool)
            split_weights(k, pool, FIRST_UNIT["merge_sb"] + 1, FIRST_UNIT["latents"] + 1)
            n.pass_over(2 * DT, 2)
            enter_gpsimd(k, pool, n, ap)
            split_weights(k, pool, FIRST_UNIT["latents"] + 1, FIRST_UNIT["mla_first"] + 1)
            latents_back_gpsimd(k, pool)
            split_weights(k, pool, FIRST_UNIT["mla_first"] + 1, FIRST_UNIT["up0"] + 1)
            low_parts(k, pool, ap, k.hh, k.hl)
            split_weights(k, pool, FIRST_UNIT["up0"] + 1, NUNITS)

        @block.scalar
        def _(act):
            ch = Chain(act, k.sem("scalar_steps"))
            n, ap = Norms(), Applies()
            loads_scalar(k, act, a)
            start_scalar(k, act, n, ap)
            sb_scalar(k, act)
            merge_scalar(k, act, a, "merge_sb", 0)
            pool_scalar(k, act, a)
            merge_scalar(k, act, a, "merge_pool", 1)
            conv_scalar(k, act, a)
            merge_scalar(k, act, a, "merge_conv", 2)
            out1_scalar(k, act, a, n)
            enter_scalar(k, act, a, n, ap)
            latents_scalar(k, act, a, n)
            ret_scalar(k, act, a, ch)
            mla_scalar(k, act, a)
            out2_scalar(k, act, a, n, ap)
            ffn_scalar(k, act)
            end_scalar(k, act, n)

        @block.vector
        def _(dve):
            ch = Chain(dve, k.sem("vector_steps"))
            n, ap = Norms(), Applies()
            start_vector(k, dve, n, ap)
            sb_vector(k, dve)
            merge_vector(k, dve, "merge_sb", 0)
            pool_vector(k, dve, ch)
            merge_vector(k, dve, "merge_pool", 1)
            conv_vector(k, dve, ch)
            merge_vector(k, dve, "merge_conv", 2)
            out1_vector(k, dve, n, ch)
            enter_vector(k, dve, n, ap, ch)
            n.pass_over(2 * DT, 2)
            latents_vector(k, dve, n, ch)
            ret_vector(k, dve, ch)
            mla_vector(k, dve, ch)
            out2_vector(k, dve, n, ap)
            ffn_vector(k, dve)
            end_vector(k, dve, n)

        @block.tensor
        def _(pe):
            n = Norms()
            start_tensor(k, pe, n)
            sb_tensor(k, pe)
            merge_tensor(k, pe, "merge_sb", 0)
            pool_tensor(k, pe)
            merge_tensor(k, pe, "merge_pool", 1)
            conv_tensor(k, pe)
            merge_tensor(k, pe, "merge_conv", 2)
            out1_tensor(k, pe, n)
            enter_tensor(k, pe, n)
            latents_tensor(k, pe, n, 2 * DT)
            ret_tensor(k, pe)
            mla_tensor(k, pe)
            out2_tensor(k, pe, n)
            ffn_tensor(k, pe, 4 * DT)
            end_tensor(k, pe, n)





def fm(v):
    return np.asarray(v).reshape(-1, P).T


def blocks(w, cols=P):
    kk, n = w.shape
    return w.reshape(kk // P, P, n // cols, cols).transpose(2, 1, 0, 3).reshape(n // cols, P, kk // P * cols)


def padded(u):
    return np.concatenate([u, np.zeros(u.shape[:2] + (UNIT - u.shape[2],), u.dtype)], 2)


def weight_stream(i):
    w_in, w2 = i["w_in"][0], i["w_in_2"][0]
    sec = [blocks(w_in[:, W * n:W * n + W]) for n in range(10)]
    gates = blocks(w_in[:, 10 * W:])
    out = []
    for p in range(PAIRS):
        out += [sec[6][p], sec[7][p], sec[8][p], sec[9][p]]

    def merge(b):
        g, br = gates[DT * b:DT * b + DT], blocks(i["w_branch"][0][b], 2 * P)
        for t in range(0, DT, 2):
            out.extend([g[t], g[t + 1], br[t // 2]])
    merge(2)
    for g in range(BT):
        out += [sec[0][g], sec[1][g], padded(i["pool_w"][0][g][None])[0]]
    merge(0)
    for t in range(BT):
        out += [sec[4][t], sec[2][t], sec[3][t], sec[5][t]]
    merge(1)
    out += list(blocks(i["w_out"][0]))
    lat = blocks(w2[:, :512])
    kpe = w2[:, 512:544]
    swap = np.concatenate([kpe[:, 8:16], kpe[:, :8], kpe[:, 24:32], kpe[:, 16:24]], 1)
    out += list(lat) + list(blocks(np.concatenate([np.zeros((D, 64), kpe.dtype), kpe, swap], 1)))
    r = [blocks(w2[:, 544 + W * n:544 + W * n + W]) for n in range(4)]
    for h in range(RH):
        out += [r[1][h], r[2][h], r[0][h], r[3][h]]
    uq, ukv = i["w_uq_2"][0], i["w_ukv_2"][0]
    for p in range(PAIRS):
        for h in (2 * p, 2 * p + 1):
            m = uq[:, 96 * h:96 * h + 96]
            pe = m[:, 64:]
            sw = np.concatenate([pe[:, 8:16], pe[:, :8], pe[:, 24:32], pe[:, 16:24]], 1)
            q, kv = blocks(np.concatenate([m, sw], 1))[0], blocks(ukv[:, P * h:P * h + P])[0]
            out += [padded(np.concatenate([q, kv], 1)[None])[0]]
    out += list(blocks(i["w_out_2"][0]))
    up, down = blocks(i["w_up_2"][0]), i["w_down_2"][0]

    def add_up(g):
        out.extend([up[2 * g], up[FT + 2 * g], up[2 * g + 1], up[FT + 2 * g + 1]])

    def add_down(g):
        rows = down[2 * P * g:2 * P * g + 2 * P]
        out.extend(rows.reshape(2, P, 2, W).transpose(2, 1, 0, 3).reshape(2, P, UNIT))
    add_up(0)
    for g in range(1, FT // 2):
        add_up(g)
        add_down(g - 1)
    add_down(FT // 2 - 1)
    assert len(out) == NUNITS
    return np.stack(out)


def vectors(i):
    cw2 = np.concatenate([i["conv_w_2"][0], i["conv_b_2"][0][None]])
    cw2 = cw2.reshape(4, 2, FT // 1, P).transpose(3, 2, 1, 0).reshape(P, -1)
    cw = np.concatenate([i["conv_w"][0], i["conv_b"][0][None]]).reshape(4, BT, P).transpose(2, 1, 0).reshape(P, -1)
    c = np.stack([fm(i["c_2"][0]), fm(i["c_ctx_2"])], 2).reshape(P, -1)
    parts = [fm(i["pre_norm_g"][0]), fm(i["pool_scale"][0]), cw, fm(i["post_norm_g"][0]), c, fm(i["b_ada_2"][0]),
             fm(i["g_norm1_2"][0]), fm(i["g_q_2"][0]), fm(i["g_kv_2"][0]), fm(i["g_ret_2"][0]),
             fm(i["g_norm2_2"][0]), cw2, fm(i["g_final_2"]), np.tile(i["ret_decay_2"][0].reshape(1, -1), (P, 1))]
    v = np.ascontiguousarray(np.concatenate(parts, 1))
    assert v.shape == (P, NPARAM)
    return v


def tokens_last(x):
    return np.ascontiguousarray(x.T.reshape(-1, P, x.shape[0]).transpose(1, 0, 2))



def kernel(**inputs):
    import concourse.bacc as _bacc
    from concourse.bass_utils import run_bass_kernel_spmd as _run

    i = {name: np.asarray(v) for name, v in inputs.items()}
    ret_table, mla_table = rope_tables()
    arrays = {"in_stream": weight_stream(i), "in_w_ada": np.ascontiguousarray(blocks(i["w_ada_2"][0])),
              "in_x": tokens_last(i["x"][0]), "in_context": tokens_last(i["ctx_2"][0]),
              "in_params": vectors(i), "in_consts": constants(),
              "in_ret_table": np.ascontiguousarray(ret_table.reshape(P, 2, S)), "in_mla_table": mla_table}
    nc = _bacc.Bacc("TRN2", target_bir_lowering=False, num_devices=1)
    args = [nc.dram_tensor(n, v.shape, mybir.dt.from_np(v.dtype), kind="ExternalInput").ap() for n, v in arrays.items()]
    out = nc.dram_tensor("out_0_dram", (P, DT, S), F32, kind="ExternalOutput").ap()
    two_blocks_program(nc, *args, out)
    r = _run(nc, [arrays], core_ids=[0])
    got = np.asarray(r.results[0]["out_0_dram"])
    return np.ascontiguousarray(got.transpose(2, 1, 0).reshape(1, S, D))
```
